# Optimizing a Trainium2 kernel written in Bass

```python
import math
import jax
import jax.numpy as jnp
from jax import lax
import numpy as np

D_MODEL = 1024
BATCH = 1
SEQ = 1024
DEPTH = 2
DEC_BATCH = 8
DEC_SEQ = 1
PAST_LEN = 2048
PAGE_SIZE = 128

N_META = 16
QBLK = 128
N_BUCKETS = 32
MAX_DIST = 128
EPS = 1e-6

A_HEADS = 8
A_KV = 2
A_GROUP = A_HEADS // A_KV
A_DH = 64
A_DV = 2 * A_DH
A_WIDTH = A_HEADS * A_DV

B_HEADS = 4
B_DK = 128
B_DV = 128
B_WIDTH = B_HEADS * B_DV
B_QKV = 2 * B_HEADS * B_DK + B_WIDTH
CONV_W = 4
GDN_CHUNK = 64

C_HEADS = 8
C_KV = 2
C_GROUP = C_HEADS // C_KV
C_DH = 128
C_WIDTH = C_HEADS * C_DH
IDX_HEADS = 8
IDX_DIM = 64
TOPK_MAX = 256

N_BIAS_HEADS = A_HEADS
N_EVEN = (DEPTH + 1) // 2
N_ODD = DEPTH // 2

EVEN_COLS = (A_HEADS * 2 * A_DH, A_KV * 2 * A_DH, A_KV * A_DV, A_WIDTH, B_QKV, B_WIDTH, B_HEADS, B_HEADS)
ODD_COLS = (C_HEADS * C_DH, C_KV * C_DH, C_KV * C_DH, C_WIDTH, IDX_HEADS * IDX_DIM, IDX_DIM, IDX_HEADS)

kernel_name = 'hybrid_diffattn_gdn_dsa_step'

def _rmsnorm(x, g):
    xf = x.astype(jnp.float32)
    y = xf * lax.rsqrt(jnp.mean(xf * xf, axis=-1, keepdims=True) + EPS)
    return (y * g.astype(jnp.float32)).astype(x.dtype)

def _l2norm(x):
    return x * lax.rsqrt(jnp.sum(x * x, axis=-1, keepdims=True) + EPS)

def _split_cols(z, sizes):
    return jnp.split(z, np.cumsum(sizes)[:-1].tolist(), axis=-1)

def _split_meta(t, axis, size):
    meta = lax.slice_in_dim(t, 0, N_META, axis=axis)
    rest = lax.slice_in_dim(t, N_META, t.shape[axis], axis=axis)
    shp = rest.shape[:axis] + (rest.shape[axis] // size, size) + rest.shape[axis + 1:]
    return meta, jnp.moveaxis(rest.reshape(shp), axis, 0)

def _merge_meta(meta, rest, axis):
    rest = jnp.moveaxis(rest, 0, axis)
    shp = rest.shape[:axis] + (rest.shape[axis] * rest.shape[axis + 1],) + rest.shape[axis + 2:]
    return jnp.concatenate([meta, rest.reshape(shp).astype(meta.dtype)], axis=axis)

def _gather_rows(rows, idx):
    return jax.vmap(lambda r, i: r[i])(rows, idx)

def _t5_bias(dist, table):
    n = jnp.maximum(dist, 0)
    exact = N_BUCKETS // 2
    nf = jnp.maximum(n, 1).astype(jnp.float32)
    large = exact + (jnp.log(nf / exact) / math.log(MAX_DIST / exact) * (N_BUCKETS - exact)).astype(jnp.int32)
    bucket = jnp.where(n < exact, n, jnp.minimum(large, N_BUCKETS - 1))
    return table[bucket].astype(jnp.float32)

def _diff_lambda(lq1, lk1, lq2, lk2, lam_init):
    f32 = jnp.float32
    return (jnp.exp(jnp.sum(lq1.astype(f32) * lk1.astype(f32)))
            - jnp.exp(jnp.sum(lq2.astype(f32) * lk2.astype(f32))) + lam_init)

def _diff_attn(q, k, v, pos_q, pos_k, lam, table):
    tq, tk = pos_q.shape[0], pos_k.shape[0]
    s = jnp.einsum('bqhgcd,bkhcd->bhgcqk', q, k).astype(jnp.float32) * A_DH ** -0.5
    bias = jnp.transpose(_t5_bias(pos_q[:, None] - pos_k[None, :], table), (2, 0, 1))
    bias = bias.reshape(A_KV, A_GROUP, 1, tq, tk)
    mask = pos_k[None, :] <= pos_q[:, None]
    p = jax.nn.softmax(jnp.where(mask, s + bias, -jnp.inf), axis=-1)
    a = p[:, :, :, 0] - lam * p[:, :, :, 1]
    o = jnp.einsum('bhgqk,bkhe->bqhge', a.astype(v.dtype), v)
    return o.reshape(o.shape[0], tq, A_HEADS, A_DV)

def _a_output(o, gate, subln, lam_init):
    b, t = gate.shape[:2]
    y = _rmsnorm(o.astype(gate.dtype), subln) * (1.0 - lam_init)
    y = y * jax.nn.silu(gate.reshape(b, t, A_HEADS, A_DV))
    return y.reshape(b, t, A_WIDTH)

def _gdn_inputs(qkv, conv_buf, conv_w, a_raw, b_raw, a_log, dt_bias):
    b, t = qkv.shape[:2]
    xpad = jnp.concatenate([conv_buf.astype(qkv.dtype), qkv], axis=1)
    conv = sum(conv_w[i] * xpad[:, i:i + t] for i in range(CONV_W))
    new_buf = xpad[:, xpad.shape[1] - (CONV_W - 1):]
    act = jax.nn.silu(conv).astype(jnp.float32)
    q, k, v = _split_cols(act, (B_HEADS * B_DK, B_HEADS * B_DK, B_WIDTH))
    q = _l2norm(q.reshape(b, t, B_HEADS, B_DK)) * B_DK ** -0.5
    k = _l2norm(k.reshape(b, t, B_HEADS, B_DK))
    v = v.reshape(b, t, B_HEADS, B_DV)
    g = -jnp.exp(a_log.astype(jnp.float32)) * jax.nn.softplus(a_raw.astype(jnp.float32) + dt_bias.astype(jnp.float32))
    beta = jax.nn.sigmoid(b_raw.astype(jnp.float32))
    heads_first = lambda z: jnp.moveaxis(z, 2, 1)
    return heads_first(q), heads_first(k), heads_first(v), heads_first(g), heads_first(beta), new_buf

def _gdn_chunk(s0, q, k, v, g, beta):
    c = q.shape[2]
    ti = jnp.arange(c)
    incl = ti[:, None] >= ti[None, :]
    strict = ti[:, None] > ti[None, :]
    gcum = jnp.cumsum(g, axis=-1)
    diff = gcum[..., :, None] - gcum[..., None, :]
    decay = jnp.where(incl, jnp.exp(jnp.where(incl, diff, 0.0)), 0.0)
    kk = jnp.einsum('bhid,bhjd->bhij', k, k)
    a = jnp.where(strict, beta[..., :, None] * decay * kk, 0.0) + jnp.eye(c, dtype=q.dtype)
    rhs = beta[..., None] * (v - jnp.exp(gcum)[..., None] * jnp.einsum('bhid,bhde->bhie', k, s0))
    u = lax.linalg.triangular_solve(a, rhs, left_side=True, lower=True, unit_diagonal=True)
    qk = jnp.einsum('bhid,bhjd->bhij', q, k) * decay
    o = jnp.exp(gcum)[..., None] * jnp.einsum('bhid,bhde->bhie', q, s0) + jnp.einsum('bhij,bhje->bhie', qk, u)
    g_last = gcum[..., -1:]
    s_new = jnp.exp(g_last)[..., None] * s0 + jnp.einsum('bhid,bhie->bhde', k * jnp.exp(g_last - gcum)[..., None], u)
    return s_new, o

def _gdn_output(o, gate, norm_g):
    b, t = gate.shape[:2]
    y = _rmsnorm(jnp.moveaxis(o, 1, 2).astype(gate.dtype), norm_g)
    y = y * jax.nn.silu(gate.reshape(b, t, B_HEADS, B_DV))
    return y.reshape(b, t, B_WIDTH)

def _even_project(x, w_in):
    b, t = x.shape[:2]
    qa, ka, va, ga, qkv, gb, ab, bb = _split_cols(x @ w_in, EVEN_COLS)
    return (qa.reshape(b, t, A_KV, A_GROUP, 2, A_DH), ka.reshape(b, t, A_KV, 2, A_DH),
            va.reshape(b, t, A_KV, A_DV), ga, qkv, gb, ab, bb)

def _even_prompt(h, ep, lam, lam_init, table):
    norm, w_in, w_out, subln, conv_w, a_log, dt_bias, norm_g = ep
    b, seq_len = h.shape[:2]
    qa, ka, va, ga, qkv, gb, ab, bb = _even_project(_rmsnorm(h, norm), w_in)
    pos = jnp.arange(seq_len)
    q_meta, q_rest = _split_meta(qa, 1, QBLK)
    p_meta, p_rest = _split_meta(pos, 0, QBLK)
    o_meta = _diff_attn(q_meta, ka, va, p_meta, pos, lam, table)
    o_rest = lax.map(lambda qp: _diff_attn(qp[0], ka, va, qp[1], pos, lam, table), (q_rest, p_rest))
    ya = _a_output(_merge_meta(o_meta, o_rest, 1), ga, subln, lam_init)
    conv0 = jnp.zeros((b, CONV_W - 1, B_QKV), h.dtype)
    q, k, v, g, beta, conv_new = _gdn_inputs(qkv, conv0, conv_w, ab, bb, a_log, dt_bias)
    s0 = jnp.zeros((b, B_HEADS, B_DK, B_DV), jnp.float32)
    s_meta, ob_meta = _gdn_chunk(s0, q[:, :, :N_META], k[:, :, :N_META], v[:, :, :N_META],
                                 g[:, :, :N_META], beta[:, :, :N_META])
    chunks = tuple(_split_meta(z, 2, GDN_CHUNK)[1] for z in (q, k, v, g, beta))
    s_fin, ob_rest = lax.scan(lambda s, xs: _gdn_chunk(s, *xs), s_meta, chunks)
    yb = _gdn_output(_merge_meta(ob_meta, ob_rest, 2), gb, norm_g)
    out = jnp.concatenate([ya, yb], axis=-1) @ w_out
    return h + out, (ka, va, s_fin.astype(h.dtype), conv_new)

def _even_sample(h, cache_k, cache_v, s_prev, conv_prev, page_table, li, ep, lam, lam_init, table):
    norm, w_in, w_out, subln, conv_w, a_log, dt_bias, norm_g = ep
    b, t = h.shape[:2]
    past = page_table.shape[1] * PAGE_SIZE
    qa, ka, va, ga, qkv, gb, ab, bb = _even_project(_rmsnorm(h, norm), w_in)
    k_all = jnp.concatenate([cache_k[li, page_table].reshape((b, past) + ka.shape[2:]).astype(ka.dtype), ka], axis=1)
    v_all = jnp.concatenate([cache_v[li, page_table].reshape((b, past) + va.shape[2:]).astype(va.dtype), va], axis=1)
    pos_q = past + jnp.arange(t)
    pos_k = jnp.arange(past + t)
    ya = _a_output(_diff_attn(qa, k_all, v_all, pos_q, pos_k, lam, table), ga, subln, lam_init)
    q, k, v, g, beta, conv_new = _gdn_inputs(qkv, conv_prev, conv_w, ab, bb, a_log, dt_bias)
    s_new, ob = _gdn_chunk(s_prev.astype(jnp.float32), q, k, v, g, beta)
    yb = _gdn_output(ob, gb, norm_g)
    out = jnp.concatenate([ya, yb], axis=-1) @ w_out
    return h + out, (ka, va, s_new.astype(s_prev.dtype), conv_new)

def _odd_project(x, w_in):
    b, t = x.shape[:2]
    qc, kc, vc, gc, qi, ki, wi = _split_cols(x @ w_in, ODD_COLS)
    return (qc.reshape(b, t, C_KV, C_GROUP, C_DH), kc.reshape(b, t, C_KV, C_DH), vc.reshape(b, t, C_KV, C_DH),
            gc, qi.reshape(b, t, IDX_HEADS, IDX_DIM), ki, wi)

def _index_select(qi, wi, ki, pos_q, k_sel):
    dots = jnp.einsum('bqhd,bkd->bqhk', qi, ki).astype(jnp.float32) * IDX_DIM ** -0.5
    score = jnp.einsum('bqh,bqhk->bqk', wi.astype(jnp.float32) * IDX_HEADS ** -0.5, jax.nn.relu(dots))
    admissible = jnp.arange(ki.shape[1])[None, :] <= pos_q[:, None]
    _, idx = lax.top_k(jnp.where(admissible, score, -jnp.inf), k_sel)
    return idx, idx <= pos_q[None, :, None]

def _sparse_attn(qc, kg, vg, pos_q, idx, valid, table):
    b, tq, kn = idx.shape
    s = jnp.einsum('bqhgd,bqkhd->bhgqk', qc, kg).astype(jnp.float32) * C_DH ** -0.5
    bias = jnp.transpose(_t5_bias(pos_q[None, :, None] - idx, table), (0, 3, 1, 2)).reshape(b, C_KV, C_GROUP, tq, kn)
    p = jax.nn.softmax(jnp.where(valid[:, None, None], s + bias, -jnp.inf), axis=-1)
    o = jnp.einsum('bhgqk,bqkhd->bqhgd', p.astype(vg.dtype), vg)
    return o.reshape(b, tq, C_HEADS, C_DH)

def _c_output(o, gate, w_out):
    b, t = gate.shape[:2]
    return (o.reshape(b, t, C_WIDTH).astype(gate.dtype) * jax.nn.silu(gate)) @ w_out

def _odd_prompt(h, op, table):
    norm, w_in, w_out = op
    seq_len = h.shape[1]
    qc, kc, vc, gc, qi, ki, wi = _odd_project(_rmsnorm(h, norm), w_in)
    k_sel = min(TOPK_MAX, seq_len // 4)
    pos = jnp.arange(seq_len)

    def block(args):
        qc_b, qi_b, wi_b, pos_b = args
        idx, valid = _index_select(qi_b, wi_b, ki, pos_b, k_sel)
        return _sparse_attn(qc_b, _gather_rows(kc, idx), _gather_rows(vc, idx), pos_b, idx, valid, table)

    parts = [_split_meta(z, 1, QBLK) for z in (qc, qi, wi)] + [_split_meta(pos, 0, QBLK)]
    o_meta = block(tuple(p[0] for p in parts))
    o_rest = lax.map(block, tuple(p[1] for p in parts))
    out = _c_output(_merge_meta(o_meta, o_rest, 1), gc, w_out)
    return h + out, (kc, vc, ki)

def _odd_sample(h, cache_k, cache_v, cache_i, page_table, li, op, table):
    norm, w_in, w_out = op
    b, t = h.shape[:2]
    past = page_table.shape[1] * PAGE_SIZE
    qc, kc, vc, gc, qi, ki, wi = _odd_project(_rmsnorm(h, norm), w_in)
    ki_all = jnp.concatenate([cache_i[li, page_table].reshape(b, past, IDX_DIM).astype(ki.dtype), ki], axis=1)
    pos_q = past + jnp.arange(t)
    idx, valid = _index_select(qi, wi, ki_all, pos_q, min(TOPK_MAX, (past + t) // 4))
    in_past = (idx < past)[..., None, None]
    row = jnp.minimum(idx, past - 1)
    page = _gather_rows(page_table, row // PAGE_SIZE)
    off = row % PAGE_SIZE
    new = jnp.clip(idx - past, 0, t - 1)
    kg = jnp.where(in_past, cache_k[li, page, off].astype(kc.dtype), _gather_rows(kc, new))
    vg = jnp.where(in_past, cache_v[li, page, off].astype(vc.dtype), _gather_rows(vc, new))
    out = _c_output(_sparse_attn(qc, kg, vg, pos_q, idx, valid, table), gc, w_out)
    return h + out, (kc, vc, ki)

def setup_inputs(seed: int = 0) -> dict:
    key = jax.random.key(seed)
    ks = jax.random.split(key, 32)
    f32 = jnp.float32
    n_pages = PAST_LEN // PAGE_SIZE
    n_pool = (DEC_BATCH * n_pages * 5) // 4

    def nrm(i, shape, scale):
        return jax.random.normal(ks[i], shape, f32) * scale

    def gain(i, shape):
        return 1.0 + 0.02 * jax.random.normal(ks[i], shape, f32)

    page_table = jax.random.permutation(ks[0], n_pool)[:DEC_BATCH * n_pages].reshape(DEC_BATCH, n_pages).astype(jnp.int32)
    dt = jnp.exp(jax.random.uniform(ks[1], (N_EVEN, B_HEADS), f32, math.log(1e-3), math.log(1e-1)))
    return {
        'x_prompt': nrm(2, (BATCH, SEQ, D_MODEL), 1.0),
        'x_sample': nrm(3, (DEC_BATCH, DEC_SEQ, D_MODEL), 1.0),
        'cache_a_k': nrm(4, (N_EVEN, n_pool, PAGE_SIZE, A_KV, 2, A_DH), 1.0),
        'cache_a_v': nrm(5, (N_EVEN, n_pool, PAGE_SIZE, A_KV, A_DV), 1.0),
        'state_b_s': nrm(6, (N_EVEN, DEC_BATCH, B_HEADS, B_DK, B_DV), 0.3),
        'state_b_conv': nrm(7, (N_EVEN, DEC_BATCH, CONV_W - 1, B_QKV), 1.0),
        'cache_c_k': nrm(8, (N_ODD, n_pool, PAGE_SIZE, C_KV, C_DH), 1.0),
        'cache_c_v': nrm(9, (N_ODD, n_pool, PAGE_SIZE, C_KV, C_DH), 1.0),
        'cache_c_idx': nrm(10, (N_ODD, n_pool, PAGE_SIZE, IDX_DIM), 1.0),
        'page_table': page_table,
        'meta': nrm(11, (N_META, D_MODEL), 1.0),
        'bias_table': nrm(12, (N_BUCKETS, N_BIAS_HEADS), 0.5),
        'final_norm': gain(13, (D_MODEL,)),
        'norm_e': gain(14, (N_EVEN, D_MODEL)),
        'w_in_e': nrm(15, (N_EVEN, D_MODEL, sum(EVEN_COLS)), D_MODEL ** -0.5),
        'w_out_e': nrm(16, (N_EVEN, A_WIDTH + B_WIDTH, D_MODEL), (A_WIDTH + B_WIDTH) ** -0.5),
        'lam_q1': nrm(17, (N_EVEN, A_DH), 0.1),
        'lam_k1': nrm(18, (N_EVEN, A_DH), 0.1),
        'lam_q2': nrm(19, (N_EVEN, A_DH), 0.1),
        'lam_k2': nrm(20, (N_EVEN, A_DH), 0.1),
        'subln_a': gain(21, (N_EVEN, A_DV)),
        'conv_b': nrm(22, (N_EVEN, CONV_W, B_QKV), CONV_W ** -0.5),
        'a_log_b': jnp.log(jax.random.uniform(ks[23], (N_EVEN, B_HEADS), f32, 1.0, 16.0)),
        'dt_bias_b': dt + jnp.log(-jnp.expm1(-dt)),
        'norm_b': gain(24, (N_EVEN, B_DV)),
        'norm_o': gain(25, (N_ODD, D_MODEL)),
        'w_in_o': nrm(26, (N_ODD, D_MODEL, sum(ODD_COLS)), D_MODEL ** -0.5),
        'w_out_o': nrm(27, (N_ODD, C_WIDTH, D_MODEL), C_WIDTH ** -0.5),
    }

def reference(x_prompt, x_sample, cache_a_k, cache_a_v, state_b_s, state_b_conv, cache_c_k, cache_c_v, cache_c_idx,
              page_table, meta, bias_table, final_norm, norm_e, w_in_e, w_out_e, lam_q1, lam_k1, lam_q2, lam_k2,
              subln_a, conv_b, a_log_b, dt_bias_b, norm_b, norm_o, w_in_o, w_out_o):
    b = x_prompt.shape[0]
    hp = jnp.concatenate([jnp.broadcast_to(meta.astype(x_prompt.dtype)[None], (b, N_META, D_MODEL)), x_prompt], axis=1)
    hs = x_sample
    even_p, even_s, odd_p, odd_s = [], [], [], []
    for layer in range(DEPTH):
        li = layer // 2
        if layer % 2 == 0:
            lam_init = 0.8 - 0.6 * math.exp(-0.3 * layer)
            lam = _diff_lambda(lam_q1[li], lam_k1[li], lam_q2[li], lam_k2[li], lam_init)
            ep = (norm_e[li], w_in_e[li], w_out_e[li], subln_a[li], conv_b[li], a_log_b[li], dt_bias_b[li], norm_b[li])
            hp, rows = _even_prompt(hp, ep, lam, lam_init, bias_table)
            even_p.append(rows)
            hs, rows = _even_sample(hs, cache_a_k, cache_a_v, state_b_s[li], state_b_conv[li], page_table, li,
                                    ep, lam, lam_init, bias_table)
            even_s.append(rows)
        else:
            op = (norm_o[li], w_in_o[li], w_out_o[li])
            hp, rows = _odd_prompt(hp, op, bias_table)
            odd_p.append(rows)
            hs, rows = _odd_sample(hs, cache_c_k, cache_c_v, cache_c_idx, page_table, li, op, bias_table)
            odd_s.append(rows)
    pa_k, pa_v, pb_s, pb_conv = [jnp.stack(z) for z in zip(*even_p)]
    sa_k, sa_v, sb_s, sb_conv = [jnp.stack(z) for z in zip(*even_s)]
    pc_k, pc_v, pc_idx = [jnp.stack(z) for z in zip(*odd_p)]
    sc_k, sc_v, sc_idx = [jnp.stack(z) for z in zip(*odd_s)]
    y_prompt = _rmsnorm(hp, final_norm)[:, N_META:]
    y_sample = _rmsnorm(hs, final_norm)
    return (y_prompt, y_sample, pa_k, pa_v, pb_s, pb_conv, pc_k, pc_v, pc_idx, sa_k, sa_v, sb_s, sb_conv, sc_k, sc_v, sc_idx)


_drawn_inputs = setup_inputs


def setup_inputs(seed=0):
    import zlib

    import numpy as np

    out = dict(_drawn_inputs(seed))
    spreads = {}
    factors = {'final_norm': 7.453,
     'lam_q1': 2.796,
     'lam_k1': 5.399,
     'lam_q2': 5.962,
     'lam_k2': 8.0,
     'subln_a': 25.338,
     'norm_b': 28.707,
     'cache_c_k': 4.307,
     'cache_c_v': 3.238,
     'cache_c_idx': 3.263,
     'norm_o': 2.7}
    for name, (base, spread) in spreads.items():
        noise = np.random.default_rng([zlib.crc32(name.encode()), seed]).standard_normal(out[name].shape)
        drawn = base * np.exp(spread * noise) if base else spread * noise
        out[name] = jnp.asarray(drawn.astype(out[name].dtype))
    for name, factor in factors.items():
        out[name] = (out[name] * factor).astype(out[name].dtype)
    return out
```

```python
from contextlib import ExitStack

import numpy as np

import concourse.bass as bass
import concourse.mybir as mybir

F32 = mybir.dt.float32
I32 = mybir.dt.int32
ALU = mybir.AluOpType
ACT = mybir.ActivationFunctionType
AX = mybir.AxisListType.X

P = 128
D = 1024
KC = D // P
N_META, SEQ, NB = 16, 1024, 8
L = N_META + SEQ
T = L + NB
FULL = L // P
TAIL = L - FULL * P
LAST = T - FULL * P
NT = FULL + 1
EPS = 1e-6
PAGE, N_PAGES = 128, 16
PAST = PAGE * N_PAGES
H, KV, G = 8, 2, 4
LAM_INIT = 0.8 - 0.6
B_H = 4
CONV = 4
TOPK = 256
NEG = -1e30
SLICES = [(0, 350), (350, 350), (700, 348)]
FAR = FULL * P + P - 1
BIAS_W = FAR + P

EVEN = {"groups": [(1024, 512), (1536, 512), (2048, 512), (4096, 512), (4608, 8)], "gates": (1536, 2048, 4096),
        "mid": 2560}
ODD = {"groups": [(1024, 512), (1536, 512), (2048, 512), (3072, 72)], "gates": (1536, 2048), "mid": 2560}
TOK_K, TOK_V, TOK_G, TOK_R = 0, 256, 512, 1536
TOK_W = 1536 + 520


def row_view(ap):
    return ap.rearrange("(o n) -> o n", o=1)


def over_tiles(eng, body):
    with eng.Fori(0, FULL // 2) as i:
        body(2 * i, i, 0, P)
        body(2 * i + 1, i, 1, P)
    body(FULL, FULL // 2, 0, LAST)


class Steps:

    def __init__(self, eng, sem, base=0):
        self.eng, self.sem, self.base, self.n = eng, sem, base, 0

    def after(self, ins):
        self.n += 1
        ins.then_inc(self.sem, 1)
        self.eng.wait_ge(self.sem, self.base + self.n)


def alone(eng, m):
    eng.sem_inc(m.s_idle, 1)



def load_rows(nc, m, io, tag):
    rows_in = m.sem(f"{tag}_rows_in")
    with nc.Block() as block:
        @block.sync
        def _(sp):
            xp = io["x_prompt"].rearrange("b s d -> (b s) d")
            xs = io["x_sample"].rearrange("b s d -> (b s) d")
            first = P - N_META
            sp.dma_start(m.h[0:N_META, 0, :], io["meta"]).then_inc(rows_in, 16)
            sp.dma_start(m.h[N_META:P, 0, :], xp[0:first, :]).then_inc(rows_in, 16)
            body = xp[first:first + (FULL - 1) * P, :].rearrange("(t p) d -> p t d", p=P)
            sp.dma_start(m.h[:, 1:FULL, :], body).then_inc(rows_in, 16)
            sp.dma_start(m.h[0:TAIL, FULL, :], xp[SEQ - TAIL:SEQ, :]).then_inc(rows_in, 16)
            sp.dma_start(m.h[TAIL:LAST, FULL, :], xs).then_inc(rows_in, 16)
            sp.wait_ge(rows_in, 16 * 5)


def load_constants(nc, m, io):
    consts_in = m.sem("consts_in")
    with nc.Block() as block:
        @block.sync
        def _(sp):
            sp.dma_start(m.ident[:], io["c_ident"]).then_inc(consts_in, 16)
            sp.dma_start(m.pages[:], row_view(io["page_table"].rearrange("a b -> (a b)"))).then_inc(consts_in, 16)
            sp.dma_start(m.halves[:], io["c_halves"]).then_inc(consts_in, 16)
            sp.wait_ge(consts_in, 48)

        @block.vector
        def _(dve):
            dve.memset(m.ones[:], 1.0)
            dve.memset(m.eps[:], EPS)
            dve.wait_ge(consts_in, 48)
            nc.vector.tensor_copy(m.halves_wide[:], m.halves[:].rearrange("p (c o) -> p c o", o=1)
                                  .to_broadcast([P, 3, P]))



def norm_and_turn(nc, m, gain, tag):
    with ExitStack() as own:
        E = own.enter_context
        squares = E(nc.sbuf_tensor(f"{tag}_squares", [P, D], F32))
        ss = E(nc.sbuf_tensor(f"{tag}_ss", [P, NT], F32))
        rstd = E(nc.sbuf_tensor(f"{tag}_rstd", [P, NT], F32))
        scaled = E(nc.sbuf_tensor(f"{tag}_scaled", [P, 2, D], F32))
        gain_t = E(nc.sbuf_tensor(f"{tag}_gain", [P, KC], F32))
        gain_in, summed, root, sq_step, scaled_ready, turned, copied, dve_step = (
            m.sem(f"{tag}_{x}") for x in ("gain_in", "summed", "root", "sq_step", "scaled", "turned", "copied", "step"))
        with nc.Block() as block:
            @block.sync
            def _(sp):
                with nc.allow_non_contiguous_dma(reason="a gain vector onto partitions"):
                    sp.dma_start(gain_t[:], gain.rearrange("(c p) -> p c", p=P)).then_inc(gain_in, 16)

            @block.scalar
            def _(act):
                own_steps = Steps(act, sq_step)
                for t in range(NT):
                    r = P if t < FULL else LAST
                    own_steps.after(nc.scalar.activation(squares[0:r], m.h[0:r, t, :], ACT.Square,
                                                         accum_out=ss[0:r, t:t + 1]))
                nc.scalar.activation(rstd[:, 0:FULL], ss[:, 0:FULL], ACT.Sqrt, scale=1.0 / D,
                                     bias=m.eps[:, 0:1])
                nc.scalar.activation(rstd[0:LAST, FULL:NT], ss[0:LAST, FULL:NT], ACT.Sqrt, scale=1.0 / D,
                                     bias=m.eps[0:LAST, 0:1]).then_inc(root, 1)

            @block.vector
            def _(dve):
                steps = Steps(dve, dve_step)
                dve.wait_ge(root, 1)
                nc.vector.reciprocal(rstd[:, 0:FULL], rstd[:, 0:FULL])
                steps.after(nc.vector.reciprocal(rstd[0:LAST, FULL:NT], rstd[0:LAST, FULL:NT]))
                dve.sem_inc(copied, 2)
                dve.wait_ge(gain_in, 16)

                def scale(t, slot, r):
                    nc.vector.tensor_scalar(scaled[0:r, slot], m.h[0:r, bass.ds(t, 1), :], rstd[0:r, bass.ds(t, 1)],
                                            None, ALU.mult).then_inc(scaled_ready, 1)

                def tile(t, turn, slot, r):
                    scale(t, slot, r)
                    dve.wait_ge(turned, t + 1)
                    src = m.ps[:, 2 * slot:2 * slot + 2, :].rearrange("p a (b c) -> p (a b) c", c=P)[:, :, 0:r]
                    dst = m.actT[:, 0:KC, bass.ds(t * P, r)]
                    g = gain_t[:].rearrange("p (c o) -> p c o", o=1).to_broadcast([P, KC, r])
                    nc.vector.tensor_tensor(dst, src, g, ALU.mult).then_inc(copied, 1)

                over_tiles(dve, tile)

            @block.tensor
            def _(pe):
                def tile(t, turn, slot, r):
                    pe.wait_ge(scaled_ready, t + 1)
                    pe.wait_ge(copied, t + 1)
                    for c in range(KC):
                        bank, at = 2 * slot + c // 4, (c % 4) * P
                        last = nc.tensor.transpose(m.ps[:, bank, at:at + r], scaled[0:r, slot, c * P:(c + 1) * P],
                                                   m.ident[0:r, 0:r])
                    last.then_inc(turned, 1)

                over_tiles(pe, tile)



def project_tokens(nc, m, w, cols, tok, tag):
    groups = cols["groups"]
    starts = [sum(g[1] for g in groups[:j]) for j in range(len(groups))]
    width = sum(g[1] for g in groups)
    by_act = [j for j, (c0, _) in enumerate(groups) if c0 in cols["gates"]]
    by_dve = [j for j in range(len(groups)) if j not in by_act]
    n_act, n_dve = len(by_act), len(by_dve)
    with ExitStack() as own:
        E = own.enter_context
        wt = E(nc.sbuf_tensor(f"{tag}_w", [P, KC, width], F32))
        rows = E(nc.sbuf_tensor(f"{tag}_rows", [P, 2, KC, P], F32))
        stage = E(nc.sbuf_tensor(f"{tag}_stage", [P, 2, width], F32))
        w_in = [m.sem(f"{tag}_w_in{j}") for j in range(len(groups))]
        rows_ready, product, act_out, dve_out = (
            m.sem(f"{tag}_{x}") for x in ("rows", "product", "act_out", "dve_out"))
        stored = [m.sem(f"{tag}_stored{s}") for s in range(2)]
        wr = w.rearrange("(c p) n -> p c n", p=P)
        with nc.Block() as block:
            @block.sync
            def _(sp):
                for j, (c0, n) in enumerate(groups):
                    sp.dma_start(wt[:, :, starts[j]:starts[j] + n], wr[:, :, c0:c0 + n]).then_inc(w_in[j], 16)
                for s in range(2):
                    sp.sem_inc(stored[s], 16)

                def tile(t, turn, slot, r):
                    sp.wait_ge(act_out, n_act * (t + 2))
                    alone(sp, m)
                    sp.wait_ge(dve_out, n_dve * (t + 2))
                    alone(sp, m)
                    sp.dma_start(tok[bass.ds(t * P, r), 0:width], stage[0:r, slot, :]).then_inc(stored[slot], 16)

                over_tiles(sp, tile)
                sp.wait_ge(stored[0], 16 * (FULL // 2 + 2))
                sp.wait_ge(stored[1], 16 * (FULL // 2 + 1))

            @block.scalar
            def _(act):
                act.sem_inc(act_out, n_act)

                def stage_rows(t, turn, slot, r):
                    nc.scalar.copy(rows[:, slot, :, 0:r], m.actT[:, 0:KC, bass.ds(t * P, r)]).then_inc(rows_ready, 1)

                def tile(t, turn, slot, r):
                    for j in by_act:
                        act.wait_ge(product, len(groups) * t + j + 1)
                        if j == by_act[0]:
                            act.wait_ge(stored[slot], 16 * (turn + 1))
                        nc.scalar.activation(stage[0:r, slot, starts[j]:starts[j] + groups[j][1]],
                                             m.ps[0:r, j, 0:groups[j][1]], ACT.Silu).then_inc(act_out, 1)
                    act.wait_ge(product, len(groups) * (t + 1))

                stage_rows(0, 0, 0, P)
                with act.Fori(0, FULL // 2 - 1) as i:
                    stage_rows(2 * i + 1, i, 1, P)
                    tile(2 * i, i, 0, P)
                    stage_rows(2 * i + 2, i + 1, 0, P)
                    tile(2 * i + 1, i, 1, P)
                stage_rows(FULL - 1, FULL // 2 - 1, 1, P)
                tile(FULL - 2, FULL // 2 - 1, 0, P)
                stage_rows(FULL, FULL // 2, 0, LAST)
                tile(FULL - 1, FULL // 2 - 1, 1, P)
                tile(FULL, FULL // 2, 0, LAST)

            @block.vector
            def _(dve):
                dve.sem_inc(dve_out, n_dve)

                def tile(t, turn, slot, r):
                    for j in by_dve:
                        dve.wait_ge(product, len(groups) * t + j + 1)
                        if j == by_dve[0]:
                            dve.wait_ge(stored[slot], 16 * (turn + 1))
                        nc.vector.tensor_copy(stage[0:r, slot, starts[j]:starts[j] + groups[j][1]],
                                              m.ps[0:r, j, 0:groups[j][1]]).then_inc(dve_out, 1)

                over_tiles(dve, tile)

            @block.tensor
            def _(pe):
                for j in range(len(groups)):
                    pe.wait_ge(w_in[j], 16)

                def tile(t, turn, slot, r):
                    pe.wait_ge(rows_ready, t + 1)
                    for j, (_, n) in enumerate(groups):
                        if j in by_act:
                            pe.wait_ge(act_out, n_act * t + by_act.index(j) + 1)
                        else:
                            pe.wait_ge(dve_out, n_dve * t + by_dve.index(j) + 1)
                        for c in range(KC):
                            last = nc.tensor.matmul(m.ps[0:r, j, 0:n], rows[:, slot, c, 0:r],
                                                    wt[:, c, starts[j]:starts[j] + n],
                                                    start=(c == 0), stop=(c == KC - 1))
                        last.then_inc(product, 1)

                over_tiles(pe, tile)



def project_features(nc, m, w, parts, tag):
    with ExitStack() as own:
        E = own.enter_context
        wring = E(nc.sbuf_tensor(f"{tag}_w", [P, 2, KC, 2 * P], F32))
        w_in = [m.sem(f"{tag}_w_in{s}") for s in range(2)]
        product, act_out, dve_out = (m.sem(f"{tag}_{x}") for x in ("product", "act_out", "dve_out"))
        credit = 4 * len(SLICES)
        wr = w.rearrange("(c p) n -> p c n", p=P)
        NS = len(SLICES)

        def over_turns(eng, body):
            base = 0
            for part in parts:
                with eng.Fori(0, part[1] // 4) as i:
                    body(base + i, i, part)
                base += part[1] // 4

        with nc.Block() as block:
            @block.sync
            def _(sp):
                def turn(n, i, part):
                    for s in range(2):
                        sp.wait_ge(product, 2 * NS * (2 * n + s + 1))
                        sp.dma_start(wring[:, s], wr[:, :, bass.ds(part[0] + i * 4 * P + s * 2 * P, 2 * P)])\
                            .then_inc(w_in[s], 16)

                over_turns(sp, turn)

            @block.tensor
            def _(pe):
                pe.sem_inc(product, credit)

                def turn(n, i, part):
                    for s in range(2):
                        pe.wait_ge(w_in[s], 16 * n + 16)
                        for j in range(2):
                            for k, (t0, tn) in enumerate(SLICES):
                                pe.wait_ge(act_out if j == 0 else dve_out, NS * (2 * n + s) + k + 1)
                                for c in range(KC):
                                    last = nc.tensor.matmul(m.ps[:, NS * j + k, 0:tn],
                                                            wring[:, s, c, j * P:(j + 1) * P],
                                                            m.actT[:, c, t0:t0 + tn],
                                                            start=(c == 0), stop=(c == KC - 1))
                                last.then_inc(product, 1)

                over_turns(pe, turn)

            def evacuate(eng, j, out, copy):
                eng.sem_inc(out, NS)

                def turn(n, i, part):
                    for s in range(2):
                        for k, (t0, tn) in enumerate(SLICES):
                            eng.wait_ge(product, credit + NS * (2 * (2 * n + s) + j) + k + 1)
                            copy(part[2][:, bass.ds(4 * i + 2 * s + j, 1), t0:t0 + tn],
                                 m.ps[:, NS * j + k, 0:tn]).then_inc(out, 1)

                over_turns(eng, turn)

            @block.scalar
            def _(act):
                evacuate(act, 0, act_out, nc.scalar.copy)

            @block.vector
            def _(dve):
                evacuate(dve, 1, dve_out, nc.vector.tensor_copy)



def convolve(nc, m, io):
    NF = 12
    with ExitStack() as own:
        E = own.enter_context
        past = E(nc.sbuf_tensor("cv_past", [NB * 3 + CONV, NF * P], F32))
        pastT = E(nc.sbuf_tensor("cv_pastT", [P, NF, NB * 3 + CONV], F32))
        fresh = E(nc.sbuf_tensor("cv_fresh", [3 + NB, NF * P], F32))
        y = E(nc.sbuf_tensor("cv_y", [P, 2, L], F32))
        ys = E(nc.sbuf_tensor("cv_ys", [P, 2, NF, NB], F32))
        past_in, turned, copied, conv_out, conv_step, sample_out, silued, stored = (
            m.sem("cv_" + x) for x in ("past_in", "turned", "copied", "out", "step", "sample", "silued", "stored"))
        taps = NB * 3

        with nc.Block() as block:
            @block.sync
            def _(sp):
                conv_state = io["state_b_conv"][0]
                sp.dma_start(past[0:taps, :], conv_state.rearrange("b r c -> (b r) c")).then_inc(past_in, 16)
                sp.dma_start(past[taps:taps + CONV, :], io["conv_b"][0]).then_inc(past_in, 16)
                sp.dma_start(io["sb_conv"][0, :, 0:2, :], conv_state[:, 1:3, :]).then_inc(stored, 16)
                sp.wait_ge(copied, 2)
                sp.dma_start(io["pb_conv"][0, 0], fresh[0:3, :]).then_inc(stored, 16)
                sp.dma_start(io["sb_conv"][0, :, 2, :], fresh[3:3 + NB, :]).then_inc(stored, 16)
                sp.wait_ge(stored, 48)

            @block.tensor
            def _(pe):
                for f in range(NF):
                    nc.tensor.transpose(m.ps[0:3 + NB, 1 + f // 4, f % 4 * P:f % 4 * P + P],
                                        m.mixT[:, f, L - 3:T], m.ident[:])
                pe.wait_ge(past_in, 32)
                n = taps + CONV
                for f in range(NF):
                    last = nc.tensor.transpose(m.ps[:, 0, f * n:f * n + n], past[:, f * P:(f + 1) * P],
                                               m.ident[0:n, 0:n])
                last.then_inc(turned, 1)

            @block.scalar
            def _(act):
                n = taps + CONV
                act.wait_ge(turned, 1)
                nc.scalar.copy(pastT[:], m.ps[:, 0, 0:NF * n].rearrange("p (f n) -> p f n", n=n)).then_inc(copied, 1)
                nc.scalar.copy(fresh[:].rearrange("p (a b) -> p a b", b=512), m.ps[0:3 + NB, 1:4, :])\
                    .then_inc(copied, 1)
                act.wait_ge(sample_out, 1)
                nc.scalar.activation(m.mixT[:, :, L:T], ys[:, 0], ACT.Silu)
                with act.Fori(0, NF // 2) as i:
                    for s in range(2):
                        act.wait_ge(conv_out, 2 * i + s + 1)
                        nc.scalar.activation(m.mixT[:, bass.ds(2 * i + s, 1), 0:L], y[:, s], ACT.Silu)\
                            .then_inc(silued, 1)

            @block.vector
            def _(dve):
                dve.wait_ge(copied, 2)
                steps = Steps(dve, conv_step)
                w = lambda i: pastT[:, :, taps + i:taps + i + 1].to_broadcast([P, NF, NB])
                old = pastT[:, :, 0:taps].rearrange("p f (b r) -> p f b r", r=3)
                steps.after(nc.vector.tensor_tensor(ys[:, 0], m.mixT[:, :, L:T], w(3), ALU.mult))
                for r in range(3):
                    steps.after(nc.vector.tensor_tensor(ys[:, 1], old[:, :, :, r], w(r), ALU.mult))
                    ins = nc.vector.tensor_tensor(ys[:, 0], ys[:, 0], ys[:, 1], ALU.add)
                    if r < 2:
                        steps.after(ins)
                ins.then_inc(sample_out, 1)
                dve.sem_inc(silued, 2)
                n0 = steps.n
                with dve.Fori(0, NF // 2) as i:
                    steps = Steps(dve, conv_step, 6 * i + n0)
                    for s in range(2):
                        f = bass.ds(2 * i + s, 1)
                        x = lambda a, b: m.mixT[:, f, a:b]
                        tap = lambda k: pastT[:, f, taps + k:taps + k + 1].rearrange("p a b -> p (a b)")
                        dve.wait_ge(silued, 2 * i + s + 1)
                        steps.after(nc.vector.tensor_scalar(y[:, s:s + 1, :], x(0, L), tap(3), None, ALU.mult))
                        for k in range(1, CONV):
                            ins = nc.vector.scalar_tensor_tensor(out=y[:, s:s + 1, k:L], in0=x(0, L - k),
                                                                 scalar=tap(3 - k), in1=y[:, s:s + 1, k:L],
                                                                 op0=ALU.mult, op1=ALU.add)
                            if k < CONV - 1:
                                steps.after(ins)
                        ins.then_inc(conv_out, 1)


def normalise_qk(nc, m, io):
    with ExitStack() as own:
        E = own.enter_context
        sq = E(nc.sbuf_tensor("l2_sq", [P, 2, T], F32))
        root = E(nc.sbuf_tensor("l2_root", [P, 2, T], F32))
        epsq = E(nc.sbuf_tensor("l2_epsq", [P, 1], F32))
        squared, summed, rooted, scaled, inverse, eps_set = (
            m.sem("l2_" + x) for x in ("squared", "summed", "rooted", "scaled", "inverse", "eps_set"))
        NS = len(SLICES)
        with nc.Block() as block:
            @block.scalar
            def _(act):
                act.sem_inc(rooted, 2)
                act.wait_ge(eps_set, 1)

                def square(n, s):
                    act.wait_ge(summed, n + 1)
                    nc.scalar.activation(sq[:, s:s + 1], m.mixT[:, bass.ds(n, 1), :], ACT.Square)\
                        .then_inc(squared, 1)

                def roots(n, s, scale, eps):
                    act.wait_ge(summed, n + 3)
                    act.wait_ge(scaled, n + 1)
                    for k, (t0, tn) in enumerate(SLICES):
                        last = nc.scalar.activation(root[:, s, t0:t0 + tn], m.ps[:, NS * s + k, 0:tn], ACT.Sqrt,
                                                    scale=scale, bias=eps)
                    last.then_inc(rooted, 1)

                for base, scale, eps in ((0, float(P), epsq[:, 0:1]), (2, 1.0, m.eps[:, 0:1])):
                    with act.Fori(0, 2) as i:
                        for s in range(2):
                            square(2 * (base + i) + s, s)
                        for s in range(2):
                            roots(2 * (base + i) + s, s, scale, eps)

            @block.tensor
            def _(pe):
                pe.sem_inc(summed, 2)
                with pe.Fori(0, B_H) as i:
                    for s in range(2):
                        pe.wait_ge(squared, 2 * i + s + 1)
                        pe.wait_ge(rooted, 2 * i + s + 1)
                        for k, (t0, tn) in enumerate(SLICES):
                            last = nc.tensor.matmul(m.ps[:, NS * s + k, 0:tn], m.ones[:], sq[:, s, t0:t0 + tn],
                                                    start=True, stop=True)
                        last.then_inc(summed, 1)

            @block.vector
            def _(dve):
                dve.memset(epsq[:], EPS * P).then_inc(eps_set, 1)
                dve.sem_inc(scaled, 2)
                with dve.Fori(0, B_H) as i:
                    for s in range(2):
                        n = 2 * i + s
                        dve.wait_ge(rooted, n + 3)
                        nc.vector.reciprocal(root[:, s], root[:, s]).then_inc(inverse, 1)
                        dve.wait_ge(inverse, n + 1)
                        nc.vector.tensor_tensor(m.mixT[:, bass.ds(n, 1), :], m.mixT[:, bass.ds(n, 1), :],
                                                root[:, s:s + 1], ALU.mult).then_inc(scaled, 1)


def delta_gates(nc, m, io):
    NG = NT + NB
    with ExitStack() as own:
        E = own.enter_context
        x = E(nc.sbuf_tensor("dg_x", [P, NG, 4], F32))
        e = E(nc.sbuf_tensor("dg_e", [P, NG, 4], F32))
        e2 = E(nc.sbuf_tensor("dg_e2", [P, NG, 4], F32))
        per_head = E(nc.sbuf_tensor("dg_head", [P, 2, 4], F32))
        rate = E(nc.sbuf_tensor("dg_rate", [P, 4], F32))
        cleared, raw_in, magnitude, exps, step = (m.sem("dg_" + n) for n in
                                                  ("cleared", "raw_in", "magnitude", "exps", "step"))
        with nc.Block() as block:
            @block.sync
            def _(sp):
                c0 = TOK_R + 512
                sp.wait_ge(cleared, 1)
                sp.dma_start(m.gates[:, 0:FULL, :], m.tok[0:FULL * P, c0:c0 + 8].rearrange("(t p) c -> p t c", p=P))\
                    .then_inc(raw_in, 16)
                sp.dma_start(m.gates[0:TAIL, FULL, :], m.tok[FULL * P:L, c0:c0 + 8]).then_inc(raw_in, 16)
                sample = m.tok[L:T, c0:c0 + 8].rearrange("(o b) c -> o b c", o=1).to_broadcast([P, NB, 8])
                sp.dma_start(m.gates[:, NT:NG, :], sample).then_inc(raw_in, 16)
                sp.dma_start(per_head[:, 0], io["dt_bias_b"].to_broadcast([P, 4])).then_inc(raw_in, 16)
                sp.dma_start(per_head[:, 1], io["a_log_b"].to_broadcast([P, 4])).then_inc(raw_in, 16)

            @block.scalar
            def _(act):
                act.wait_ge(raw_in, 80)
                nc.scalar.activation(rate[:], per_head[:, 1], ACT.Exp)
                nc.scalar.activation(e2[:], m.gates[:, :, 4:8], ACT.Exp, scale=-1.0)
                act.wait_ge(magnitude, 1)
                nc.scalar.activation(e[:], e[:], ACT.Exp, scale=-1.0).then_inc(exps, 1)
                act.wait_ge(exps, 1)
                nc.scalar.activation(e[:], e[:], ACT.Ln, bias=m.ones[:, 0:1]).then_inc(exps, 1)

            @block.vector
            def _(dve):
                dve.memset(m.gates[:, FULL, :], 0.0).then_inc(cleared, 1)
                dve.wait_ge(raw_in, 80)
                steps = Steps(dve, step)
                head = lambda ap: ap.rearrange("p (o h) -> p o h", o=1).to_broadcast([P, NG, 4])
                steps.after(nc.vector.tensor_tensor(x[:], m.gates[:, :, 0:4], head(per_head[:, 0]), ALU.add))
                nc.vector.scalar_tensor_tensor(out=e[:], in0=x[:], scalar=-1.0, in1=x[:], op0=ALU.mult, op1=ALU.max)\
                    .then_inc(magnitude, 1)
                dve.wait_ge(exps, 2)
                steps.after(nc.vector.scalar_tensor_tensor(out=x[:], in0=x[:], scalar=0.0, in1=e[:], op0=ALU.max,
                                                           op1=ALU.add))
                steps.after(nc.vector.scalar_tensor_tensor(out=m.gates[:, :, 0:4], in0=x[:], scalar=-1.0,
                                                           in1=head(rate[:]), op0=ALU.mult, op1=ALU.mult))
                steps.after(nc.vector.tensor_scalar(e2[:], e2[:], 1.0, None, ALU.add))
                nc.vector.reciprocal(m.gates[:, :, 4:8], e2[:])



def delta_prompt(nc, m, io):
    C4 = [P, B_H, P]
    with ExitStack() as own:
        E = own.enter_context
        sb = lambda name, shape=C4: E(nc.sbuf_tensor("dp_" + name, shape, F32))
        qkv = sb("qkv", [P, 12, P])
        state = sb("state")
        gu, far, decay, low, up = sb("gu"), sb("far"), sb("decay"), sb("low"), sb("up")
        cums = sb("cums", [P, 8])
        ecum, erest, etot, nbg = (sb(x, [P, B_H]) for x in ("ecum", "erest", "etot", "nbg"))
        N, NT_, D1, D1T = sb("N"), sb("NT"), sb("D1"), sb("D1T")
        N2, N2T, N4, G1, G1T = sb("N2"), sb("N2T"), sb("N4"), sb("G1"), sb("G1T")
        T_, TT, U = sb("T"), sb("TT"), sb("U")
        between = sb("between", [P, 4, B_H, P])
        qk, kd, vb, u = sb("qk"), sb("kd"), sb("vb"), sb("u")
        rhs, o, osq, y = gu, G1T, N2, D1
        oss, ors = sb("oss", [P, B_H]), sb("ors", [P, B_H])
        gate = sb("gate", [P, 512])
        masks = sb("masks", [P, 7, P])
        norm_g = sb("norm_g", [P, 1])
        names = ("masks_in state_zero staged gu_ready sums_mm rows_mm cums_out far_out decayed masked kk_mm qk_mm "
                 "turn_mm n_out nt_mm nt_out blocks_out between_out sq_mm sq_out quad_mm quad_out t8_mm "
                 "t8_out lt_mm lt_out lift_mm lift_out ks_mm rhs_out u_mm u_out qs_mm o_part o_mm o_out "
                 "ds_mm state_out oss_out ors_root y_out y_mm y_turned gate_in exps_out scaled_out own_step "
                 "chunk_done state_stored").split()
        s = {x: m.sem("dp_" + x) for x in names}
        UPPER, STRICT, EIGHT = 0, 1, 2
        ps4 = lambda bank, r, c: m.ps[:, bank, :].rearrange("p (h c) -> p h c", h=B_H)[0:r, :, 0:c]

        def over_chunks(eng, body):
            with eng.Fori(0, FULL) as c:
                body(c, P)
            body(FULL, TAIL)

        def spans(C):
            return [b for b in (8, 16, 32, 64) if b < C]

        with nc.Block() as block:
            @block.sync
            def _(sp):
                sp.dma_start(masks[:], io["c_delta_masks"]).then_inc(s["masks_in"], 16)
                with nc.allow_non_contiguous_dma(reason="a gain vector onto partitions"):
                    sp.dma_start(norm_g[:], io["norm_b"].rearrange("o p -> p o")).then_inc(s["masks_in"], 16)

                def chunk(c, C):
                    sp.wait_ge(s["y_out"], c + 1)
                    sp.dma_start(gate[0:C, :], m.tok[bass.ds(c * P, C), TOK_R:TOK_R + 512]).then_inc(s["gate_in"], 16)

                over_chunks(sp, chunk)
                sp.wait_ge(s["state_out"], NT)
                sp.dma_start(io["pb_s"][0, 0].rearrange("h k v -> k h v"), state[:]).then_inc(s["state_stored"], 16)
                sp.wait_ge(s["state_stored"], 16)

            @block.gpsimd
            def _(pool):
                pool.wait_ge(s["masks_in"], 32)

                def chunk(c, C):
                    bc = lambda i: masks[0:C, i:i + 1, 0:C].to_broadcast([C, B_H, C])
                    col = lambda ap: ap.rearrange("p (h o) -> p h o", o=1).to_broadcast([C, B_H, C])
                    g = lambda a: m.gates[0:C, bass.ds(c, 1), a:a + 4].rearrange("p o h -> p (o h)")
                    pool.wait_ge(s["chunk_done"], c + 1)
                    nc.gpsimd.tensor_copy(qkv[:, :, 0:C], m.mixT[:, :, bass.ds(c * P, C)]).then_inc(s["staged"], 1)
                    nc.gpsimd.tensor_tensor(gu[0:C, :, 0:C], bc(UPPER), col(g(0)), ALU.mult).then_inc(s["gu_ready"], 1)
                    pool.wait_ge(s["decayed"], c + 1)
                    nc.gpsimd.tensor_tensor(up[0:C, :, 0:C], decay[0:C, :, 0:C], bc(UPPER), ALU.mult)\
                        .then_inc(s["masked"], 1)
                    nc.gpsimd.tensor_tensor(low[0:C, :, 0:C], decay[0:C, :, 0:C], bc(STRICT), ALU.mult)\
                        .then_inc(s["masked"], 1)
                    pool.wait_ge(s["masked"], 3 * c + 2)
                    nc.gpsimd.tensor_tensor(low[0:C, :, 0:C], low[0:C, :, 0:C], col(g(4)), ALU.mult)\
                        .then_inc(s["masked"], 1)
                    pool.wait_ge(s["nt_out"], c + 1)
                    for j, b in enumerate(spans(C)):
                        last = nc.gpsimd.tensor_tensor(between[0:C, j, :, 0:C], NT_[0:C, :, 0:C], bc(3 + j), ALU.mult)
                    last.then_inc(s["between_out"], 1)

                over_chunks(pool, chunk)

            @block.scalar
            def _(act):
                def chunk(c, C):
                    act.wait_ge(s["cums_out"], c + 1)
                    nc.scalar.activation(etot[:], cums[:, 4:8], ACT.Exp)
                    nc.scalar.activation(ecum[0:C], cums[0:C, 0:4], ACT.Exp)
                    nc.scalar.activation(erest[0:C], erest[0:C], ACT.Exp).then_inc(s["exps_out"], 1)
                    act.wait_ge(s["far_out"], c + 1)
                    nc.scalar.activation(decay[0:C, :, 0:C], far[0:C, :, 0:C], ACT.Exp, scale=-1.0)\
                        .then_inc(s["decayed"], 1)
                    act.wait_ge(s["nt_mm"], c + 1)
                    nc.scalar.copy(NT_[0:C, :, 0:C], ps4(6, C, C)).then_inc(s["nt_out"], 1)
                    act.wait_ge(s["sq_mm"], c + 1)
                    nc.scalar.copy(N2[0:C, :, 0:C], ps4(7, C, C))
                    nc.scalar.copy(N2T[0:C, :, 0:C], ps4(0, C, C)).then_inc(s["sq_out"], 1)
                    act.wait_ge(s["quad_mm"], c + 1)
                    nc.scalar.copy(N4[0:C, :, 0:C], ps4(1, C, C)).then_inc(s["quad_out"], 1)
                    n = len(spans(C))
                    for j in range(n):
                        act.wait_ge(s["lt_mm"], 4 * c + j + 1)
                        nc.scalar.copy(U[0:C, :, 0:C], ps4(4, C, C)).then_inc(s["lt_out"], 1)
                    act.wait_ge(s["u_mm"], c + 1)
                    nc.scalar.copy(u[0:C], ps4(2, C, P)).then_inc(s["u_out"], 1)
                    act.wait_ge(s["o_out"], c + 1)
                    for h in range(B_H):
                        last = nc.scalar.activation(osq[0:C, h], o[0:C, h], ACT.Square, accum_out=oss[0:C, h:h + 1])
                    last.then_inc(s["oss_out"], 1)
                    act.wait_ge(s["oss_out"], c + 1)
                    nc.scalar.activation(ors[0:C], oss[0:C], ACT.Sqrt, scale=1.0 / P, bias=m.eps[0:C, 0:1])\
                        .then_inc(s["ors_root"], 1)
                    act.wait_ge(s["y_mm"], c + 1)
                    nc.scalar.activation(m.actT[:, H:H + B_H, bass.ds(c * P, C)], ps4(5, P, C), ACT.Copy,
                                         scale=norm_g[:, 0:1]).then_inc(s["y_turned"], 1)

                over_chunks(act, chunk)

            @block.vector
            def _(dve):
                dve.memset(state[:], 0.0).then_inc(s["state_zero"], 1)
                dve.sem_inc(s["y_out"], 1)
                STEPS = {P: 8, TAIL: 8}

                def chunk(c, C):
                    w = (slice(0, C), slice(None), slice(0, C))
                    bc = lambda i: masks[0:C, i:i + 1, 0:C].to_broadcast([C, B_H, C])
                    col = lambda ap, n: ap.rearrange("p (h o) -> p h o", o=1).to_broadcast([C, B_H, n])
                    beta = m.gates[0:C, bass.ds(c, 1), 4:8].rearrange("p o h -> p (o h)")
                    steps = Steps(dve, s["own_step"], 8 * c)
                    dve.wait_ge(s["sums_mm"], c + 1)
                    steps.after(nc.vector.tensor_copy(cums[0:P], m.ps[0:P, 0, 0:8]))
                    nc.vector.tensor_tensor(erest[0:C], cums[0:C, 4:8], cums[0:C, 0:4], ALU.subtract)\
                        .then_inc(s["cums_out"], 1)
                    dve.wait_ge(s["rows_mm"], c + 1)
                    steps.after(nc.vector.tensor_tensor(far[w], ps4(1, C, C), col(cums[0:C, 0:4], C), ALU.subtract))
                    nc.vector.scalar_tensor_tensor(out=far[w], in0=far[w], scalar=-1.0, in1=far[w], op0=ALU.mult,
                                                   op1=ALU.max).then_inc(s["far_out"], 1)
                    dve.wait_ge(s["exps_out"], c + 1)
                    steps.after(nc.vector.scalar_tensor_tensor(out=nbg[0:C], in0=ecum[0:C], scalar=-1.0, in1=beta,
                                                               op0=ALU.mult, op1=ALU.mult))
                    dve.wait_ge(s["turn_mm"], c + 1)
                    nc.vector.tensor_tensor(kd[0:C], ps4(4, C, P), col(erest[0:C], P), ALU.mult)
                    nc.vector.tensor_tensor(vb[0:C], ps4(5, C, P), col(beta, P), ALU.mult).then_inc(s["scaled_out"], 1)
                    dve.wait_ge(s["masked"], 3 * c + 3)
                    nc.vector.tensor_tensor(qk[w], ps4(3, C, C), up[w], ALU.mult)
                    nc.vector.tensor_tensor(N[w], ps4(2, C, C), low[w], ALU.mult).then_inc(s["n_out"], 1)
                    dve.wait_ge(s["n_out"], c + 1)
                    nc.vector.tensor_tensor(D1[w], N[w], bc(EIGHT), ALU.mult)
                    dve.wait_ge(s["nt_out"], c + 1)
                    nc.vector.tensor_tensor(D1T[w], NT_[w], bc(EIGHT), ALU.mult).then_inc(s["blocks_out"], 1)
                    ident = m.ident[0:C, 0:C].rearrange("p (o c) -> p o c", o=1).to_broadcast([C, B_H, C])
                    dve.wait_ge(s["blocks_out"], c + 1)
                    nc.vector.tensor_tensor(G1[w], ident, D1[w], ALU.subtract)
                    steps.after(nc.vector.tensor_tensor(G1T[w], ident, D1T[w], ALU.subtract))
                    dve.wait_ge(s["sq_out"], c + 1)
                    nc.vector.tensor_tensor(G1[w], G1[w], N2[w], ALU.add)
                    steps.after(nc.vector.tensor_tensor(G1T[w], G1T[w], N2T[w], ALU.add))
                    dve.wait_ge(s["quad_mm"], c + 1)
                    nc.vector.tensor_tensor(G1[w], G1[w], ps4(2, C, C), ALU.subtract)
                    nc.vector.tensor_tensor(G1T[w], G1T[w], ps4(3, C, C), ALU.subtract).then_inc(s["quad_out"], 1)
                    dve.wait_ge(s["t8_mm"], c + 1)
                    nc.vector.tensor_tensor(T_[w], G1[w], ps4(6, C, C), ALU.add)
                    nc.vector.tensor_tensor(TT[w], G1T[w], ps4(7, C, C), ALU.add).then_inc(s["t8_out"], 1)
                    for j in range(len(spans(C))):
                        dve.wait_ge(s["lift_mm"], 4 * c + j + 1)
                        nc.vector.tensor_tensor(T_[w], T_[w], ps4(6, C, C), ALU.subtract)
                        nc.vector.tensor_tensor(TT[w], TT[w], ps4(7, C, C), ALU.subtract).then_inc(s["lift_out"], 1)
                        dve.wait_ge(s["lift_out"], 4 * c + j + 1)
                    dve.wait_ge(s["ks_mm"], c + 1)
                    for h in range(B_H):
                        last = nc.vector.scalar_tensor_tensor(out=rhs[0:C, h], in0=ps4(0, C, P)[:, h],
                                                              scalar=nbg[0:C, h:h + 1], in1=vb[0:C, h],
                                                              op0=ALU.mult, op1=ALU.add)
                    last.then_inc(s["rhs_out"], 1)
                    steps.after(nc.vector.tensor_tensor(o[0:C], ps4(1, C, P), col(ecum[0:C], P), ALU.mult))
                    dve.wait_ge(s["o_mm"], c + 1)
                    nc.vector.tensor_tensor(o[0:C], o[0:C], ps4(3, C, P), ALU.add).then_inc(s["o_out"], 1)
                    dve.wait_ge(s["ds_mm"], c + 1)
                    for h in range(B_H):
                        last = nc.vector.scalar_tensor_tensor(out=state[:, h], in0=state[:, h],
                                                              scalar=etot[:, h:h + 1], in1=ps4(4, P, P)[:, h],
                                                              op0=ALU.mult, op1=ALU.add)
                    last.then_inc(s["state_out"], 1)
                    dve.wait_ge(s["ors_root"], c + 1)
                    steps.after(nc.vector.reciprocal(ors[0:C], ors[0:C]))
                    g4 = gate[0:C, :].rearrange("p (h d) -> p h d", h=B_H)
                    dve.wait_ge(s["gate_in"], 16 * c + 16)
                    steps.after(nc.vector.tensor_tensor(y[0:C], o[0:C], g4, ALU.mult))
                    nc.vector.tensor_tensor(y[0:C], y[0:C], col(ors[0:C], P), ALU.mult).then_inc(s["y_out"], 1)
                    assert steps.n == 8, steps.n

                over_chunks(dve, chunk)

            @block.tensor
            def _(pe):
                pe.sem_inc(s["chunk_done"], 1)
                pe.wait_ge(s["masks_in"], 32)
                pe.wait_ge(s["state_zero"], 1)

                def chunk(c, C):
                    def four(bank, lhs, rhs, r, n, turn=False):
                        for h in range(B_H):
                            out = m.ps[0:r, bank, h * P:h * P + n]
                            if turn:
                                last = nc.tensor.transpose(out, lhs(h), rhs)
                            else:
                                last = nc.tensor.matmul(out, lhs(h), rhs(h), start=True, stop=True)
                        return last

                    cc = lambda t: (lambda h: t[0:C, h, 0:C])
                    full = lambda t: (lambda h: t[0:C, h, :])
                    q = lambda h: qkv[:, h, 0:C]
                    k = lambda h: qkv[:, 4 + h, 0:C]
                    v = lambda h: qkv[:, 8 + h, 0:C]
                    S = lambda h: state[:, h, :]
                    g = m.gates[0:C, bass.ds(c, 1), 0:4].rearrange("p o h -> p (o h)")
                    pe.wait_ge(s["staged"], c + 1)
                    nc.tensor.matmul(m.ps[0:C, 0, 0:4], masks[0:C, UPPER, 0:C], g, start=True, stop=True)
                    nc.tensor.matmul(m.ps[:, 0, 4:8], m.ones[0:C, :], g, start=True, stop=True).then_inc(s["sums_mm"], 1)
                    pe.wait_ge(s["gu_ready"], c + 1)
                    nc.tensor.matmul(ps4(1, C, C), m.ones[0:C, 0:C], gu[0:C, :, 0:C], start=True, stop=True)\
                        .then_inc(s["rows_mm"], 1)
                    four(2, k, k, C, C)
                    four(3, k, q, C, C)
                    four(4, k, m.ident[:], C, P, turn=True)
                    four(5, v, m.ident[:], C, P, turn=True).then_inc(s["turn_mm"], 1)
                    pe.wait_ge(s["n_out"], c + 1)
                    four(6, cc(N), m.ident[0:C, 0:C], C, C, turn=True).then_inc(s["nt_mm"], 1)
                    pe.wait_ge(s["blocks_out"], c + 1)
                    four(7, cc(D1T), cc(D1), C, C)
                    four(0, cc(D1), cc(D1T), C, C).then_inc(s["sq_mm"], 1)
                    pe.wait_ge(s["sq_out"], c + 1)
                    four(1, cc(N2T), cc(N2), C, C)
                    four(2, cc(D1T), cc(N2), C, C)
                    four(3, cc(N2), cc(D1T), C, C).then_inc(s["quad_mm"], 1)
                    pe.wait_ge(s["quad_out"], 2 * c + 2)
                    four(6, cc(G1T), cc(N4), C, C)
                    four(7, cc(N4), cc(G1T), C, C).then_inc(s["t8_mm"], 1)
                    pe.wait_ge(s["between_out"], c + 1)
                    pe.wait_ge(s["t8_out"], c + 1)
                    for j in range(len(spans(C))):
                        if j:
                            pe.wait_ge(s["lift_out"], 4 * c + j)
                        four(4, lambda h: between[0:C, j, h, 0:C], cc(T_), C, C).then_inc(s["lt_mm"], 1)
                        pe.wait_ge(s["lt_out"], 4 * c + j + 1)
                        four(6, cc(TT), cc(U), C, C)
                        four(7, cc(U), cc(TT), C, C).then_inc(s["lift_mm"], 1)
                    pe.wait_ge(s["lift_out"], 4 * c + len(spans(C)))
                    four(0, k, S, C, P)
                    four(1, q, S, C, P).then_inc(s["ks_mm"], 1)
                    pe.wait_ge(s["rhs_out"], c + 1)
                    four(2, cc(TT), full(rhs), C, P).then_inc(s["u_mm"], 1)
                    pe.wait_ge(s["u_out"], c + 1)
                    four(3, cc(qk), full(u), C, P).then_inc(s["o_mm"], 1)
                    four(4, full(kd), full(u), P, P).then_inc(s["ds_mm"], 1)
                    pe.wait_ge(s["y_out"], c + 2)
                    four(5, full(y), m.ident[0:C, 0:C], P, C, turn=True).then_inc(s["y_mm"], 1)
                    pe.wait_ge(s["state_out"], c + 1)
                    pe.wait_ge(s["y_turned"], c + 1)
                    pe.sem_inc(s["chunk_done"], 1)

                over_chunks(pe, chunk)



def delta_samples(nc, m, io):
    NS_ = NB * B_H
    with ExitStack() as own:
        E = own.enter_context
        sb = lambda name, shape: E(nc.sbuf_tensor("ds_" + name, shape, F32))
        S = sb("state", [P, NS_, P])
        eg, t, u = sb("eg", [P, NB, B_H]), sb("t", [P, NB, B_H]), sb("u", [P, NB, B_H])
        diag, ku = sb("diag", [P, B_H, P]), sb("ku", [P, B_H, P])
        gate, norm_g = sb("gate", [NB, 512]), sb("norm_g", [P, 1])
        o, osq, rs = sb("o", [P, NB, B_H]), sb("osq", [P, NS_]), sb("rs", [P, NS_])
        names = "in_ eg_out ks_mm own_step diag_out bcast_mm ku_out state_out o_mm osq_out sum_mm rs_out gate_mm stored"
        s = {x: m.sem("ds_" + x) for x in names.split()}
        heads = lambda f: m.mixT[:, f:f + B_H, L:T].rearrange("p h b -> p b h")
        with nc.Block() as block:
            @block.sync
            def _(sp):
                sp.dma_start(S[:], io["state_b_s"][0].rearrange("b h k v -> k (b h) v")).then_inc(s["in_"], 16)
                sp.dma_start(gate[:], m.tok[L:T, TOK_R:TOK_R + 512]).then_inc(s["in_"], 16)
                with nc.allow_non_contiguous_dma(reason="a gain vector onto partitions"):
                    sp.dma_start(norm_g[:], io["norm_b"].rearrange("o p -> p o")).then_inc(s["in_"], 16)
                sp.wait_ge(s["state_out"], NB)
                sp.dma_start(io["sb_s"][0].rearrange("b h k v -> k (b h) v"), S[:]).then_inc(s["stored"], 16)
                sp.wait_ge(s["stored"], 16)

            @block.scalar
            def _(act):
                nc.scalar.activation(eg[:], m.gates[:, NT:NT + NB, 0:4], ACT.Exp).then_inc(s["eg_out"], 1)
                act.wait_ge(s["o_mm"], 1)
                nc.scalar.copy(o[:], m.ps[:, 3, 0:NS_].rearrange("p (b h) -> p b h", h=B_H))
                nc.scalar.activation(osq[:], m.ps[:, 3, 0:NS_], ACT.Square).then_inc(s["osq_out"], 1)
                act.wait_ge(s["sum_mm"], 1)
                nc.scalar.activation(rs[:], m.ps[:, 4, 0:NS_], ACT.Sqrt, scale=1.0 / P, bias=m.eps[:, 0:1])\
                    .then_inc(s["rs_out"], 1)

            @block.tensor
            def _(pe):
                pe.wait_ge(s["in_"], 48)
                for n in range(NS_):
                    last = nc.tensor.matmul(m.ps[:, 0, n:n + 1], S[:, n, :], m.mixT[:, B_H + n % B_H, L + n // B_H:
                                                                                   L + n // B_H + 1],
                                            start=True, stop=True)
                last.then_inc(s["ks_mm"], 1)
                for h in range(B_H):
                    last = nc.tensor.transpose(m.ps[:, 5, h * NB:(h + 1) * NB], gate[:, h * P:(h + 1) * P],
                                               m.ident[0:NB, 0:NB])
                last.then_inc(s["gate_mm"], 1)
                with pe.Fori(0, NB) as b:
                    pe.wait_ge(s["diag_out"], b + 1)
                    nc.tensor.matmul(m.ps[:, 1, :].rearrange("p (h c) -> p h c", h=B_H), m.ones[:], diag[:],
                                     start=True, stop=True).then_inc(s["bcast_mm"], 1)
                pe.wait_ge(s["state_out"], NB)
                for n in range(NS_):
                    last = nc.tensor.matmul(m.ps[:, 3, n:n + 1], S[:, n, :],
                                            m.mixT[:, n % B_H, L + n // B_H:L + n // B_H + 1], start=True, stop=True)
                last.then_inc(s["o_mm"], 1)
                pe.wait_ge(s["osq_out"], 1)
                nc.tensor.matmul(m.ps[:, 4, 0:NS_], m.ones[:], osq[:], start=True, stop=True).then_inc(s["sum_mm"], 1)

            @block.vector
            def _(dve):
                steps = Steps(dve, s["own_step"])
                dve.wait_ge(s["eg_out"], 1)
                dve.wait_ge(s["ks_mm"], 1)
                steps.after(nc.vector.tensor_tensor(t[:], m.ps[:, 0, 0:NS_].rearrange("p (b h) -> p b h", h=B_H),
                                                    eg[:], ALU.mult))
                steps.after(nc.vector.tensor_tensor(t[:], heads(2 * B_H), t[:], ALU.subtract))
                steps.after(nc.vector.tensor_tensor(u[:], t[:], m.gates[:, NT:NT + NB, 4:8], ALU.mult))
                n0 = steps.n
                wide = lambda ap: ap.rearrange("p b h -> p h b").to_broadcast([P, B_H, P])
                eye = m.ident[:].rearrange("p (o c) -> p o c", o=1).to_broadcast([P, B_H, P])
                with dve.Fori(0, NB) as b:
                    steps = Steps(dve, s["own_step"], 2 * b + n0)
                    sample = S[:, bass.ds(4 * b, 4), :]
                    one = bass.ds(b, 1)
                    nc.vector.tensor_tensor(diag[:], eye, wide(u[:, one, :]), ALU.mult).then_inc(s["diag_out"], 1)
                    steps.after(nc.vector.tensor_tensor(sample, sample, wide(eg[:, one, :]), ALU.mult))
                    dve.wait_ge(s["bcast_mm"], b + 1)
                    k = m.mixT[:, B_H:2 * B_H, bass.ds(L + b, 1)].to_broadcast([P, B_H, P])
                    steps.after(nc.vector.tensor_tensor(ku[:], m.ps[:, 1, :].rearrange("p (h c) -> p h c", h=B_H), k,
                                                        ALU.mult))
                    nc.vector.tensor_tensor(sample, sample, ku[:], ALU.add).then_inc(s["state_out"], 1)
                steps = Steps(dve, s["own_step"], 2 * NB + n0)
                dve.wait_ge(s["osq_out"], 1)
                steps.after(nc.vector.tensor_scalar(o[:], o[:], norm_g[:, 0:1], None, ALU.mult))
                dve.wait_ge(s["gate_mm"], 1)
                steps.after(nc.vector.tensor_tensor(o[:], o[:], m.ps[:, 5, 0:NS_].rearrange("p (h b) -> p b h", b=NB),
                                                    ALU.mult))
                dve.wait_ge(s["rs_out"], 1)
                steps.after(nc.vector.reciprocal(rs[:], rs[:]))
                out = m.actT[:, H:H + B_H, L:T].rearrange("p h b -> p b h")
                nc.vector.tensor_tensor(out, o[:], rs[:].rearrange("p (b h) -> p b h", h=B_H), ALU.mult)



def bias_rows(nc, m, io):
    with ExitStack() as own:
        E = own.enter_context
        buckets = E(nc.sbuf_tensor("br_buckets", [33, BIAS_W], F32))
        table = E(nc.sbuf_tensor("br_table", [33, H], F32))
        farthest = E(nc.sbuf_tensor("br_far", [32, H], F32))
        rows = E(nc.sbuf_tensor("br_rows", [H, BIAS_W], F32))
        vec = E(nc.sbuf_tensor("br_vec", [P, 4, 64], F32))
        dots = E(nc.sbuf_tensor("br_dots", [P, 2], F32))
        names = "in_ table_out mm rows_out stored dots_out lam_exp step"
        s = {x: m.sem("br_" + x) for x in names.split()}
        parts = [(a, min(512, BIAS_W - a)) for a in range(0, BIAS_W, 512)]
        with nc.Block() as block:
            @block.sync
            def _(sp):
                sp.dma_start(buckets[:], io["c_buckets"]).then_inc(s["in_"], 16)
                sp.dma_start(table[0:32], io["bias_table"]).then_inc(s["in_"], 16)
                sp.dma_start(farthest[:], io["bias_table"][31:32, :].to_broadcast([32, H])).then_inc(s["in_"], 16)
                for j, v in enumerate((io["lam_q1"], io["lam_k1"], io["lam_q2"], io["lam_k2"])):
                    sp.dma_start(vec[:, j], v.to_broadcast([P, 64])).then_inc(s["in_"], 16)
                sp.wait_ge(s["rows_out"], 1)
                sp.dma_start(m.bias, rows[:]).then_inc(s["stored"], 16)
                sp.wait_ge(s["stored"], 16)

            @block.vector
            def _(dve):
                steps = Steps(dve, s["step"])
                dve.memset(table[32:33], NEG)
                dve.wait_ge(s["in_"], 112)
                nc.vector.tensor_tensor(table[0:32], table[0:32], farthest[:], ALU.subtract).then_inc(s["table_out"], 1)
                for j in range(2):
                    steps.after(nc.vector.tensor_tensor(vec[:, 2 * j], vec[:, 2 * j], vec[:, 2 * j + 1], ALU.mult))
                    last = nc.vector.tensor_reduce(dots[:, j:j + 1], vec[:, 2 * j], AX, ALU.add)
                last.then_inc(s["dots_out"], 1)
                dve.wait_ge(s["mm"], 1)
                for j, (a, n) in enumerate(parts):
                    last = nc.vector.tensor_copy(rows[:, a:a + n], m.ps[0:H, j, 0:n])
                last.then_inc(s["rows_out"], 1)
                dve.wait_ge(s["lam_exp"], 1)
                steps.after(nc.vector.tensor_tensor(m.lam[:], dots[:, 1:2], dots[:, 0:1], ALU.subtract))
                nc.vector.tensor_scalar(m.lam[:], m.lam[:], -LAM_INIT, None, ALU.add)

            @block.scalar
            def _(act):
                act.wait_ge(s["dots_out"], 1)
                nc.scalar.activation(dots[:], dots[:], ACT.Exp).then_inc(s["lam_exp"], 1)

            @block.tensor
            def _(pe):
                pe.wait_ge(s["table_out"], 1)
                for j, (a, n) in enumerate(parts):
                    last = nc.tensor.matmul(m.ps[0:H, j, 0:n], table[:], buckets[:, a:a + n], start=True, stop=True)
                last.then_inc(s["mm"], 1)


def load_kv(nc, m, tok, tag):
    with ExitStack() as own:
        E = own.enter_context
        k = E(nc.sbuf_tensor(f"{tag}_k", [P, NT, KV * P], F32))
        kv_in, turned, cleared = (m.sem(f"{tag}_{x}") for x in ("in", "turned", "cleared"))
        with nc.Block() as block:
            @block.sync
            def _(sp):
                sp.wait_ge(cleared, 1)
                for dst, c0 in ((k, TOK_K), (m.v, TOK_V)):
                    src = tok[:, c0:c0 + KV * P]
                    sp.dma_start(dst[:, 0:FULL, :], src[0:FULL * P].rearrange("(t p) c -> p t c", p=P))\
                        .then_inc(kv_in, 16)
                    sp.dma_start(dst[0:LAST, FULL, :], src[FULL * P:T]).then_inc(kv_in, 16)
                sp.wait_ge(kv_in, 64)

            @block.tensor
            def _(pe):
                pe.wait_ge(kv_in, 64)
                for g in range(KV):
                    for t in range(NT):
                        r = P if t < FULL else LAST
                        last = nc.tensor.transpose(m.ps[:, 3 * g + t // 4, t % 4 * P:t % 4 * P + r],
                                                   k[0:r, t, g * P:(g + 1) * P], m.ident[0:r, 0:r])
                last.then_inc(turned, 1)

            @block.vector
            def _(dve):
                dve.memset(m.v[:, FULL, :], 0.0).then_inc(cleared, 1)
                dve.wait_ge(turned, 1)
                for g in range(KV):
                    for j in range(3):
                        n = min(512, T - 512 * j)
                        nc.vector.tensor_copy(m.kT[:, g, 512 * j:512 * j + n], m.ps[:, 3 * g + j, 0:n])



class Plan:

    def __init__(self, t):
        self.t, self.R, self.nb, self.q0 = t, P if t < FULL else TAIL, t + 1, t * P
        self.W = self.q0 + self.R
        self.regions, self.turns, self.outs = ((0, 2), (4, 5), (6, 7)) if self.W <= 1024 else ((0, 3), (6, 6), (7, 7))
        self.groups = [(a, min(4, self.nb - a)) for a in range(0, self.nb, 4)]


def prompt_attention(nc, m, tok, diff, out_gain):
    NC = 2 if diff else 1
    tag = "aa" if diff else "ac"
    NEAR = 2 * P
    with ExitStack() as own:
        E = own.enter_context
        sb = lambda name, shape: E(nc.sbuf_tensor(f"{tag}_{name}", shape, F32))
        bias = sb("bias", [P, H, NEAR])
        q = sb("q", [P, 2, NC, P])
        prob = sb("prob", [P, 2, NC, L])
        mix = sb("mix", [P, 2, L]) if diff else None
        probT = sb("probT", [P, 2, NT, P])
        mx, den = sb("mx", [P, 2, NC]), sb("den", [P, 2, NC])
        gate, o, y = sb("gate", [P, 2, D]), sb("o", [P, 2, D]), sb("y", [P, D])
        upside = o[:].rearrange("p a (h c) -> p (a h) c", c=NEAR)
        flip = sb("flip", [P, P])
        oss, rs, minus_half = sb("oss", [P, H]), sb("rs", [P, H]), sb("minus_half", [P, H])
        gain = sb("gain", [P, 1])
        names = ("bias_in bias_mm bias_out gate_in gain_in gain_out q_ready scores_mm near_out maxed exp_half combined turned probs_out "
                 "pv_mm o_out rs_out y_ready y_mm y_turned half_set step step2 pool_step recip_out")
        s = {x: m.sem(f"{tag}_{x}") for x in names.split()}

        plans = [Plan(t) for t in range(NT)]
        turned_before = [sum(H * len(p.groups) for p in plans[:t]) for t in range(NT)]

        def region(p, n, c, w0, w1):
            at = p.regions[c if diff else n % 2] * 512
            return m.ps[:].rearrange("p b c -> p (b c)")[0:p.R, at + w0:at + w1]

        def over_heads(eng, p, parts):
            with eng.Fori(0, KV) as i:
                for part, j in parts:
                    part(p, i, j, p.t * H + i * G + j)

        lag = lambda first, second: [(first, 0), (first, 1), (second, 0), (first, 2), (second, 1), (first, 3),
                                     (second, 2), (second, 3)]

        with nc.Block() as block:
            @block.sync
            def _(sp):
                src = bass.AP(m.bias.tensor, FULL * P - P, [[1, P], [BIAS_W, H], [1, NEAR]])
                sp.dma_start(upside, src).then_inc(s["bias_in"], 16)
                sp.dma_start(flip[:], m.flip).then_inc(s["bias_in"], 16)
                with nc.allow_non_contiguous_dma(reason="a gain vector onto partitions"):
                    if diff:
                        sp.dma_start(gain[:], out_gain.rearrange("o p -> p o")).then_inc(s["gain_in"], 16)
                for p in plans:
                    if p.t >= 2:
                        sp.wait_ge(s["y_ready"], p.t - 1)
                    if p.t >= 1:
                        sp.wait_ge(s["gate_in"], 16 * p.t)
                    sp.dma_start(gate[0:p.R, p.t % 2, :], tok[p.q0:p.q0 + p.R, TOK_G:TOK_G + D])\
                        .then_inc(s["gate_in"], 16)

            @block.gpsimd
            def _(pool):
                nc.gpsimd.memset(minus_half[:], -0.5).then_inc(s["half_set"], 1)
                pool.wait_ge(s["half_set"], 1)
                if diff:
                    pool.wait_ge(s["gain_in"], 16)
                    nc.gpsimd.tensor_scalar(gain[:], gain[:], 1.0 - LAM_INIT, None, ALU.mult).then_inc(s["gain_out"], 1)

                def head(p, kv, j, n):
                    pool.wait_ge(s["scores_mm"], NC * n + NC)
                    alone(pool, m)
                    for c in range(NC):
                        last = nc.gpsimd.tensor_tensor(q[:, j % 2, c, 0:p.R],
                                                       m.qT[:, bass.ds(kv * G + j, 1), p.q0:p.q0 + p.R],
                                                       m.halves_wide[:, c if diff else 2, 0:p.R], ALU.mult)
                    last.then_inc(s["q_ready"], 1)

                for p in plans:
                    over_heads(pool, p, [(head, j) for j in range(G)])
                    if diff:
                        pool.wait_ge(s["rs_out"], 2 * p.t + 1)
                        nc.gpsimd.tensor_tensor(rs[0:p.R], rs[0:p.R], minus_half[0:p.R], ALU.pow).then_inc(s["rs_out"], 1)

            @block.tensor
            def _(pe):
                pe.wait_ge(s["bias_in"], 32)
                for k in range(4):
                    last = nc.tensor.matmul(m.ps[:, k, :].rearrange("p (h c) -> p h c", c=NEAR), flip[:],
                                            upside[:, 2 * k:2 * k + 2, :], start=True, stop=True)
                last.then_inc(s["bias_mm"], 1)
                pe.wait_ge(s["bias_out"], 1)
                pe.sem_inc(s["scores_mm"], 2 * NC)
                pe.wait_ge(s["half_set"], 1)

                def scores(p, kv, j, n):
                    pe.wait_ge(s["q_ready"], n + 1)
                    for c in range(NC):
                        if diff:
                            pe.wait_ge(s["exp_half"], NC * n + c + 1)
                        else:
                            pe.wait_ge(s["exp_half"], n + 1)
                        alone(pe, m)
                        for w in range(0, p.W, 512):
                            w1 = min(w + 512, p.W)
                            last = nc.tensor.matmul(region(p, j, c, w, w1), q[:, j % 2, c, 0:p.R],
                                                    m.kT[:, bass.ds(kv, 1), w:w1], start=True, stop=True)
                        last.then_inc(s["scores_mm"], 1)

                def outputs(p, kv, j, n):
                    src = mix[:, j % 2] if diff else prob[:, j % 2, 0]
                    pe.wait_ge(s["combined"] if diff else s["exp_half"], n + 3)
                    alone(pe, m)
                    g0 = turned_before[p.t] + (n - p.t * H) * len(p.groups)
                    for k, (b0, bn) in enumerate(p.groups):
                        bank = p.turns[k % 2]
                        if k >= len(set(p.turns)):
                            pe.wait_ge(s["probs_out"], g0 + k - len(set(p.turns)) + 1)
                            alone(pe, m)
                        for b in range(b0, b0 + bn):
                            w1 = min(b * P + P, p.W)
                            last = nc.tensor.transpose(m.ps[0:w1 - b * P, bank, (b - b0) * P:(b - b0) * P + p.R],
                                                       src[0:p.R, b * P:w1], m.ident[0:p.R, 0:p.R])
                        last.then_inc(s["turned"], 1)
                    pe.wait_ge(s["probs_out"], g0 + len(p.groups))
                    pe.wait_ge(s["o_out"], n + 1 if p.outs[0] != p.outs[1] else n + 2)
                    alone(pe, m)
                    for b in range(p.nb):
                        last = nc.tensor.matmul(m.ps[0:p.R, p.outs[j % 2], 0:P], probT[:, j % 2, b, 0:p.R],
                                                m.v[:, b, bass.ds(kv * P, P)], start=(b == 0),
                                                stop=(b == p.nb - 1))
                    last.then_inc(s["pv_mm"], 1)

                def turn_out(p):
                    pe.wait_ge(s["y_ready"], p.t + 1)
                    for h in range(H):
                        last = nc.tensor.transpose(m.ps[:, h // 4, h % 4 * P:h % 4 * P + p.R],
                                                   y[0:p.R, h * P:(h + 1) * P], m.ident[0:p.R, 0:p.R])
                    last.then_inc(s["y_mm"], 1)

                for p in plans:
                    if p.t == FULL:
                        pe.wait_ge(s["o_out"], FULL * H + 2)
                    over_heads(pe, p, lag(scores, outputs))
                    turn_out(p)
                    pe.wait_ge(s["y_turned"], p.t + 1)

            @block.scalar
            def _(act):
                def exps(p, kv, j, n):
                    if not diff:
                        act.wait_ge(s["o_out"], n + 1)
                    for c in range(NC):
                        act.wait_ge(s["maxed"], NC * n + c + 1)
                        if diff:
                            act.wait_ge(s["combined"], n + 1)
                        elif c == 0:
                            act.wait_ge(s["pv_mm"], n + 1)
                        dst = prob[0:p.R, j % 2, c, 0:p.W]
                        src = region(p, j, c, 0, p.W) if diff or p.t < 2 else dst
                        nc.scalar.activation(dst, src, ACT.Exp, bias=mx[0:p.R, j % 2, c:c + 1],
                                             accum_out=den[0:p.R, j % 2, c:c + 1]).then_inc(s["exp_half"], 1)

                def outputs(p, kv, j, n):
                    g0 = turned_before[p.t] + (n - p.t * H) * len(p.groups)
                    for k, (b0, bn) in enumerate(p.groups):
                        act.wait_ge(s["turned"], g0 + k + 1)
                        if k == 0:
                            act.wait_ge(s["pv_mm"], n + 1)
                        bank = p.turns[k % 2]
                        whole = bn if (b0 + bn) * P <= p.W else bn - 1
                        if whole:
                            last = nc.scalar.copy(
                                probT[:, j % 2, b0:b0 + whole, 0:p.R],
                                m.ps[:, bank, 0:whole * P].rearrange("p (b c) -> p b c", c=P)[:, :, 0:p.R])
                        if whole < bn:
                            K = p.W - (b0 + whole) * P
                            last = nc.scalar.copy(probT[0:K, j % 2, b0 + whole, 0:p.R],
                                                  m.ps[0:K, bank, whole * P:whole * P + p.R])
                        last.then_inc(s["probs_out"], 1)
                    act.wait_ge(s["pv_mm"], n + 3)
                    dst = o[0:p.R, p.t % 2, bass.ds((kv * G + j) * P, P)]
                    if diff:
                        nc.scalar.copy(dst, m.ps[0:p.R, p.outs[j % 2], 0:P]).then_inc(s["o_out"], 1)
                    else:
                        act.wait_ge(s["recip_out"], n + 1)
                        nc.scalar.activation(dst, m.ps[0:p.R, p.outs[j % 2], 0:P], ACT.Copy,
                                             scale=den[0:p.R, j % 2, 0:1]).then_inc(s["o_out"], 1)

                act.sem_inc(s["exp_half"], 2)
                act.sem_inc(s["o_out"], 2)
                act.sem_inc(s["pv_mm"], 2)
                if diff:
                    act.wait_ge(s["gain_out"], 1)
                for p in plans:
                    if p.t == FULL:
                        act.wait_ge(s["y_turned"], FULL)
                    over_heads(act, p, lag(exps, outputs))
                    act.wait_ge(s["y_mm"], p.t + 1)
                    for k in range(2):
                        src = m.ps[:, k, :].rearrange("p (h c) -> p h c", c=P)[:, :, 0:p.R]
                        dst = m.actT[:, 4 * k:4 * k + 4, p.q0:p.q0 + p.R]
                        if diff:
                            last = nc.scalar.activation(dst, src, ACT.Copy, scale=gain[:, 0:1])
                        else:
                            last = nc.scalar.copy(dst, src)
                    last.then_inc(s["y_turned"], 1)

            @block.vector
            def _(dve):
                dve.memset(probT[:, :, FULL, :], 0.0)
                dve.wait_ge(s["bias_mm"], 1)
                nc.vector.tensor_copy(bias[:], m.ps[:, 0:4, :].rearrange("p k (h c) -> p (k h) c", c=NEAR))\
                    .then_inc(s["bias_out"], 1)
                dve.wait_ge(s["bias_out"], 1)
                if diff:
                    dve.sem_inc(s["combined"], 2)

                def maxima(p, kv, j, n):
                    for c in range(NC):
                        dve.wait_ge(s["scores_mm"], NC * (n + 2) + c + 1)
                        near = max(0, p.q0 - P)
                        part = region(p, j, c, near, p.W)
                        at = near - p.q0 + P
                        nc.vector.tensor_tensor(part, part, bias[0:p.R, bass.ds(kv * G + j, 1), at:at + p.W - near],
                                                ALU.add).then_inc(s["near_out"], 1)
                        dve.wait_ge(s["near_out"], NC * n + c + 1)
                        dve.wait_ge(s["exp_half"], NC * n + 1 if diff else n + 1)
                        src = region(p, j, c, 0, p.W)
                        m1 = mx[0:p.R, j % 2, c:c + 1]
                        if diff or p.t < 2:
                            ins = nc.vector.tensor_reduce(m1, src, AX, ALU.max)
                        else:
                            dve.wait_ge(s["pv_mm"], n + 1)
                            alone(dve, m)
                            ins = nc.vector.tensor_tensor_reduce(out=prob[0:p.R, j % 2, c, 0:p.W], in0=src,
                                                                 in1=m.chosen[p.t][0:p.R, 0:p.W], scale=1.0,
                                                                 scalar=-3e38, op0=ALU.add, op1=ALU.max,
                                                                 accum_out=m1)
                        ins.then_inc(s["step"], 1)
                        dve.wait_ge(s["step"], NC * n + c + 1)
                        nc.vector.tensor_scalar(m1, m1, -1.0, None, ALU.mult).then_inc(s["maxed"], 1)

                def combine(p, kv, j, n):
                    dve.wait_ge(s["exp_half"], NC * n + NC + 2)
                    R = p.R
                    d = den[0:R, j % 2, :]
                    if not diff:
                        nc.vector.reciprocal(d, d).then_inc(s["recip_out"], 1)
                        return
                    steps = Steps(dve, s["step2"], 3 * n)
                    steps.after(nc.vector.reciprocal(d, d))
                    steps.after(nc.vector.tensor_tensor(d[:, 1:2], d[:, 1:2], m.lam[0:R], ALU.mult))
                    dve.wait_ge(s["pv_mm"], n + 1)
                    steps.after(nc.vector.tensor_scalar(mix[0:R, j % 2, 0:p.W], prob[0:R, j % 2, 0, 0:p.W],
                                                        d[:, 0:1], None, ALU.mult))
                    nc.vector.scalar_tensor_tensor(out=mix[0:R, j % 2, 0:p.W], in0=prob[0:R, j % 2, 1, 0:p.W],
                                                   scalar=d[:, 1:2], in1=mix[0:R, j % 2, 0:p.W], op0=ALU.mult,
                                                   op1=ALU.add).then_inc(s["combined"], 1)

                for p in plans:
                    over_heads(dve, p, lag(maxima, combine))
                    R = p.R
                    steps = Steps(dve, s["pool_step"], (3 if diff else 0) * p.t)
                    w = slice(0, R), p.t % 2
                    dve.wait_ge(s["o_out"], H * (p.t + 1) + 2)
                    dve.wait_ge(s["gate_in"], 16 * p.t + 16)
                    if p.t >= 1:
                        dve.wait_ge(s["y_mm"], p.t)
                    if diff:
                        steps.after(nc.vector.tensor_tensor(y[0:R], o[w], o[w], ALU.mult))
                        steps.after(nc.vector.tensor_reduce(oss[0:R], y[0:R].rearrange("p (h d) -> p h d", d=P), AX,
                                                            ALU.add))
                        nc.vector.tensor_scalar(rs[0:R], oss[0:R], 1.0 / P, EPS, ALU.mult, ALU.add)\
                            .then_inc(s["rs_out"], 1)
                        steps.after(nc.vector.tensor_tensor(y[0:R], o[w], gate[w], ALU.mult))
                        dve.wait_ge(s["rs_out"], 2 * p.t + 2)
                        y3 = y[0:R].rearrange("p (h d) -> p h d", d=P)
                        r3 = rs[0:R].rearrange("p (h o) -> p h o", o=1).to_broadcast([R, H, P])
                        nc.vector.tensor_tensor(y3, y3, r3, ALU.mult).then_inc(s["y_ready"], 1)
                    else:
                        nc.vector.tensor_tensor(y[0:R], o[w], gate[w], ALU.mult).then_inc(s["y_ready"], 1)



def sample_attention(nc, m, io, tok, diff, cache_k, cache_v, out_gain):
    NC = 2 if diff else 1
    RB = H * NC
    RG = G * NC
    R = NB * RB
    NO = NB * H
    QP = 4
    tag = "sa" if diff else "sc"
    with ExitStack() as own:
        E = own.enter_context
        sb = lambda name, shape: E(nc.sbuf_tensor(f"{tag}_{name}", shape, F32))
        qz = sb("qz", [P, NB * KV, R])
        ring = 4
        kpages = sb("kpages", [P, ring, QP, KV * P])
        kTs = sb("kTs", [P, KV, QP * P])
        vpages = sb("vpages", [P, 2, N_PAGES, KV * P])
        vnew, gate = sb("vnew", [NB, KV * P]), sb("gate", [NB, D])
        sel_b, sel_h, own_mask = sb("sel_b", [NB, R]), sb("sel_h", [H, R]), sb("own_mask", [NB, NB])
        near = sb("near", [H, PAGE + 1])
        prob = sb("prob", [R, PAST + NB])
        probT, newT = sb("probT", [P, N_PAGES, NO]), sb("newT", [NB, NO])
        mx, den, parity = sb("mx", [R, 2]), sb("den", [R, 2]), sb("parity", [R, 2])
        o, osq, rs = sb("o", [P, NO]), sb("osq", [P, NO]), sb("rs", [P, NO])
        gain = sb("gain", [P, 1])
        names = ("small_in zeroed q_out turned_a turned_d k_act k_dve scores_mm last_mm maxed step exped scaled pt_mm "
                 "pt_out pv_mm pv_b osq_out sum_mm rs_out gate_mm o_out")
        s = {x: m.sem(f"{tag}_{x}") for x in names.split()}
        k_in = [m.sem(f"{tag}_k_in{j}") for j in range(ring)]
        v_in = [m.sem(f"{tag}_v_in{j}") for j in range(2)]
        ck = cache_k.rearrange("n t a b c -> n t (a b c)") if diff else cache_k.rearrange("n t a b -> n t (a b)")
        cv = cache_v.rearrange("n t a b -> n t (a b)")
        N_PT = N_PAGES // QP
        n_small = 7 + (1 if diff else 0)

        with nc.Block() as block:
            @block.sync
            def _(sp):
                pool_pages = cache_k.shape[0]

                def page(dst, cache, index, sem):
                    at = sp.value_load(m.pages[0:1, bass.ds(index, 1)], min_val=0, max_val=pool_pages - 1)
                    sp.dma_start(dst, cache[bass.ds(at, 1), :, :].rearrange("o t c -> t (o c)")).then_inc(sem, 16)

                sp.dma_start(sel_b[:], io["c_sel_b2"] if diff else io["c_sel_b1"]).then_inc(s["small_in"], 16)
                sp.dma_start(sel_h[:], io["c_sel_h2"] if diff else io["c_sel_h1"]).then_inc(s["small_in"], 16)
                sp.dma_start(own_mask[:], io["c_own_mask"]).then_inc(s["small_in"], 16)
                sp.dma_start(parity[:], io["c_parity"][0:R]).then_inc(s["small_in"], 16)
                sp.dma_start(near[:], m.bias[:, FAR - PAGE:FAR + 1]).then_inc(s["small_in"], 16)
                sp.dma_start(vnew[:], tok[L:T, TOK_V:TOK_V + KV * P]).then_inc(s["small_in"], 16)
                sp.dma_start(gate[:], tok[L:T, TOK_G:TOK_G + D]).then_inc(s["small_in"], 16)
                if diff:
                    with nc.allow_non_contiguous_dma(reason="a gain vector onto partitions"):
                        sp.dma_start(gain[:], out_gain.rearrange("o p -> p o")).then_inc(s["small_in"], 16)
                with sp.Fori(0, N_PAGES // QP) as kq:
                    for b in range(NB):
                        slot = b % ring
                        sp.wait_ge(s["turned_d"], kq * NB + b + 1)
                        alone(sp, m)
                        for j in range(QP):
                            page(kpages[:, slot, j, :], ck, kq * QP + (b * N_PAGES + j), k_in[slot])
                with sp.Fori(0, NB // 2) as i:
                    for b in range(2):
                        sp.wait_ge(s["pv_b"], 2 * i + b + 1)
                        alone(sp, m)
                        for j in range(N_PAGES):
                            page(vpages[:, b, j, :], cv, i * (2 * N_PAGES) + (b * N_PAGES + j), v_in[b])

            @block.tensor
            def _(pe):
                pe.sem_inc(s["turned_d"], ring)
                pe.sem_inc(s["pv_b"], 2)
                pe.wait_ge(s["q_out"], 1)
                pe.wait_ge(s["small_in"], 16 * n_small)
                with pe.Fori(0, N_PAGES // QP) as kq:
                    def turn(b, g):
                        if g == 0:
                            pe.wait_ge(k_in[b % ring], (kq * (NB // ring) + b // ring) * (16 * QP) + 16 * QP)
                        pe.wait_ge(s["k_act"] if g == 0 else s["k_dve"], kq * NB + b + 1)
                        for j in range(QP):
                            last = nc.tensor.transpose(m.ps[:, 4 + g, j * P:(j + 1) * P],
                                                       kpages[:, b % ring, j, g * P:(g + 1) * P], m.ident[:])
                        last.then_inc(s["turned_a"] if g == 0 else s["turned_d"], 1)

                    def product(b, g):
                        pe.wait_ge(s["k_act"] if g == 0 else s["k_dve"], kq * NB + b + 2)
                        alone(pe, m)
                        last = nc.tensor.matmul(m.ps[0:R, bass.ds(kq, 1), :], qz[:, 2 * b + g, :], kTs[:, g, :],
                                                start=(b == 0 and g == 0), stop=(b == NB - 1 and g == KV - 1))
                        last.then_inc(s["scores_mm"], 1)

                    turn(0, 0)
                    for b in range(NB):
                        turn(b, 1)
                        product(b, 0)
                        if b < NB - 1:
                            turn(b + 1, 0)
                        product(b, 1)
                extra = dict(stop=True, skip_group_check=True)
                nc.tensor.matmul(m.ps[0:R, 3, 512 - PAGE:512], sel_h[:], near[:, 0:PAGE], start=False, **extra)
                if not diff:
                    for j in range(4):
                        nc.tensor.matmul(m.ps[0:R, j, :], sel_b[:], m.chosen_s[:, 512 * j:512 * j + 512],
                                         start=False, **extra)
                    nc.tensor.matmul(m.ps[0:R, 6, 0:NB], sel_b[:], m.chosen_s[:, PAST:PAST + NB], start=True,
                                     stop=False)
                else:
                    nc.tensor.matmul(m.ps[0:R, 6, 0:NB], sel_b[:], own_mask[:], start=True, stop=False)
                nc.tensor.matmul(m.ps[0:R, 6, 0:NB], sel_h[:], near[:, PAGE:PAGE + 1].to_broadcast([H, NB]),
                                 start=False, stop=False)
                for n in range(NB * KV):
                    last = nc.tensor.matmul(m.ps[0:R, 6, 0:NB], qz[:, n, :], m.kT[:, n % KV, L:T], start=False,
                                            stop=(n == NB * KV - 1))
                last.then_inc(s["last_mm"], 1)
                for h in range(H):
                    last = nc.tensor.transpose(m.ps[:, 7, 64 + h * NB:64 + h * NB + NB], gate[:, h * P:(h + 1) * P],
                                               m.ident[0:NB, 0:NB])
                last.then_inc(s["gate_mm"], 1)
                pe.wait_ge(s["scaled"], 1)
                pe.wait_ge(s["k_act"], 4 * NB + 1)
                pe.wait_ge(s["k_dve"], 4 * NB + 1)
                for j in range(N_PT):
                    if j >= 2:
                        pe.wait_ge(s["pt_out"], j - 1)
                    for b in range(QP):
                        last = nc.tensor.transpose(m.ps[:, 4 + j % 2, b * R:(b + 1) * R],
                                                   prob[:, (QP * j + b) * P:(QP * j + b + 1) * P], m.ident[0:R, 0:R])
                    last.then_inc(s["pt_mm"], 1)
                nc.tensor.transpose(m.ps[0:NB, 6, 0:R], prob[:, PAST:PAST + NB], m.ident[0:R, 0:R]).then_inc(s["pt_mm"], 1)
                pe.wait_ge(s["pt_out"], N_PT + 1)
                with pe.Fori(0, NB // 2) as i:
                    for b in range(2):
                        pe.wait_ge(v_in[b], i * (16 * N_PAGES) + 16 * N_PAGES)
                        alone(pe, m)
                        for g in range(KV):
                            cols = bass.ds(i * (2 * H) + (b * H + g * G), G)
                            for j in range(N_PAGES):
                                nc.tensor.matmul(m.ps[:, 0, cols], vpages[:, b, j, g * P:(g + 1) * P],
                                                 probT[:, j, cols], start=(j == 0), stop=False)
                            last = nc.tensor.matmul(m.ps[:, 0, cols], vnew[:, g * P:(g + 1) * P], newT[:, cols],
                                                    start=False, stop=True)
                        last.then_inc(s["pv_b"], 1)
                if diff:
                    pe.wait_ge(s["osq_out"], 1)
                    nc.tensor.matmul(m.ps[:, 1, 0:NO], m.ones[:], osq[:], start=True, stop=True).then_inc(s["sum_mm"], 1)

            @block.scalar
            def _(act):
                act.sem_inc(s["k_act"], 1)
                with act.Fori(0, N_PAGES // QP) as kq:
                    for b in range(NB):
                        act.wait_ge(s["turned_a"], kq * NB + b + 1)
                        act.wait_ge(s["scores_mm"], kq * (2 * NB) + (2 * b + 1))
                        nc.scalar.copy(kTs[:, 0, :], m.ps[:, 4, :]).then_inc(s["k_act"], 1)
                act.wait_ge(s["maxed"], 1)
                keys = m.ps[0:R, 0:4, :].rearrange("p a b -> p (a b)")
                nc.scalar.activation(prob[:, 0:PAST], keys, ACT.Exp, bias=mx[:, 0:1], accum_out=den[:, 0:1])
                nc.scalar.activation(prob[:, PAST:], m.ps[0:R, 6, 0:NB], ACT.Exp, bias=mx[:, 0:1],
                                     accum_out=den[:, 1:2]).then_inc(s["exped"], 1)
                act.wait_ge(s["pv_b"], NB + 2)
                nc.scalar.copy(o[:], m.ps[:, 0, 0:NO])
                nc.scalar.activation(osq[:], m.ps[:, 0, 0:NO], ACT.Square).then_inc(s["osq_out"], 1)
                if diff:
                    act.wait_ge(s["sum_mm"], 1)
                    nc.scalar.activation(rs[:], m.ps[:, 1, 0:NO], ACT.Sqrt, scale=1.0 / P, bias=m.eps[:, 0:1])\
                        .then_inc(s["rs_out"], 1)

            @block.vector
            def _(dve):
                dve.sem_inc(s["k_dve"], 1)
                dve.sem_inc(s["scores_mm"], 2)
                dve.memset(qz[:], 0.0).then_inc(s["zeroed"], 1)
                dve.wait_ge(s["zeroed"], 1)
                for b in range(NB):
                    for g in range(KV):
                        n = KV * b + g
                        for c in range(NC):
                            out = qz[:, n, RG * n:RG * n + RG].rearrange("p (h c) -> p h c", c=NC)[:, :, c]
                            src = m.qT[:, G * g:G * g + G, L + b]
                            last = nc.vector.tensor_scalar(out, src, m.halves[:, c:c + 1] if diff else float(P) ** -0.5,
                                                           None, ALU.mult)
                last.then_inc(s["q_out"], 1)
                with dve.Fori(0, N_PAGES // QP) as kq:
                    for b in range(NB):
                        dve.wait_ge(s["turned_d"], kq * NB + b + ring + 1)
                        dve.wait_ge(s["scores_mm"], kq * (2 * NB) + (2 * b + 2))
                        nc.vector.tensor_copy(kTs[:, 1, :], m.ps[:, 5, :]).then_inc(s["k_dve"], 1)
                steps = Steps(dve, s["step"])
                dve.wait_ge(s["last_mm"], 1)
                keys = m.ps[0:R, 0:4, :].rearrange("p a b -> p (a b)")
                nc.vector.tensor_reduce(mx[:, 0:1], keys, AX, ALU.max)
                steps.after(nc.vector.tensor_reduce(mx[:, 1:2], m.ps[0:R, 6, 0:NB], AX, ALU.max))
                nc.vector.tensor_scalar(mx[:, 0:1], mx[:, 0:1], mx[:, 1:2], -1.0, ALU.max, ALU.mult).then_inc(s["maxed"], 1)
                dve.wait_ge(s["exped"], 1)
                steps.after(nc.vector.tensor_tensor(den[:, 0:1], den[:, 0:1], den[:, 1:2], ALU.add))
                steps.after(nc.vector.reciprocal(den[:, 0:1], den[:, 0:1]))
                if diff:
                    steps.after(nc.vector.scalar_tensor_tensor(out=parity[:, 0:1], in0=parity[:, 1:2],
                                                               scalar=m.lam[:, 0:1], in1=parity[:, 0:1],
                                                               op0=ALU.mult, op1=ALU.add))
                    steps.after(nc.vector.tensor_tensor(den[:, 0:1], den[:, 0:1], parity[:, 0:1], ALU.mult))
                nc.vector.tensor_scalar(prob[:], prob[:], den[:, 0:1], None, ALU.mult).then_inc(s["scaled"], 1)

                def turned(dst, src):
                    if diff:
                        return nc.vector.tensor_reduce(dst, src.rearrange("p a (n c) -> p a n c", c=2), AX, ALU.add)
                    return nc.vector.tensor_copy(dst, src)

                for j in range(N_PT):
                    dve.wait_ge(s["pt_mm"], j + 1)
                    turned(probT[:, QP * j:QP * j + QP, :],
                           m.ps[:, 4 + j % 2, 0:QP * R].rearrange("p (a r) -> p a r", r=R)).then_inc(s["pt_out"], 1)
                dve.wait_ge(s["pt_mm"], N_PT + 1)
                turned(newT[:].rearrange("p (a n) -> p a n", a=1),
                       m.ps[0:NB, 6, 0:R].rearrange("p (a r) -> p a r", a=1)).then_inc(s["pt_out"], 1)
                dve.wait_ge(s["osq_out"], 1)
                dve.wait_ge(s["gate_mm"], 1)
                gates = m.ps[:, 7, 64:64 + NO].rearrange("p (h b) -> p b h", b=NB)
                o3 = o[:].rearrange("p (b h) -> p b h", h=H)
                out = m.actT[:, 0:H, L:T].rearrange("p h b -> p b h")
                if not diff:
                    nc.vector.tensor_tensor(out, o3, gates, ALU.mult)
                else:
                    steps.after(nc.vector.tensor_tensor(o3, o3, gates, ALU.mult))
                    steps.after(nc.vector.tensor_scalar(o[:], o[:], gain[:, 0:1], 1.0 - LAM_INIT, ALU.mult, ALU.mult))
                    dve.wait_ge(s["rs_out"], 1)
                    steps.after(nc.vector.reciprocal(rs[:], rs[:]))
                    nc.vector.tensor_tensor(out, o3, rs[:].rearrange("p (b h) -> p b h", h=H), ALU.mult)



def project_out(nc, m, w, chunks, tag):
    with ExitStack() as own:
        E = own.enter_context
        wt = E(nc.sbuf_tensor(f"{tag}_w", [P, chunks, D], F32))
        rows = E(nc.sbuf_tensor(f"{tag}_rows", [P, 2, chunks, P], F32))
        w_in, rows_ready, product, added = (m.sem(f"{tag}_{x}") for x in ("w_in", "rows", "product", "added"))
        with nc.Block() as block:
            @block.sync
            def _(sp):
                sp.dma_start(wt[:], w.rearrange("(c p) n -> p c n", p=P)).then_inc(w_in, 16)

            @block.scalar
            def _(act):
                act.sem_inc(product, 4)

                def tile(t, turn, slot, r):
                    act.wait_ge(product, 2 * t + 2)
                    nc.scalar.copy(rows[:, slot, :, 0:r], m.actT[:, 0:chunks, bass.ds(t * P, r)])\
                        .then_inc(rows_ready, 1)

                over_tiles(act, tile)

            @block.tensor
            def _(pe):
                pe.wait_ge(w_in, 16)

                def tile(t, turn, slot, r):
                    pe.wait_ge(rows_ready, t + 1)
                    pe.wait_ge(added, t + 1)
                    for j in range(2):
                        for c in range(chunks):
                            last = nc.tensor.matmul(m.ps[0:r, 2 * slot + j, :], rows[:, slot, c, 0:r],
                                                    wt[:, c, j * 512:(j + 1) * 512], start=(c == 0),
                                                    stop=(c == chunks - 1))
                        last.then_inc(product, 1)

                over_tiles(pe, tile)

            @block.vector
            def _(dve):
                dve.sem_inc(added, 2)

                def tile(t, turn, slot, r):
                    dve.wait_ge(product, 2 * t + 6)
                    h = m.h[0:r, bass.ds(t, 1), :].rearrange("p o (a b) -> p (o a) b", b=512)
                    nc.vector.tensor_tensor(h, h, m.ps[0:r, 2 * slot:2 * slot + 2, :], ALU.add).then_inc(added, 1)

                over_tiles(dve, tile)


def move_rows(nc, m, tag, save):
    moved = m.sem(tag)
    with nc.Block() as block:
        @block.sync
        def _(sp):
            full = m.h_dram[0:FULL * P, :].rearrange("(t p) d -> p t d", p=P)
            pairs = [(full, m.h[:, 0:FULL, :]), (m.h_dram[FULL * P:T, :], m.h[0:LAST, FULL, :])]
            for dram, sbuf in pairs:
                sp.dma_start(*((dram, sbuf) if save else (sbuf, dram))).then_inc(moved, 16)
            sp.wait_ge(moved, 32)


def store_kv(nc, m, tok, outs):
    with nc.Block() as block:
        @block.sync
        def _(sp):
            for out, r0, r1, c0, c1 in outs:
                sp.dma_start(out, tok[r0:r1, c0:c1]).then_inc(m.s_out, 16)
                m.n_out += 1



def index_prompt(nc, m):
    with ExitStack() as own:
        E = own.enter_context
        k2 = E(nc.sbuf_tensor("ix_k2", [P, NT, P], F32))
        q = E(nc.sbuf_tensor("ix_q", [P, 2, P], F32))
        w = E(nc.sbuf_tensor("ix_w", [P, NT, 8], F32))
        r = E(nc.sbuf_tensor("ix_relu", [P, 2, L], F32))
        causal = E(nc.sbuf_tensor("ix_causal", [P, P], F32))
        names = "k_in w_in turned copied q_ready dots relued w_scaled summed step cleared"
        s = {x: m.sem("ix_" + x) for x in names.split()}
        tiles = [t for t in range(NT) if t * P >= TOPK]
        HI = 8

        def shape(t):
            R = P if t < FULL else TAIL
            return R, t * P + R

        def over_heads(eng, k, part):
            with eng.Fori(0, HI // 2) as a:
                for parity in range(2):
                    part(a, parity, k * HI + 2 * a + parity)

        with nc.Block() as block:
            @block.sync
            def _(sp):
                for half in range(2):
                    dst = slice(64 * half, 64 * half + 64)
                    src = m.tok1[:, TOK_R:TOK_R + 64]
                    sp.dma_start(k2[:, 0:FULL, dst], src[0:FULL * P].rearrange("(t p) c -> p t c", p=P))\
                        .then_inc(s["k_in"], 16)
                    sp.dma_start(k2[0:LAST, FULL, dst], src[FULL * P:T]).then_inc(s["k_in"], 16)
                src = m.tok1[:, TOK_R + 64:TOK_R + 72]
                sp.dma_start(w[:, 0:FULL, :], src[0:FULL * P].rearrange("(t p) c -> p t c", p=P)).then_inc(s["w_in"], 16)
                sp.dma_start(w[0:TAIL, FULL, :], src[FULL * P:L]).then_inc(s["w_in"], 16)
                sp.dma_start(causal[:], m.causal).then_inc(s["w_in"], 16)

            @block.gpsimd
            def _(pool):
                for k, t in enumerate(tiles):
                    R, W = shape(t)

                    def head(a, parity, n):
                        pool.wait_ge(s["dots"], n + 1)
                        alone(pool, m)
                        nc.gpsimd.tensor_tensor(q[:, parity, 0:R], m.qiT[:, bass.ds(a, 1), t * P:t * P + R],
                                                m.halves_wide[:, parity, 0:R], ALU.mult).then_inc(s["q_ready"], 1)

                    over_heads(pool, k, head)

            @block.tensor
            def _(pe):
                pe.sem_inc(s["dots"], 2)
                pe.wait_ge(s["k_in"], 64)
                for t in range(NT):
                    n = P if t < FULL else LAST
                    last = nc.tensor.transpose(m.ps[:, t // 4, t % 4 * P:t % 4 * P + n], k2[0:n, t, :],
                                               m.ident[0:n, 0:n])
                last.then_inc(s["turned"], 1)
                pe.wait_ge(s["copied"], 1)
                for k, t in enumerate(tiles):
                    R, W = shape(t)

                    def head(a, parity, n):
                        pe.wait_ge(s["q_ready"], n + 1)
                        pe.wait_ge(s["relued"], n + 1)
                        alone(pe, m)
                        for c in range(0, W, 512):
                            c1 = min(c + 512, W)
                            last = nc.tensor.matmul(m.ps[0:R, 3 * parity + c // 512, 0:c1 - c], q[:, parity, 0:R],
                                                    m.kiT[:, c:c1], start=True, stop=True)
                        last.then_inc(s["dots"], 1)

                    over_heads(pe, k, head)

            @block.scalar
            def _(act):
                act.wait_ge(s["turned"], 1)
                nc.scalar.copy(m.kiT[:], m.ps[:, 0:3, :].rearrange("p a b -> p (a b)")[:, 0:T]).then_inc(s["copied"], 1)
                act.sem_inc(s["relued"], 2)
                for k, t in enumerate(tiles):
                    R, W = shape(t)

                    def head(a, parity, n):
                        act.wait_ge(s["dots"], n + 3)
                        act.wait_ge(s["summed"], n + 1)
                        src = m.ps[0:R, 3 * parity:3 * parity + 3, :].rearrange("p a b -> p (a b)")[:, 0:W]
                        nc.scalar.activation(r[0:R, parity, 0:W], src, ACT.Relu).then_inc(s["relued"], 1)

                    over_heads(act, k, head)

            @block.vector
            def _(dve):
                for t in tiles:
                    R, W = shape(t)
                    last = dve.memset(m.chosen[t][0:R, :], 0.0)
                last.then_inc(s["cleared"], 1)
                dve.wait_ge(s["cleared"], 1)
                for k, t in enumerate(tiles):
                    R, W = shape(t)
                    d = m.chosen[t][0:R, W - R:W]
                    if k == 0:
                        dve.wait_ge(s["w_in"], 48)
                        nc.vector.tensor_scalar(w[:, 0:FULL], w[:, 0:FULL], float(HI) ** -0.5, None, ALU.mult)
                        nc.vector.tensor_scalar(w[0:TAIL, FULL], w[0:TAIL, FULL], float(HI) ** -0.5, None, ALU.mult)\
                            .then_inc(s["w_scaled"], 1)
                        dve.wait_ge(s["w_scaled"], 1)
                    nc.vector.tensor_tensor(d, d, causal[0:R, 0:R], ALU.add).then_inc(s["step"], 1)
                dve.wait_ge(s["step"], len(tiles))
                dve.sem_inc(s["summed"], 2)
                for k, t in enumerate(tiles):
                    R, W = shape(t)

                    def head(a, parity, n):
                        dve.wait_ge(s["relued"], n + 3)
                        nc.vector.scalar_tensor_tensor(out=m.chosen[t][0:R, :], in0=r[0:R, parity, 0:W],
                                                       scalar=w[0:R, t, bass.ds(2 * a + parity, 1)],
                                                       in1=m.chosen[t][0:R, :], op0=ALU.mult, op1=ALU.add)\
                            .then_inc(s["summed"], 1)
                        dve.wait_ge(s["summed"], n + 3)

                    over_heads(dve, k, head)


def index_samples(nc, m, io):
    HP = N_PAGES // 2
    with ExitStack() as own:
        E = own.enter_context
        sb = lambda name, shape: E(nc.sbuf_tensor("is_" + name, shape, F32))
        qz = sb("qz", [P, NB, 2, 8])
        kp = sb("pages", [P, 2, HP, 2, 64])
        kT = sb("kT", [P, 2, HP * P])
        relu = sb("relu", [8, 2, PAST + NB])
        wi, wT, wz, eye = sb("wi", [NB, 8]), sb("wT", [8, NB]), sb("wz", [8, NB, NB]), sb("eye", [8, NB, NB])
        own_mask = sb("own", [NB, NB])
        names = "zeroed q_in w_in w_mm w_out wz_out turned kT_out dots relued summed"
        s = {x: m.sem("is_" + x) for x in names.split()}
        k_in = [m.sem(f"is_k_in{j}") for j in range(2)]
        ci = io["cache_c_idx"][0]
        with nc.Block() as block:
            @block.sync
            def _(sp):
                sp.wait_ge(s["zeroed"], 1)
                with nc.allow_non_contiguous_dma(reason="query columns to other partitions"):
                    for half in range(2):
                        for parity in range(2):
                            for b in range(NB):
                                sp.dma_start(qz[half * 64:half * 64 + 64, b, half, parity:8:2],
                                             m.qiT[parity * 64:parity * 64 + 64, :, L + b]).then_inc(s["q_in"], 16)
                sp.dma_start(wi[:], m.tok1[L:T, TOK_R + 64:TOK_R + 72]).then_inc(s["w_in"], 16)
                sp.dma_start(eye[:], io["c_eye8"]).then_inc(s["w_in"], 16)
                sp.dma_start(own_mask[:], io["c_own_mask"]).then_inc(s["w_in"], 16)
                with sp.Fori(0, NB // 2) as i:
                    for b in range(2):
                        sp.wait_ge(s["turned"], (2 * i + b) * 2 + 2)
                        alone(sp, m)
                        for j in range(N_PAGES):
                            at = sp.value_load(m.pages[0:1, bass.ds(i * (2 * N_PAGES) + (b * N_PAGES + j), 1)],
                                               min_val=0, max_val=ci.shape[0] - 1)
                            sp.dma_start(kp[:, b, j % HP, j // HP, :],
                                         ci[bass.ds(at, 1), :, :].rearrange("o t c -> t (o c)")).then_inc(k_in[b], 16)

            @block.tensor
            def _(pe):
                pe.sem_inc(s["turned"], 4)
                pe.wait_ge(s["w_in"], 48)
                nc.tensor.transpose(m.ps[0:8, 6, 0:NB], wi[:], m.ident[0:NB, 0:NB]).then_inc(s["w_mm"], 1)
                pe.wait_ge(s["q_in"], 16 * 4 * NB)
                pe.wait_ge(s["wz_out"], 1)
                for b in range(NB):
                    slot = b % 2
                    pe.wait_ge(k_in[slot], 16 * N_PAGES * (b // 2 + 1))
                    for j in range(2):
                        pe.wait_ge(s["kT_out"], 2 * b + j + 1)
                        for x in range(4):
                            last = nc.tensor.transpose(m.ps[:, 4, x * P:(x + 1) * P],
                                                       kp[:, slot, 4 * j + x].rearrange("p a b -> p (a b)"),
                                                       m.ident[:])
                        last.then_inc(s["turned"], 1)
                    pe.wait_ge(s["kT_out"], 2 * b + 3)
                    for j in range(5):
                        n = 5 * b + j
                        pe.wait_ge(s["relued"], n + 1)
                        if j < 4:
                            out, half = m.ps[0:8, 5 + n % 2, :], j // 2
                            rhs = kT[:, slot, j % 2 * 512:j % 2 * 512 + 512]
                        else:
                            out, half, rhs = m.ps[0:8, 5 + n % 2, 0:NB], 0, m.kiT[:, L:T]
                        nc.tensor.matmul(out, qz[:, b, half, :], rhs, start=True, stop=True).then_inc(s["dots"], 1)
                    for j in range(5):
                        pe.wait_ge(s["relued"], 5 * b + j + 3)
                        out = m.ps[0:NB, j, :] if j < 4 else m.ps[0:NB, 7, 0:NB]
                        rhs = relu[:, slot, 512 * j:512 * j + (512 if j < 4 else NB)]
                        last = nc.tensor.matmul(out, wz[:, b, :], rhs, start=(b == 0), stop=(b == NB - 1))
                    last.then_inc(s["summed"], 1)

            @block.scalar
            def _(act):
                act.sem_inc(s["relued"], 2)
                act.sem_inc(s["summed"], 2)
                for b in range(NB):
                    act.wait_ge(s["summed"], b + 1)
                    for j in range(5):
                        n = 5 * b + j
                        act.wait_ge(s["dots"], n + 1)
                        w = 512 if j < 4 else NB
                        nc.scalar.activation(relu[:, b % 2, 512 * j:512 * j + w], m.ps[0:8, 5 + n % 2, 0:w], ACT.Relu,
                                             scale=64 ** -0.5).then_inc(s["relued"], 1)

            @block.vector
            def _(dve):
                dve.sem_inc(s["kT_out"], 1)
                dve.memset(qz[:], 0.0).then_inc(s["zeroed"], 1)
                dve.wait_ge(s["w_mm"], 1)
                nc.vector.tensor_copy(wT[:], m.ps[0:8, 6, 0:NB]).then_inc(s["w_out"], 1)
                dve.wait_ge(s["w_out"], 1)
                nc.vector.tensor_tensor(wz[:], wT[:].rearrange("p (b o) -> p b o", o=1).to_broadcast([8, NB, NB]),
                                        eye[:], ALU.mult).then_inc(s["wz_out"], 1)
                for b in range(NB):
                    for j in range(2):
                        dve.wait_ge(s["turned"], 2 * b + j + 5)
                        if b >= 2:
                            dve.wait_ge(s["dots"], 5 * (b - 1))
                        nc.vector.tensor_copy(kT[:, b % 2, 512 * j:512 * j + 512], m.ps[:, 4, :]).then_inc(s["kT_out"], 1)
                dve.wait_ge(s["summed"], NB + 2)
                nc.vector.tensor_copy(m.chosen_s[:, 0:PAST], m.ps[0:NB, 0:4, :].rearrange("p a b -> p (a b)"))
                nc.vector.tensor_tensor(m.chosen_s[:, PAST:], m.ps[0:NB, 7, 0:NB], own_mask[:], ALU.add)



def choose(nc, m):
    tiles = [(m.chosen[t], P if t < FULL else TAIL) for t in range(NT) if t * P >= TOPK] + [(m.chosen_s, NB)]
    NTL = len(tiles)
    BITS = 31
    with ExitStack() as own:
        E = own.enter_context
        sb = lambda name, shape, dt=F32: E(nc.sbuf_tensor("ch_" + name, shape, dt))
        wmax = max(x.shape[-1] for x, _ in tiles)
        hits, equal, rank = sb("hits", [P, wmax]), sb("equal", [P, wmax]), sb("rank", [P, wmax])
        count, need, sign, below = (sb(x, [P, NTL]) for x in ("count", "need", "sign", "below"))
        extra, thresh, left = (sb(x, [P, NTL]) for x in ("extra", "thresh", "left"))
        cand, flip = sb("cand", [P, NTL], I32), sb("flip", [P, NTL], I32)
        bits = sb("bits", [P, BITS])
        next_bits = sb("next", [P, BITS], I32)
        bits_in, step, loop_step = m.sem("ch_bits_in"), m.sem("ch_step"), m.sem("ch_loop")
        with nc.Block() as block:
            @block.sync
            def _(sp):
                sp.dma_start(bits[:], m.bits).then_inc(bits_in, 16)
                sp.dma_start(next_bits[:], m.next_bits).then_inc(bits_in, 16)

            @block.vector
            def _(dve):
                steps = Steps(dve, step)
                V = nc.vector
                dve.memset(count[:], 0.0)
                for j, (x, r) in enumerate(tiles):
                    dve.memset(extra[:, j:j + 1], float(x.shape[-1] + 1 - 2 * TOPK))
                steps.after(dve.memset(cand[:], 1 << (BITS - 1)))
                for j, (x, r) in enumerate(tiles):
                    steps.after(V.tensor_scalar(hits[0:r, 0:x.shape[-1]], x[0:r], 0.0, None, ALU.is_ge, ALU.add,
                                                accum_out=count[0:r, j:j + 1]))
                steps.after(V.tensor_scalar(below[:], count[:], float(TOPK), None, ALU.is_lt))
                steps.after(V.tensor_scalar(sign[:], below[:], -2.0, 1.0, ALU.mult, ALU.add))
                steps.after(V.tensor_tensor(need[:], below[:], extra[:], ALU.mult))
                steps.after(V.tensor_scalar(need[:], need[:], float(TOPK), None, ALU.add))
                for j, (x, r) in enumerate(tiles):
                    last = V.tensor_scalar(x[0:r], x[0:r], sign[0:r, j:j + 1], None, ALU.mult)
                    steps.after(last)
                dve.wait_ge(bits_in, 32)
                LOOP = NTL + 3
                with dve.Fori(0, BITS) as i:
                    steps_i = Steps(dve, loop_step, LOOP * i)
                    for j, (x, r) in enumerate(tiles):
                        ins = V.tensor_scalar(hits[0:r, 0:x.shape[-1]], x[0:r], cand[0:r, j:j + 1].bitcast(F32), None,
                                              ALU.is_ge, ALU.add, accum_out=count[0:r, j:j + 1])
                        steps_i.after(ins)
                    steps_i.after(V.tensor_tensor(below[:], count[:], need[:], ALU.is_lt))
                    steps_i.after(V.tensor_scalar(flip[:], below[:], bits[:, bass.ds(i, 1)], None, ALU.mult))
                    steps_i.after(V.scalar_tensor_tensor(out=cand[:], in0=cand[:], scalar=next_bits[:, bass.ds(i, 1)],
                                                         in1=flip[:], op0=ALU.bitwise_xor, op1=ALU.bitwise_xor))
                    assert steps_i.n == LOOP
                steps.after(V.tensor_tensor(thresh[:], cand[:].bitcast(F32), sign[:], ALU.mult))
                for j, (x, r) in enumerate(tiles):
                    w = x.shape[-1]
                    G_, Q, K = hits[0:r, 0:w], equal[0:r, 0:w], rank[0:r, 0:w]
                    t = thresh[0:r, j:j + 1]
                    steps.after(V.tensor_scalar(x[0:r], x[0:r], sign[0:r, j:j + 1], None, ALU.mult))
                    steps.after(V.tensor_scalar(G_, x[0:r], t, None, ALU.is_gt, ALU.add,
                                                accum_out=count[0:r, j:j + 1]))
                    steps.after(V.tensor_scalar(left[0:r, j:j + 1], count[0:r, j:j + 1], -1.0, float(TOPK), ALU.mult,
                                                ALU.add))
                    steps.after(V.tensor_scalar(Q, x[0:r], t, None, ALU.is_equal))
                    steps.after(V.tensor_tensor_scan(K, Q, Q, 0.0, ALU.add, ALU.max))
                    steps.after(V.scalar_tensor_tensor(out=K, in0=K, scalar=left[0:r, j:j + 1], in1=Q, op0=ALU.is_le,
                                                       op1=ALU.mult))
                    steps.after(V.tensor_tensor(G_, G_, K, ALU.add))
                    steps.after(V.tensor_scalar(x[0:r], G_, -NEG, NEG, ALU.mult, ALU.add))



def finish(nc, m, io):
    with ExitStack() as own:
        E = own.enter_context
        gain = E(nc.sbuf_tensor("fn_gain", [P, D], F32))
        squares = E(nc.sbuf_tensor("fn_sq", [P, D], F32))
        y = E(nc.sbuf_tensor("fn_y", [P, NT, D], F32))
        ss, rstd = E(nc.sbuf_tensor("fn_ss", [P, NT], F32)), E(nc.sbuf_tensor("fn_rstd", [P, NT], F32))
        gain_in, sq_step, root, step, y_out = (m.sem("fn_" + x) for x in ("gain_in", "sq", "root", "step", "y_out"))
        rows = lambda t: P if t < FULL else LAST
        with nc.Block() as block:
            @block.scalar
            def _(act):
                steps = Steps(act, sq_step)
                for t in range(NT):
                    r = rows(t)
                    steps.after(nc.scalar.activation(squares[0:r], m.h[0:r, t, :], ACT.Square,
                                                     accum_out=ss[0:r, t:t + 1]))
                for t in range(NT):
                    r = rows(t)
                    last = nc.scalar.activation(rstd[0:r, t:t + 1], ss[0:r, t:t + 1], ACT.Sqrt, scale=1.0 / D,
                                                bias=m.eps[0:r, 0:1])
                last.then_inc(root, 1)

            @block.vector
            def _(dve):
                dve.wait_ge(gain_in, 16)
                dve.wait_ge(root, 1)
                steps = Steps(dve, step)
                for t in range(NT):
                    r = rows(t)
                    steps.after(nc.vector.reciprocal(rstd[0:r, t:t + 1], rstd[0:r, t:t + 1]))
                    nc.vector.scalar_tensor_tensor(out=y[0:r, t], in0=m.h[0:r, t], scalar=rstd[0:r, t:t + 1],
                                                   in1=gain[0:r], op0=ALU.mult, op1=ALU.mult).then_inc(y_out, 1)

            @block.sync
            def _(sp):
                sp.dma_start(gain[:], row_view(io["final_norm"]).to_broadcast([P, D])).then_inc(gain_in, 16)
                yp = io["y_prompt"][0]
                first = P - N_META
                sp.wait_ge(y_out, 1)
                sp.dma_start(yp[0:first, :], y[N_META:P, 0, :]).then_inc(m.s_out, 16)
                with sp.Fori(1, FULL) as t:
                    sp.wait_ge(y_out, t + 1)
                    sp.dma_start(yp[bass.ds(t * P - N_META, P), :], y[:, bass.ds(t, 1), :]).then_inc(m.s_out, 16)
                sp.wait_ge(y_out, NT)
                sp.dma_start(yp[SEQ - TAIL:SEQ, :], y[0:TAIL, FULL, :]).then_inc(m.s_out, 16)
                sp.dma_start(io["y_sample"].rearrange("b o d -> (b o) d"), y[TAIL:LAST, FULL, :]).then_inc(m.s_out, 16)
                m.n_out += FULL + 2
                sp.wait_ge(m.s_out, 16 * m.n_out)



INPUTS = ['x_prompt', 'x_sample', 'cache_a_k', 'cache_a_v', 'state_b_s', 'state_b_conv', 'cache_c_k', 'cache_c_v',
          'cache_c_idx', 'page_table', 'meta', 'bias_table', 'final_norm', 'norm_e', 'w_in_e', 'w_out_e', 'lam_q1',
          'lam_k1', 'lam_q2', 'lam_k2', 'subln_a', 'conv_b', 'a_log_b', 'dt_bias_b', 'norm_b', 'norm_o', 'w_in_o',
          'w_out_o']


def buckets():
    d = FAR - np.arange(BIAS_W)
    n = np.maximum(d, 0)
    nf = np.maximum(n, 1).astype(np.float32)
    large = 16 + (np.log(nf / 16) / np.log(128 / 16) * 16).astype(np.int32)
    bucket = np.where(n < 16, n, np.minimum(large, 31))
    out = np.zeros((33, BIAS_W), np.float32)
    out[bucket, np.arange(BIAS_W)] = d >= 0
    out[32] = d < 0
    return out


def constants():
    i = np.arange(P)
    row, col = i[:, None], i[None, :]
    masks = [row <= col, row > col, row // 8 == col // 8]
    masks += [(row // (2 * b) == col // (2 * b)) & (row // b % 2 == 0) & (col // b % 2 == 1) for b in (8, 16, 32, 64)]
    return {"c_ident": np.eye(P, dtype=np.float32),
            "c_buckets": buckets(),
            "c_sel_b1": np.repeat(np.eye(NB), H, 1).astype(np.float32),
            "c_sel_b2": np.repeat(np.eye(NB), 2 * H, 1).astype(np.float32),
            "c_sel_h1": np.tile(np.eye(H), (1, NB)).astype(np.float32),
            "c_sel_h2": np.tile(np.repeat(np.eye(H), 2, 1), (1, NB)).astype(np.float32),
            "c_own_mask": (NEG * (1 - np.eye(NB))).astype(np.float32),
            "c_causal": (NEG * (i[None, :] > i[:, None])).astype(np.float32),
            "c_bits": np.tile(2.0 ** (30 - np.arange(31)), (P, 1)).astype(np.float32),
            "c_next_bits": np.tile(np.array([1 << (29 - k) if k < 30 else 0 for k in range(31)]), (P, 1))
            .astype(np.int32),
            "c_eye8": np.tile(8 ** -0.5 * np.eye(NB), (8, 1, 1)).astype(np.float32),
            "c_flip": np.eye(P, dtype=np.float32)[::-1].copy(),
            "c_parity": (i[:, None] % 2 == np.arange(2)).astype(np.float32),
            "c_halves": np.concatenate([64 ** -0.5 * (i[:, None] // 64 == np.arange(2)), np.full((P, 1), P ** -0.5)],
                                       1).astype(np.float32),
            "c_delta_masks": np.stack(masks, 1).astype(np.float32)}


OUTPUTS = {
    "y_prompt": (1, SEQ, D), "y_sample": (NB, 1, D),
    "pa_k": (1, 1, L, KV, 2, 64), "pa_v": (1, 1, L, KV, P), "pb_s": (1, 1, B_H, P, P), "pb_conv": (1, 1, 3, 1536),
    "pc_k": (1, 1, L, KV, P), "pc_v": (1, 1, L, KV, P), "pc_idx": (1, 1, L, 64),
    "sa_k": (1, NB, 1, KV, 2, 64), "sa_v": (1, NB, 1, KV, P), "sb_s": (1, NB, B_H, P, P), "sb_conv": (1, NB, 3, 1536),
    "sc_k": (1, NB, 1, KV, P), "sc_v": (1, NB, 1, KV, P), "sc_idx": (1, NB, 1, 64),
}


def kv_outputs(k_p, v_p, k_s, v_s):
    return [(k_p, 0, L, TOK_K, TOK_K + 256), (v_p, 0, L, TOK_V, TOK_V + 256),
            (k_s, L, T, TOK_K, TOK_K + 256), (v_s, L, T, TOK_V, TOK_V + 256)]


class Shared:
    pass


def build(nc, io):
    with ExitStack() as ctx:
        E = ctx.enter_context
        m = Shared()
        m.s_out, m.n_out = E(nc.semaphore("outputs_stored")), 0
        m.s_idle = E(nc.semaphore("waits_alone"))
        in_use = []

        def sem(name):
            in_use.append(nc.alloc_semaphore(name=name))
            return in_use[-1]

        def recycle():
            nc.clear_and_free_semaphores(in_use)
            in_use.clear()
            nc.all_engine_barrier()

        m.sem = sem
        dram = lambda name, shape: nc.dram_tensor(name, shape, F32, kind="Internal").ap()
        m.tok, m.tok1 = dram("tok_rows", (T, TOK_W)), dram("tok_rows_1", (T, TOK_W))
        m.h_dram = dram("h_rows", (T, D))
        m.bias = dram("bias_rows", (H, BIAS_W))
        m.causal, m.bits, m.next_bits, m.flip = io["c_causal"], io["c_bits"], io["c_next_bits"], io["c_flip"]
        m.ps = E(nc.psum_tensor("banks", [P, 8, 512], F32))
        m.ident = E(nc.sbuf_tensor("ident", [P, P], F32))
        m.ones = E(nc.sbuf_tensor("ones", [P, P], F32))
        m.eps = E(nc.sbuf_tensor("eps", [P, 1], F32))
        m.halves = E(nc.sbuf_tensor("halves", [P, 3], F32))
        m.halves_wide = E(nc.sbuf_tensor("halves_wide", [P, 3, P], F32))
        m.pages = E(nc.sbuf_tensor("pages", [1, NB * N_PAGES], I32))
        m.lam = E(nc.sbuf_tensor("lam", [P, 1], F32))
        m.actT = E(nc.sbuf_tensor("actT", [P, 12, T], F32))
        load_constants(nc, m, io)
        bias_rows(nc, m, io)
        with ExitStack() as scope:
            m.h = scope.enter_context(nc.sbuf_tensor("h_in", [P, NT, D], F32))
            load_rows(nc, m, io, "ld0")
            norm_and_turn(nc, m, io["norm_e"][0], "n0")
        project_tokens(nc, m, io["w_in_e"][0], EVEN, m.tok, "pt0")
        store_kv(nc, m, m.tok, kv_outputs(io["pa_k"].rearrange("a b l k c d -> (a b l) (k c d)"),
                                          io["pa_v"].rearrange("a b l k d -> (a b l) (k d)"),
                                          io["sa_k"].rearrange("a b l k c d -> (a b l) (k c d)"),
                                          io["sa_v"].rearrange("a b l k d -> (a b l) (k d)")))
        with ExitStack() as layer:
            m.qT = layer.enter_context(nc.sbuf_tensor("a_qT", [P, H, T], F32))
            with ExitStack() as delta:
                m.mixT = delta.enter_context(nc.sbuf_tensor("b_qkvT", [P, 12, T], F32))
                m.gates = delta.enter_context(nc.sbuf_tensor("b_gates", [P, NT + NB, 8], F32))
                project_features(nc, m, io["w_in_e"][0], [(0, H, m.qT), (EVEN["mid"], 12, m.mixT)], "pf0")
                convolve(nc, m, io)
                normalise_qk(nc, m, io)
                delta_gates(nc, m, io)
                delta_prompt(nc, m, io)
                delta_samples(nc, m, io)
            recycle()
            m.kT = layer.enter_context(nc.sbuf_tensor("a_kT", [P, KV, T], F32))
            m.v = layer.enter_context(nc.sbuf_tensor("a_v", [P, NT, KV * P], F32))
            load_kv(nc, m, m.tok, "kv0")
            prompt_attention(nc, m, m.tok, True, io["subln_a"])
            sample_attention(nc, m, io, m.tok, True, io["cache_a_k"][0], io["cache_a_v"][0], io["subln_a"])
        recycle()
        with ExitStack() as scope:
            m.h = scope.enter_context(nc.sbuf_tensor("h_mid", [P, NT, D], F32))
            load_rows(nc, m, io, "ld1")
            project_out(nc, m, io["w_out_e"][0], 12, "po0")
            norm_and_turn(nc, m, io["norm_o"][0], "n1")
            move_rows(nc, m, "h_saved", True)
        project_tokens(nc, m, io["w_in_o"][0], ODD, m.tok1, "pt1")
        store_kv(nc, m, m.tok1, kv_outputs(io["pc_k"].rearrange("a b l k d -> (a b l) (k d)"),
                                           io["pc_v"].rearrange("a b l k d -> (a b l) (k d)"),
                                           io["sc_k"].rearrange("a b l k d -> (a b l) (k d)"),
                                           io["sc_v"].rearrange("a b l k d -> (a b l) (k d)"))
                 + [(io["pc_idx"].rearrange("a b l d -> (a b l) d"), 0, L, TOK_R, TOK_R + 64),
                    (io["sc_idx"].rearrange("a b l d -> (a b l) d"), L, T, TOK_R, TOK_R + 64)])
        with ExitStack() as layer:
            E1 = layer.enter_context
            m.qT = E1(nc.sbuf_tensor("c_qT", [P, H, T], F32))
            widths = {t: t * P + (P if t < FULL else TAIL) for t in range(NT) if t * P >= TOPK}
            m.chosen = {t: E1(nc.sbuf_tensor(f"c_chosen{t}", [P, w], F32)) for t, w in widths.items()}
            m.chosen_s = E1(nc.sbuf_tensor("c_chosen_s", [NB, PAST + NB], F32))
            with ExitStack() as index:
                m.qiT = index.enter_context(nc.sbuf_tensor("c_qiT", [P, 4, T], F32))
                m.kiT = index.enter_context(nc.sbuf_tensor("c_kiT", [P, T], F32))
                project_features(nc, m, io["w_in_o"][0], [(0, H, m.qT), (ODD["mid"], 4, m.qiT)], "pf1")
                index_prompt(nc, m)
                index_samples(nc, m, io)
                choose(nc, m)
            recycle()
            m.kT = E1(nc.sbuf_tensor("c_kT", [P, KV, T], F32))
            m.v = E1(nc.sbuf_tensor("c_v", [P, NT, KV * P], F32))
            load_kv(nc, m, m.tok1, "kv1")
            prompt_attention(nc, m, m.tok1, False, None)
            sample_attention(nc, m, io, m.tok1, False, io["cache_c_k"][0], io["cache_c_v"][0], None)
        m.h = E(nc.sbuf_tensor("h_out", [P, NT, D], F32))
        move_rows(nc, m, "h_loaded", False)
        project_out(nc, m, io["w_out_o"][0], 8, "po1")
        finish(nc, m, io)


def lay_out(nc, inputs):
    aps, arrays = {}, {}
    consts = constants()
    for name in INPUTS + list(consts):
        a = np.ascontiguousarray(consts[name] if name in consts else inputs[name])
        arrays[name + "_dram"] = a
        aps[name] = nc.dram_tensor(name + "_dram", a.shape, mybir.dt.from_np(a.dtype), kind="ExternalInput").ap()
    for name, shape in OUTPUTS.items():
        aps[name] = nc.dram_tensor(name + "_dram", shape, F32, kind="ExternalOutput").ap()
    build(nc, aps)
    return arrays


def kernel(**inputs):
    import concourse.bacc as bacc
    from concourse.bass_utils import run_bass_kernel_spmd

    nc = bacc.Bacc("TRN2", target_bir_lowering=False, num_devices=1)
    arrays = lay_out(nc, inputs)
    got = run_bass_kernel_spmd(nc, [arrays], core_ids=[0]).results[0]
    return tuple(got[name + "_dram"] for name in OUTPUTS)
```

```python
from contextlib import ExitStack

import numpy as np

import concourse.bass as bass
import concourse.mybir as mybir

F32 = mybir.dt.float32
I32 = mybir.dt.int32
BF16 = mybir.dt.bfloat16
ALU = mybir.AluOpType
ACT = mybir.ActivationFunctionType
AX = mybir.AxisListType.X

P = 128
D = 1024
KC = D // P
N_META, SEQ, NB = 16, 1024, 8
L = N_META + SEQ
T = L + NB
FULL = L // P
TAIL = L - FULL * P
LAST = T - FULL * P
NT = FULL + 1
EPS = 1e-6
PAGE, N_PAGES = 128, 16
PAST = PAGE * N_PAGES
H, KV, G = 8, 2, 4
LAM_INIT = 0.8 - 0.6
B_H = 4
CONV = 4
TOPK = 256
NEG = -1e30
SLICES = [(0, 350), (350, 350), (700, 348)]
FAR = FULL * P + P - 1
BIAS_W = FAR + P

TOK_K, TOK_V, TOK_G, TOK_R = 0, 256, 512, 1536
TOK_W = 1536 + 520

KV_COLS = [(1024, 512, TOK_K, False)]
GATE_COLS = [(1536, 512, TOK_G, True), (2048, 512, TOK_G + 512, True)]
REST_0 = [(4096, 512, TOK_R, True), (4608, 8, TOK_R + 512, False)]
REST_1 = [(3072, 72, TOK_R, False)]
MID = 2560


def row_view(ap):
    return ap.rearrange("(o n) -> o n", o=1)


def over_tiles(eng, body):
    with eng.Fori(0, FULL // 2) as i:
        body(2 * i, i, 0, P)
        body(2 * i + 1, i, 1, P)
    body(FULL, FULL // 2, 0, LAST)


class Steps:

    def __init__(self, eng, sem, base=0):
        self.eng, self.sem, self.base, self.n = eng, sem, base, 0

    def after(self, ins):
        self.n += 1
        ins.then_inc(self.sem, 1)
        self.eng.wait_ge(self.sem, self.base + self.n)


def alone(eng, m):
    eng.sem_inc(m.s_idle, 1)



def load_rows(nc, m, io, tag, next_load=None):
    rows_in = m.sem(f"{tag}_rows_in")
    with nc.Block() as block:
        @block.sync
        def _(sp):
            xp = io["x_prompt"].rearrange("b s d -> (b s) d")
            xs = io["x_sample"].rearrange("b s d -> (b s) d")
            first = P - N_META
            sp.dma_start(m.h[0:N_META, 0, :], io["meta"]).then_inc(rows_in, 16)
            sp.dma_start(m.h[N_META:P, 0, :], xp[0:first, :]).then_inc(rows_in, 16)
            body = xp[first:first + (FULL - 1) * P, :].rearrange("(t p) d -> p t d", p=P)
            sp.dma_start(m.h[:, 1:FULL, :], body).then_inc(rows_in, 16)
            sp.dma_start(m.h[0:TAIL, FULL, :], xp[SEQ - TAIL:SEQ, :]).then_inc(rows_in, 16)
            sp.dma_start(m.h[TAIL:LAST, FULL, :], xs).then_inc(rows_in, 16)
            if next_load:
                next_load(sp)
            sp.wait_ge(rows_in, 16 * 5)


def load_constants(nc, m, io):
    consts_in = m.sem("consts_in")
    with nc.Block() as block:
        @block.sync
        def _(sp):
            sp.dma_start(m.ident[:], io["c_ident"]).then_inc(consts_in, 16)
            sp.dma_start(m.pages[:], row_view(io["page_table"].rearrange("a b -> (a b)"))).then_inc(consts_in, 16)
            sp.dma_start(m.halves[:], io["c_halves"]).then_inc(consts_in, 16)
            sp.wait_ge(consts_in, 48)

        @block.vector
        def _(dve):
            dve.memset(m.ones[:], 1.0)
            dve.memset(m.eps[:], EPS)
            dve.wait_ge(consts_in, 48)
            nc.vector.tensor_copy(m.halves_wide[:], m.halves[:].rearrange("p (c o) -> p c o", o=1)
                                  .to_broadcast([P, 3, P]))



def norm_and_turn(nc, m, gain, tag):
    with ExitStack() as own:
        E = own.enter_context
        squares = E(nc.sbuf_tensor(f"{tag}_squares", [P, D], F32))
        ss = E(nc.sbuf_tensor(f"{tag}_ss", [P, NT], F32))
        rstd = E(nc.sbuf_tensor(f"{tag}_rstd", [P, NT], F32))
        scaled = E(nc.sbuf_tensor(f"{tag}_scaled", [P, 2, D], F32))
        gain_t = E(nc.sbuf_tensor(f"{tag}_gain", [P, KC], F32))
        gain_in, root, sq_step, scaled_ready, turned, copied, inverse = (
            m.sem(f"{tag}_{x}") for x in ("gain_in", "root", "sq_step", "scaled", "turned", "copied", "inverse"))
        with nc.Block() as block:
            @block.scalar
            def _(act):
                with nc.allow_non_contiguous_dma(reason="a gain vector onto partitions"):
                    act.dma_start(gain_t[:], gain.rearrange("(c p) -> p c", p=P)).then_inc(gain_in, 16)
                own_steps = Steps(act, sq_step)
                for t in range(NT):
                    r = P if t < FULL else LAST
                    own_steps.after(nc.scalar.activation(squares[0:r], m.h[0:r, t, :], ACT.Square,
                                                         accum_out=ss[0:r, t:t + 1]))
                nc.scalar.activation(rstd[:, 0:FULL], ss[:, 0:FULL], ACT.Sqrt, scale=1.0 / D,
                                     bias=m.eps[:, 0:1])
                nc.scalar.activation(rstd[0:LAST, FULL:NT], ss[0:LAST, FULL:NT], ACT.Sqrt, scale=1.0 / D,
                                     bias=m.eps[0:LAST, 0:1]).then_inc(root, 1)
                act.wait_ge(inverse, 1)

                def tile(t, turn, slot, r):
                    act.wait_ge(turned, t + 1)
                    alone(act, m)
                    nc.scalar.activation(scaled[0:r, slot], m.h[0:r, bass.ds(t, 1), :], ACT.Copy,
                                         scale=rstd[0:r, bass.ds(t, 1)]).then_inc(scaled_ready, 1)

                over_tiles(act, tile)

            @block.vector
            def _(dve):
                dve.wait_ge(root, 1)
                nc.vector.reciprocal(rstd[:, 0:FULL], rstd[:, 0:FULL])
                nc.vector.reciprocal(rstd[0:LAST, FULL:NT], rstd[0:LAST, FULL:NT]).then_inc(inverse, 1)
                dve.sem_inc(copied, 2)
                dve.wait_ge(gain_in, 16)

                def tile(t, turn, slot, r):
                    dve.wait_ge(turned, t + 3)
                    src = m.ps[:, 2 * slot:2 * slot + 2, :].rearrange("p a (b c) -> p (a b) c", c=P)[:, :, 0:r]
                    dst = m.actT[:, 0:KC, bass.ds(t * P, r)]
                    g = gain_t[:].rearrange("p (c o) -> p c o", o=1).to_broadcast([P, KC, r])
                    nc.vector.tensor_tensor(dst, src, g, ALU.mult).then_inc(copied, 1)

                over_tiles(dve, tile)

            @block.tensor
            def _(pe):
                pe.sem_inc(turned, 2)

                def tile(t, turn, slot, r):
                    pe.wait_ge(scaled_ready, t + 1)
                    pe.wait_ge(copied, t + 1)
                    for c in range(KC):
                        bank, at = 2 * slot + c // 4, (c % 4) * P
                        last = nc.tensor.transpose(m.ps[:, bank, at:at + r], scaled[0:r, slot, c * P:(c + 1) * P],
                                                   m.ident[0:r, 0:r])
                    last.then_inc(turned, 1)

                over_tiles(pe, tile)



def run(nc, sync, tensor, scalar, vector):
    with nc.Block() as block:
        @block.sync
        def _(sp):
            for program in sync:
                program(sp)

        @block.tensor
        def _(pe):
            for program in tensor:
                program(pe)

        @block.scalar
        def _(act):
            for program in scalar:
                program(act)

        @block.vector
        def _(dve):
            for program in vector:
                program(dve)


def token_programs(own, nc, m, w, groups, tok, tag, two=True, spare=None):
    starts = [sum(g[1] for g in groups[:j]) for j in range(len(groups))]
    width = sum(g[1] for g in groups)
    by_act = [j for j, g in enumerate(groups) if g[3] or not two]
    by_dve = [j for j in range(len(groups)) if j not in by_act]
    n_act, n_dve = len(by_act), len(by_dve)
    stores = []
    for j, g in enumerate(groups):
        if stores and g[2] == stores[-1][2] + stores[-1][1] - stores[-1][0]:
            stores[-1] = (stores[-1][0], starts[j] + g[1], stores[-1][2])
        else:
            stores.append((starts[j], starts[j] + g[1], g[2]))
    per_tile = 16 * len(stores)
    E = own.enter_context
    own_width = width - (groups[-1][1] if spare is not None else 0)
    wt = E(nc.sbuf_tensor(f"{tag}_w", [P, KC, own_width], F32))
    weights = [wt[:, :, a:a + g[1]] if a < own_width else spare for a, g in zip(starts, groups)]
    rows = E(nc.sbuf_tensor(f"{tag}_rows", [P, 2, KC, P], F32))
    stage = E(nc.sbuf_tensor(f"{tag}_stage", [P, 2, width], F32))
    w_in = [m.sem(f"{tag}_w_in{j}") for j in range(len(groups))]
    rows_ready, product, act_out, dve_out = (
        m.sem(f"{tag}_{x}") for x in ("rows", "product", "act_out", "dve_out"))
    stored = [m.sem(f"{tag}_stored{s}") for s in range(2)]
    wr = w.rearrange("(c p) n -> p c n", p=P)

    def load(sp):
        for j, g in enumerate(groups):
            sp.dma_start(weights[j], wr[:, :, g[0]:g[0] + g[1]]).then_inc(w_in[j], 16)

    def store(sp):
        for s in range(2):
            sp.sem_inc(stored[s], per_tile)

        def tile(t, turn, slot, r):
            if n_act:
                sp.wait_ge(act_out, n_act * (t + 2))
                alone(sp, m)
            if n_dve:
                sp.wait_ge(dve_out, n_dve * (t + 2))
                alone(sp, m)
            for a, b, c0 in stores:
                sp.dma_start(tok[bass.ds(t * P, r), c0:c0 + b - a], stage[0:r, slot, a:b]).then_inc(stored[slot], 16)

        over_tiles(sp, tile)
        sp.wait_ge(stored[0], per_tile * (FULL // 2 + 2))
        sp.wait_ge(stored[1], per_tile * (FULL // 2 + 1))

    def scalar(act):
        if n_act:
            act.sem_inc(act_out, n_act)

        def stage_rows(t, turn, slot, r):
            nc.scalar.copy(rows[:, slot, :, 0:r], m.actT[:, 0:KC, bass.ds(t * P, r)]).then_inc(rows_ready, 1)

        def tile(t, turn, slot, r):
            for j in by_act:
                act.wait_ge(product, len(groups) * t + j + 1)
                if j == by_act[0]:
                    act.wait_ge(stored[slot], per_tile * (turn + 1))
                nc.scalar.activation(stage[0:r, slot, starts[j]:starts[j] + groups[j][1]],
                                     m.ps[0:r, j, 0:groups[j][1]], ACT.Silu if groups[j][3] else ACT.Copy)\
                    .then_inc(act_out, 1)
            act.wait_ge(product, len(groups) * (t + 1))

        stage_rows(0, 0, 0, P)
        with act.Fori(0, FULL // 2 - 1) as i:
            stage_rows(2 * i + 1, i, 1, P)
            tile(2 * i, i, 0, P)
            stage_rows(2 * i + 2, i + 1, 0, P)
            tile(2 * i + 1, i, 1, P)
        stage_rows(FULL - 1, FULL // 2 - 1, 1, P)
        tile(FULL - 2, FULL // 2 - 1, 0, P)
        stage_rows(FULL, FULL // 2, 0, LAST)
        tile(FULL - 1, FULL // 2 - 1, 1, P)
        tile(FULL, FULL // 2, 0, LAST)

    def vector(dve):
        if n_dve:
            dve.sem_inc(dve_out, n_dve)

            def tile(t, turn, slot, r):
                for j in by_dve:
                    dve.wait_ge(product, len(groups) * t + j + 1)
                    if j == by_dve[0]:
                        dve.wait_ge(stored[slot], per_tile * (turn + 1))
                    nc.vector.tensor_copy(stage[0:r, slot, starts[j]:starts[j] + groups[j][1]],
                                          m.ps[0:r, j, 0:groups[j][1]]).then_inc(dve_out, 1)

            over_tiles(dve, tile)

    def tensor(pe):
        def tile(t, turn, slot, r):
            pe.wait_ge(rows_ready, t + 1)
            for j, g in enumerate(groups):
                pe.wait_ge(w_in[j], 16)
                if j in by_act:
                    pe.wait_ge(act_out, n_act * t + by_act.index(j) + 1)
                else:
                    pe.wait_ge(dve_out, n_dve * t + by_dve.index(j) + 1)
                for c in range(KC):
                    last = nc.tensor.matmul(m.ps[0:r, j, 0:g[1]], rows[:, slot, c, 0:r],
                                            weights[j][:, c, :],
                                            start=(c == 0), stop=(c == KC - 1))
                last.then_inc(product, 1)

        over_tiles(pe, tile)

    return load, store, tensor, scalar, vector



def project_features(nc, m, w, parts, tag):
    with ExitStack() as own:
        load, pe, act, dve, _ = feature_programs(own, nc, m, w, parts, tag, True)
        run(nc, [load], [pe], [act], [dve])


def feature_programs(own, nc, m, w, parts, tag, two):
    E = own.enter_context
    wring = E(nc.sbuf_tensor(f"{tag}_w", [P, 2, KC, 2 * P], F32))
    w_in = [m.sem(f"{tag}_w_in{s}") for s in range(2)]
    product, first_out, second_out = (m.sem(f"{tag}_{x}") for x in ("product", "first_out", "second_out"))
    credit = 4 * len(SLICES)
    wr = w.rearrange("(c p) n -> p c n", p=P)
    NS = len(SLICES)

    def over_turns(eng, body):
        base = 0
        for part in parts:
            with eng.Fori(0, part[1] // 4) as i:
                body(base + i, i, part)
            base += part[1] // 4
        return base

    def load(sp):
        def turn(n, i, part):
            for s in range(2):
                sp.wait_ge(product, 2 * NS * (2 * n + s + 1))
                sp.dma_start(wring[:, s], wr[:, :, bass.ds(part[0] + i * 4 * P + s * 2 * P, 2 * P)])\
                    .then_inc(w_in[s], 16)

        over_turns(sp, turn)

    def tensor(pe):
        pe.sem_inc(product, credit)

        def turn(n, i, part):
            for s in range(2):
                pe.wait_ge(w_in[s], 16 * n + 16)
                for j in range(2):
                    for k, (t0, tn) in enumerate(SLICES):
                        pe.wait_ge(first_out if j == 0 else second_out, NS * (2 * n + s) + k + 1)
                        for c in range(KC):
                            last = nc.tensor.matmul(m.ps[:, NS * j + k, 0:tn],
                                                    wring[:, s, c, j * P:(j + 1) * P],
                                                    m.actT[:, c, t0:t0 + tn],
                                                    start=(c == 0), stop=(c == KC - 1))
                        last.then_inc(product, 1)

        over_turns(pe, turn)

    def evacuate(eng, tiles, copy):
        for j in tiles:
            eng.sem_inc(first_out if j == 0 else second_out, NS)

        def turn(n, i, part):
            for s in range(2):
                for j in tiles:
                    for k, (t0, tn) in enumerate(SLICES):
                        eng.wait_ge(product, credit + NS * (2 * (2 * n + s) + j) + k + 1)
                        copy(part[2][:, bass.ds(4 * i + 2 * s + j, 1), t0:t0 + tn],
                             m.ps[:, NS * j + k, 0:tn]).then_inc(first_out if j == 0 else second_out, 1)

        over_turns(eng, turn)

    def scalar(act):
        evacuate(act, [0] if two else [0, 1], nc.scalar.copy)

    def vector(dve):
        if two:
            evacuate(dve, [1], nc.vector.tensor_copy)

    def all_out(eng):
        turns = sum(part[1] // 4 for part in parts)
        eng.wait_ge(first_out, NS * (2 * turns + 1))
        eng.wait_ge(second_out, NS * (2 * turns + 1))

    return load, tensor, scalar, vector, all_out


def feature_units(own, nc, m, w, first, dest, tag):
    tiles = dest.shape[1]
    NS = len(SLICES)
    wring = own.enter_context(nc.sbuf_tensor(f"{tag}_w", [P, 2, KC, 2 * P], F32))
    w_in = [m.sem(f"{tag}_w_in{s}") for s in range(2)]
    product, copied = m.sem(f"{tag}_product"), m.sem(f"{tag}_copied")
    wr = w.rearrange("(c p) n -> p c n", p=P)

    def load(sp):
        for n in range(tiles // 2):
            if n >= 2:
                sp.wait_ge(product, 2 * NS * (n - 1))
            c0 = first + 2 * P * n
            sp.dma_start(wring[:, n % 2], wr[:, :, c0:c0 + 2 * P]).then_inc(w_in[n % 2], 16)

    def make(pe, u):
        n, bank, (t0, tn) = u // (2 * NS), u % (2 * NS), SLICES[u % NS]
        if bank == 0:
            pe.wait_ge(w_in[n % 2], 16 * (n // 2 + 1))
        if u >= 2 * NS:
            pe.wait_ge(copied, u - 2 * NS + 1)
        for c in range(KC):
            last = nc.tensor.matmul(m.ps[:, bank, 0:tn], wring[:, n % 2, c, bank // NS * P:(bank // NS + 1) * P],
                                    m.actT[:, c, t0:t0 + tn], start=(c == 0), stop=(c == KC - 1))
        last.then_inc(product, 1)

    def copy(act, u):
        t0, tn = SLICES[u % NS]
        act.wait_ge(product, u + 1)
        nc.scalar.copy(dest[:, u // NS, t0:t0 + tn], m.ps[:, u % (2 * NS), 0:tn]).then_inc(copied, 1)

    return load, make, copy



def gate_programs(own, nc, m, io):
    NG = NT + NB
    E = own.enter_context
    x = E(nc.sbuf_tensor("dg_x", [P, NG, 4], F32))
    e = E(nc.sbuf_tensor("dg_e", [P, NG, 4], F32))
    e2 = E(nc.sbuf_tensor("dg_e2", [P, NG, 4], F32))
    per_head = E(nc.sbuf_tensor("dg_head", [P, 2, 4], F32))
    rate = E(nc.sbuf_tensor("dg_rate", [P, 4], F32))
    cleared, raw_in, magnitude, exps, step = (m.sem("dg_" + n) for n in
                                              ("cleared", "raw_in", "magnitude", "exps", "step"))
    def load(sp):
        c0 = TOK_R + 512
        sp.wait_ge(cleared, 1)
        sp.dma_start(m.gates[:, 0:FULL, :], m.tok[0:FULL * P, c0:c0 + 8].rearrange("(t p) c -> p t c", p=P))\
            .then_inc(raw_in, 16)
        sp.dma_start(m.gates[0:TAIL, FULL, :], m.tok[FULL * P:L, c0:c0 + 8]).then_inc(raw_in, 16)
        sample = m.tok[L:T, c0:c0 + 8].rearrange("(o b) c -> o b c", o=1).to_broadcast([P, NB, 8])
        sp.dma_start(m.gates[:, NT:NG, :], sample).then_inc(raw_in, 16)
        sp.dma_start(per_head[:, 0], io["dt_bias_b"].to_broadcast([P, 4])).then_inc(raw_in, 16)
        sp.dma_start(per_head[:, 1], io["a_log_b"].to_broadcast([P, 4])).then_inc(raw_in, 16)

    def scalar(act):
        act.wait_ge(raw_in, 80)
        nc.scalar.activation(rate[:], per_head[:, 1], ACT.Exp)
        nc.scalar.activation(e2[:], m.gates[:, :, 4:8], ACT.Exp, scale=-1.0)
        act.wait_ge(magnitude, 1)
        nc.scalar.activation(e[:], e[:], ACT.Exp, scale=-1.0).then_inc(exps, 1)
        act.wait_ge(exps, 1)
        nc.scalar.activation(e[:], e[:], ACT.Ln, bias=m.ones[:, 0:1]).then_inc(exps, 1)

    def vector(dve):
        dve.memset(m.gates[:, FULL, :], 0.0).then_inc(cleared, 1)
        dve.wait_ge(raw_in, 80)
        steps = Steps(dve, step)
        head = lambda ap: ap.rearrange("p (o h) -> p o h", o=1).to_broadcast([P, NG, 4])
        steps.after(nc.vector.tensor_tensor(x[:], m.gates[:, :, 0:4], head(per_head[:, 0]), ALU.add))
        nc.vector.scalar_tensor_tensor(out=e[:], in0=x[:], scalar=-1.0, in1=x[:], op0=ALU.mult, op1=ALU.max)\
            .then_inc(magnitude, 1)
        dve.wait_ge(exps, 2)
        steps.after(nc.vector.scalar_tensor_tensor(out=x[:], in0=x[:], scalar=0.0, in1=e[:], op0=ALU.max,
                                                   op1=ALU.add))
        steps.after(nc.vector.scalar_tensor_tensor(out=m.gates[:, :, 0:4], in0=x[:], scalar=-1.0,
                                                   in1=head(rate[:]), op0=ALU.mult, op1=ALU.mult))
        steps.after(nc.vector.tensor_scalar(e2[:], e2[:], 1.0, None, ALU.add))
        nc.vector.reciprocal(m.gates[:, :, 4:8], e2[:])

    return load, scalar, vector


def convolve_and_normalise(nc, m, io):
    NF, NQK = 12, 2 * B_H
    NS = len(SLICES)
    with ExitStack() as own:
        E = own.enter_context
        past = E(nc.sbuf_tensor("cv_past", [NB * 3 + CONV, NF * P], F32))
        pastT = E(nc.sbuf_tensor("cv_pastT", [P, NF, NB * 3 + CONV], F32))
        fresh = E(nc.sbuf_tensor("cv_fresh", [3 + NB, NF * P], F32))
        y = E(nc.sbuf_tensor("cv_y", [P, 2, L], F32))
        ys = E(nc.sbuf_tensor("cv_ys", [P, 2, NF, NB], F32))
        past_in, turned, copied, conv_out, conv_step, sample_out, silued, stored = (
            m.sem("cv_" + x) for x in ("past_in", "turned", "copied", "out", "step", "sample", "silued", "stored"))
        taps = NB * 3
        sq = E(nc.sbuf_tensor("l2_sq", [P, 2, T], F32))
        root = E(nc.sbuf_tensor("l2_root", [P, 2, T], F32))
        epsq = E(nc.sbuf_tensor("l2_epsq", [P, 1], F32))
        squared, summed, rooted, scaled, inverse, eps_set = (
            m.sem("l2_" + x) for x in ("squared", "summed", "rooted", "scaled", "inverse", "eps_set"))
        load_weights, make_unit, copy_unit = feature_units(own, nc, m, io["w_in_e"][0], 0, m.qT, "aq")
        UNITS = H * NS
        gates_load, gates_act, gates_dve = gate_programs(own, nc, m, io)

        with nc.Block() as block:
            @block.sync
            def _(sp):
                conv_state = io["state_b_conv"][0]
                sp.dma_start(past[0:taps, :], conv_state.rearrange("b r c -> (b r) c")).then_inc(past_in, 16)
                sp.dma_start(past[taps:taps + CONV, :], io["conv_b"][0]).then_inc(past_in, 16)
                gates_load(sp)
                load_weights(sp)
                sp.dma_start(io["sb_conv"][0, :, 0:2, :], conv_state[:, 1:3, :]).then_inc(stored, 16)
                sp.wait_ge(copied, 2)
                sp.dma_start(io["pb_conv"][0, 0], fresh[0:3, :]).then_inc(stored, 16)
                sp.dma_start(io["sb_conv"][0, :, 2, :], fresh[3:3 + NB, :]).then_inc(stored, 16)
                sp.wait_ge(stored, 48)

            @block.tensor
            def _(pe):
                for f in range(NF):
                    nc.tensor.transpose(m.ps[0:3 + NB, 1 + f // 4, f % 4 * P:f % 4 * P + P],
                                        m.mixT[:, f, L - 3:T], m.ident[:])
                pe.wait_ge(past_in, 32)
                n = taps + CONV
                for f in range(NF):
                    last = nc.tensor.transpose(m.ps[:, 0, f * n:f * n + n], past[:, f * P:(f + 1) * P],
                                               m.ident[0:n, 0:n])
                last.then_inc(turned, 1)
                pe.wait_ge(copied, 2)
                for u in range(UNITS):
                    make_unit(pe, u)
                    for j in range(2 * (u - UNITS // 2), 2 * (u - UNITS // 2) + 2):
                        if j >= 0:
                            t0, tn = SLICES[j % NS]
                            pe.wait_ge(squared, j // NS + 1)
                            if j >= 2:
                                pe.wait_ge(rooted, j - 1)
                            nc.tensor.matmul(m.ps[:, 6 + j % 2, 0:tn], m.ones[:], sq[:, j // NS % 2, t0:t0 + tn],
                                             start=True, stop=True).then_inc(summed, 1)

            @block.scalar
            def _(act):
                n = taps + CONV
                act.wait_ge(turned, 1)
                nc.scalar.copy(pastT[:], m.ps[:, 0, 0:NF * n].rearrange("p (f n) -> p f n", n=n)).then_inc(copied, 1)
                nc.scalar.copy(fresh[:].rearrange("p (a b) -> p a b", b=512), m.ps[0:3 + NB, 1:4, :])\
                    .then_inc(copied, 1)
                gates_act(act)
                act.wait_ge(sample_out, 1)
                nc.scalar.activation(m.mixT[:, :, L:T], ys[:, 0], ACT.Silu).then_inc(silued, 1)
                for f in range(NF):
                    act.wait_ge(conv_out, f + 1)
                    nc.scalar.activation(m.mixT[:, f, 0:L], y[:, f % 2], ACT.Silu).then_inc(silued, 1)
                    copy_unit(act, f)

                def roots(j):
                    t, (t0, tn) = j // NS, SLICES[j % NS]
                    act.wait_ge(summed, j + 1)
                    if t >= 2:
                        act.wait_ge(scaled, t - 1)
                    scale, eps = (float(P), epsq) if t < B_H else (1.0, m.eps)
                    nc.scalar.activation(root[:, t % 2, t0:t0 + tn], m.ps[:, 6 + j % 2, 0:tn], ACT.Sqrt, scale=scale,
                                         bias=eps[:, 0:1]).then_inc(rooted, 1)

                act.wait_ge(eps_set, 1)
                act.wait_ge(silued, NF + 2)
                for k in range(UNITS // 2 + 1):
                    for j in (2 * k, 2 * k + 1):
                        if j % NS == 0 and j // NS < NQK:
                            if j // NS >= 2:
                                act.wait_ge(summed, NS * (j // NS - 1))
                            nc.scalar.activation(sq[:, j // NS % 2], m.mixT[:, j // NS], ACT.Square)\
                                .then_inc(squared, 1)
                    if k < UNITS // 2:
                        copy_unit(act, UNITS // 2 + k)
                    if k:
                        roots(2 * k - 2)
                        roots(2 * k - 1)

            @block.vector
            def _(dve):
                dve.memset(epsq[:], EPS * P).then_inc(eps_set, 1)
                gates_dve(dve)
                dve.wait_ge(copied, 2)
                steps = Steps(dve, conv_step)
                w = lambda i: pastT[:, :, taps + i:taps + i + 1].to_broadcast([P, NF, NB])
                old = pastT[:, :, 0:taps].rearrange("p f (b r) -> p f b r", r=3)
                steps.after(nc.vector.tensor_tensor(ys[:, 0], m.mixT[:, :, L:T], w(3), ALU.mult))
                for r in range(3):
                    steps.after(nc.vector.tensor_tensor(ys[:, 1], old[:, :, :, r], w(r), ALU.mult))
                    ins = nc.vector.tensor_tensor(ys[:, 0], ys[:, 0], ys[:, 1], ALU.add)
                    if r < 2:
                        steps.after(ins)
                ins.then_inc(sample_out, 1)
                dve.sem_inc(silued, 1)
                n0 = steps.n
                with dve.Fori(0, NF // 2) as i:
                    steps = Steps(dve, conv_step, 6 * i + n0)
                    for s in range(2):
                        f = bass.ds(2 * i + s, 1)
                        x = lambda a, b: m.mixT[:, f, a:b]
                        tap = lambda k: pastT[:, f, taps + k:taps + k + 1].rearrange("p a b -> p (a b)")
                        dve.wait_ge(silued, 2 * i + s + 1)
                        steps.after(nc.vector.tensor_scalar(y[:, s:s + 1, :], x(0, L), tap(3), None, ALU.mult))
                        for k in range(1, CONV):
                            ins = nc.vector.scalar_tensor_tensor(out=y[:, s:s + 1, k:L], in0=x(0, L - k),
                                                                 scalar=tap(3 - k), in1=y[:, s:s + 1, k:L],
                                                                 op0=ALU.mult, op1=ALU.add)
                            if k < CONV - 1:
                                steps.after(ins)
                        ins.then_inc(conv_out, 1)
                with dve.Fori(0, NQK // 2) as i:
                    for s in range(2):
                        n = 2 * i + s
                        dve.wait_ge(rooted, NS * n + NS)
                        nc.vector.reciprocal(root[:, s], root[:, s]).then_inc(inverse, 1)
                        dve.wait_ge(inverse, n + 1)
                        nc.vector.tensor_tensor(m.mixT[:, bass.ds(n, 1), :], m.mixT[:, bass.ds(n, 1), :],
                                                root[:, s:s + 1], ALU.mult).then_inc(scaled, 1)



def delta_prompt(nc, m, io):
    HG = B_H // 2
    with ExitStack() as own:
        E = own.enter_context
        sb = lambda name, shape: E(nc.sbuf_tensor("dp_" + name, shape, F32))
        mats = lambda name, n: sb(name, [P, 2, n, HG, P])
        qkv = mats("qkv", 3)
        state = sb("state", [P, B_H, P])
        gu, far, decay, low_up = mats("gu", 1), mats("far", 1), mats("decay", 1), mats("low_up", 2)
        nn = mats("qk_N_NT", 3)
        D1, N2, N4, G1 = mats("D1", 2), mats("N2", 2), mats("N4", 1), mats("G1", 2)
        U, between, kv = mats("U", 1), mats("between", 4), mats("kd_vb", 2)
        T_, u, rhs, o, osq, y = D1, U, gu, N4, far, decay
        cums, ex = sb("cums", [P, 2, 3, HG]), sb("ex", [P, 2, 4, HG])
        SUM, REST, TOTAL = 0, 1, 2
        CUM, LEFT, BETA, TOT = 0, 1, 2, 3
        nbg, oss, ors, minus_half = (sb(x, [P, 2, HG]) for x in ("nbg", "oss", "ors", "minus_half"))
        gate = sb("gate", [P, 512])
        masks = sb("masks", [P, 7, P])
        norm_g = sb("norm_g", [P, 1])
        names = ("staged gu_ready sums_mm rows_mm cums_out far_out decayed masked turn_mm n_out nt_mm nt_out "
                 "blocks_out between_out sq_mm sq_out quad_mm quad_out t8_mm t8_out lt_mm lt_out lift_mm lift_out "
                 "ks_mm rhs_out u_mm u_out o_mm o_out ds_mm state_out oss_out ors_out y_out y_mm y_turned exps_out "
                 "own_step").split()
        s = [{x: m.sem(f"dp{g}_{x}") for x in names} for g in range(2)]
        masks_in, gate_in, half_set, state_stored = (
            m.sem("dp_" + x) for x in ("masks_in", "gate_in", "half_set", "state_stored"))
        UPPER, STRICT, EIGHT, BETWEEN = 0, 1, 2, 3
        both = range(2)
        ps = lambda g, bank, k0, k1, r, c: m.ps[:, 4 * g + bank, :].rearrange("p (k h c) -> p k h c", k=2, h=HG)[
            0:r, k0:k1, :, 0:c]
        part = lambda t, g, k0, k1, r, c: t[0:r, g, k0:k1, :, 0:c]

        def over_chunks(eng, body):
            with eng.Fori(0, FULL) as c:
                body(c, P)
            body(FULL, TAIL)

        def spans(C):
            return [b for b in (8, 16, 32, 64) if b < C]

        def column(ap, C, n):
            kinds = ap.shape[1]
            return ap.rearrange("p k (h o) -> p k h o", o=1).to_broadcast([C, kinds, HG, n])

        def mask(C, i, n=1):
            return masks[0:C, i:i + n, 0:C].rearrange("p k (o c) -> p k o c", o=1).to_broadcast([C, n, HG, C])

        def same(ap, C, n):
            return ap[:, 0].rearrange("p (o h) c -> p o h c", o=1).to_broadcast([C, n, HG, C])

        with nc.Block() as block:
            @block.sync
            def _(sp):
                sp.dma_start(masks[:], io["c_delta_masks"]).then_inc(masks_in, 16)
                with nc.allow_non_contiguous_dma(reason="a gain vector onto partitions"):
                    sp.dma_start(norm_g[:], io["norm_b"].rearrange("o p -> p o")).then_inc(masks_in, 16)

                def chunk(c, C):
                    for g in both:
                        sp.wait_ge(s[g]["y_out"], c + 1)
                        alone(sp, m)
                    sp.dma_start(gate[0:C, :], m.tok[bass.ds(c * P, C), TOK_R:TOK_R + 512]).then_inc(gate_in, 16)

                over_chunks(sp, chunk)
                for g in both:
                    sp.wait_ge(s[g]["state_out"], NT + 1)
                sp.dma_start(io["pb_s"][0, 0].rearrange("h k v -> k h v"), state[:]).then_inc(state_stored, 16)
                sp.wait_ge(state_stored, 16)

            @block.gpsimd
            def _(pool):
                nc.gpsimd.memset(minus_half[:], -0.5).then_inc(half_set, 1)
                pool.wait_ge(half_set, 1)
                pool.wait_ge(masks_in, 32)
                mixT = m.mixT[:].rearrange("p (k h) t -> p k h t", k=3)

                def gates(c, C, g, a):
                    at = a + HG * g
                    return m.gates[0:C, bass.ds(c, 1), at:at + HG]

                def chunk(c, C):
                    for g in both:
                        pool.wait_ge(s[g]["u_mm"], c + 1)
                        alone(pool, m)
                        for k in range(3):
                            last = nc.gpsimd.tensor_copy(qkv[:, g, k, :, 0:C],
                                                         mixT[:, k, HG * g:HG * g + HG, bass.ds(c * P, C)])
                        last.then_inc(s[g]["staged"], 1)
                        nc.gpsimd.tensor_tensor(part(gu, g, 0, 1, C, C), mask(C, UPPER),
                                                column(gates(c, C, g, 0), C, C), ALU.mult).then_inc(s[g]["gu_ready"], 1)
                    for g in both:
                        pool.wait_ge(s[g]["decayed"], c + 1)
                        alone(pool, m)
                        nc.gpsimd.tensor_tensor(part(low_up, g, 0, 2, C, C), same(part(decay, g, 0, 1, C, C), C, 2),
                                                mask(C, UPPER, 2), ALU.mult).then_inc(s[g]["masked"], 1)
                        pool.wait_ge(s[g]["masked"], 2 * c + 1)
                        alone(pool, m)
                        nc.gpsimd.tensor_tensor(part(low_up, g, 1, 2, C, C), part(low_up, g, 1, 2, C, C),
                                                column(gates(c, C, g, 4), C, C), ALU.mult).then_inc(s[g]["masked"], 1)
                    for g in both:
                        pool.wait_ge(s[g]["nt_out"], c + 1)
                        alone(pool, m)
                        n = len(spans(C))
                        nc.gpsimd.tensor_tensor(part(between, g, 0, n, C, C), same(part(nn, g, 2, 3, C, C), C, n),
                                                mask(C, BETWEEN, n), ALU.mult).then_inc(s[g]["between_out"], 1)
                    for g in both:
                        pool.wait_ge(s[g]["oss_out"], c + 1)
                        alone(pool, m)
                        nc.gpsimd.tensor_scalar(ors[0:C, g], oss[0:C, g], 1.0 / P, EPS, ALU.mult, ALU.add)\
                            .then_inc(s[g]["ors_out"], 1)
                        pool.wait_ge(s[g]["ors_out"], 2 * c + 1)
                        alone(pool, m)
                        nc.gpsimd.tensor_tensor(ors[0:C, g], ors[0:C, g], minus_half[0:C, g], ALU.pow)\
                            .then_inc(s[g]["ors_out"], 1)

                over_chunks(pool, chunk)

            @block.scalar
            def _(act):
                for g in both:
                    act.sem_inc(s[g]["y_turned"], 1)

                def chunk(c, C):
                    def copy(g, dst, src, out):
                        nc.scalar.copy(dst, src).then_inc(s[g][out], 1)

                    for g in both:
                        act.wait_ge(s[g]["cums_out"], c + 1)
                        nc.scalar.activation(ex[0:C, g, CUM:LEFT + 1, :], cums[0:C, g, SUM:REST + 1, :], ACT.Exp)
                        nc.scalar.activation(ex[:, g, TOT], cums[:, g, TOTAL], ACT.Exp).then_inc(s[g]["exps_out"], 1)
                    for g in both:
                        act.wait_ge(s[g]["far_out"], c + 1)
                        nc.scalar.activation(part(decay, g, 0, 1, C, C), part(far, g, 0, 1, C, C), ACT.Exp, scale=-1.0)\
                            .then_inc(s[g]["decayed"], 1)
                    for g in both:
                        act.wait_ge(s[g]["nt_mm"], c + 1)
                        copy(g, part(nn, g, 2, 3, C, C), ps(g, 0, 0, 1, C, C), "nt_out")
                    for g in both:
                        act.wait_ge(s[g]["sq_mm"], c + 1)
                        copy(g, part(N2, g, 0, 2, C, C), ps(g, 1, 0, 2, C, C), "sq_out")
                    for g in both:
                        act.wait_ge(s[g]["quad_mm"], c + 1)
                        copy(g, part(N4, g, 0, 1, C, C), ps(g, 3, 0, 1, C, C), "quad_out")
                    for j in range(len(spans(C))):
                        for g in both:
                            act.wait_ge(s[g]["lt_mm"], 4 * c + j + 1)
                            copy(g, part(U, g, 0, 1, C, C), ps(g, 1, 0, 1, C, C), "lt_out")
                    for g in both:
                        act.wait_ge(s[g]["u_mm"], c + 2)
                        copy(g, part(u, g, 0, 1, C, P), ps(g, 0, 0, 1, C, P), "u_out")
                    for g in both:
                        act.wait_ge(s[g]["o_out"], c + 1)
                        for h in range(HG):
                            last = nc.scalar.activation(osq[0:C, g, 0, h], o[0:C, g, 0, h], ACT.Square,
                                                        accum_out=oss[0:C, g, h:h + 1])
                        last.then_inc(s[g]["oss_out"], 1)
                    for g in both:
                        act.wait_ge(s[g]["y_mm"], c + 1)
                        nc.scalar.activation(m.actT[:, H + HG * g:H + HG * g + HG, bass.ds(c * P, C)],
                                             ps(g, 3, 0, 1, P, C)[:, 0], ACT.Copy, scale=norm_g[:, 0:1])\
                            .then_inc(s[g]["y_turned"], 1)

                over_chunks(act, chunk)

            @block.vector
            def _(dve):
                dve.memset(state[:], 0.0)
                for g in both:
                    dve.sem_inc(s[g]["state_out"], 1)
                    dve.sem_inc(s[g]["y_out"], 1)

                def chunk(c, C):
                    N_STEPS = 6
                    steps = [Steps(dve, s[g]["own_step"], N_STEPS * c) for g in both]
                    V = nc.vector
                    mat = lambda t, g, k0, k1, n=C: part(t, g, k0, k1, C, n)
                    ident = m.ident[0:C, 0:C].rearrange("p (a b c) -> p a b c", a=1, b=1).to_broadcast([C, 2, HG, C])
                    for g in both:
                        at = 4 + HG * g
                        beta = m.gates[0:C, bass.ds(c, 1), at:at + HG].rearrange("p o h -> p (o h)")
                        small = lambda k, r: m.ps[0:r, 4 * g, k * HG:(k + 1) * HG]
                        dve.wait_ge(s[g]["sums_mm"], c + 1)
                        V.tensor_copy(ex[0:C, g, BETA], beta)
                        V.tensor_copy(cums[0:C, g, SUM], small(0, C))
                        steps[g].after(V.tensor_copy(cums[:, g, TOTAL], small(1, P)))
                        V.tensor_tensor(cums[0:C, g, REST], cums[0:C, g, TOTAL], cums[0:C, g, SUM], ALU.subtract)\
                            .then_inc(s[g]["cums_out"], 1)
                    for g in both:
                        dve.wait_ge(s[g]["rows_mm"], c + 1)
                        steps[g].after(V.tensor_tensor(mat(far, g, 0, 1), ps(g, 1, 0, 1, C, C),
                                                       column(cums[0:C, g, SUM:SUM + 1, :], C, C), ALU.subtract))
                        V.scalar_tensor_tensor(out=mat(far, g, 0, 1), in0=mat(far, g, 0, 1), scalar=-1.0,
                                               in1=mat(far, g, 0, 1), op0=ALU.mult, op1=ALU.max)\
                            .then_inc(s[g]["far_out"], 1)
                    for g in both:
                        dve.wait_ge(s[g]["exps_out"], c + 1)
                        V.scalar_tensor_tensor(out=nbg[0:C, g], in0=ex[0:C, g, CUM], scalar=-1.0, in1=ex[0:C, g, BETA],
                                               op0=ALU.mult, op1=ALU.mult)
                        dve.wait_ge(s[g]["turn_mm"], c + 1)
                        V.tensor_tensor(mat(kv, g, 0, 2, P), ps(g, 3, 0, 2, C, P),
                                        column(ex[0:C, g, LEFT:BETA + 1, :], C, P), ALU.mult)
                    for g in both:
                        dve.wait_ge(s[g]["masked"], 2 * c + 2)
                        V.tensor_tensor(mat(nn, g, 0, 2), ps(g, 2, 0, 2, C, C), mat(low_up, g, 0, 2), ALU.mult)\
                            .then_inc(s[g]["n_out"], 1)
                    for g in both:
                        dve.wait_ge(s[g]["n_out"], c + 1)
                        dve.wait_ge(s[g]["nt_out"], c + 1)
                        V.tensor_tensor(mat(D1, g, 0, 2), mat(nn, g, 1, 3),
                                        masks[0:C, EIGHT:EIGHT + 1, 0:C].rearrange("p k (o c) -> p k o c", o=1)
                                        .to_broadcast([C, 2, HG, C]), ALU.mult).then_inc(s[g]["blocks_out"], 1)
                    for g in both:
                        dve.wait_ge(s[g]["blocks_out"], c + 1)
                        steps[g].after(V.tensor_tensor(mat(G1, g, 0, 2), ident, mat(D1, g, 0, 2), ALU.subtract))
                    for g in both:
                        dve.wait_ge(s[g]["sq_out"], c + 1)
                        steps[g].after(V.tensor_tensor(mat(G1, g, 0, 2), mat(G1, g, 0, 2), mat(N2, g, 0, 2), ALU.add))
                    for g in both:
                        dve.wait_ge(s[g]["quad_mm"], c + 1)
                        V.tensor_tensor(mat(G1, g, 0, 2), mat(G1, g, 0, 2), ps(g, 2, 0, 2, C, C), ALU.subtract)\
                            .then_inc(s[g]["quad_out"], 1)
                    for g in both:
                        dve.wait_ge(s[g]["t8_mm"], c + 1)
                        V.tensor_tensor(mat(T_, g, 0, 2), mat(G1, g, 0, 2), ps(g, 0, 0, 2, C, C), ALU.add)\
                            .then_inc(s[g]["t8_out"], 1)
                    for j in range(len(spans(C))):
                        for g in both:
                            dve.wait_ge(s[g]["lift_mm"], 4 * c + j + 1)
                            V.tensor_tensor(mat(T_, g, 0, 2), mat(T_, g, 0, 2), ps(g, 2, 0, 2, C, C), ALU.subtract)\
                                .then_inc(s[g]["lift_out"], 1)
                    for g in both:
                        dve.wait_ge(s[g]["ks_mm"], c + 1)
                        for h in range(HG):
                            last = V.scalar_tensor_tensor(out=rhs[0:C, g, 0, h], in0=ps(g, 3, 0, 1, C, P)[:, 0, h],
                                                          scalar=nbg[0:C, g, h:h + 1], in1=kv[0:C, g, 1, h],
                                                          op0=ALU.mult, op1=ALU.add)
                        last.then_inc(s[g]["rhs_out"], 1)
                        steps[g].after(V.tensor_tensor(mat(o, g, 0, 1, P), ps(g, 3, 1, 2, C, P),
                                                       column(ex[0:C, g, CUM:CUM + 1, :], C, P), ALU.mult))
                    for g in both:
                        dve.wait_ge(s[g]["o_mm"], c + 1)
                        V.tensor_tensor(mat(o, g, 0, 1, P), mat(o, g, 0, 1, P), ps(g, 1, 0, 1, C, P), ALU.add)\
                            .then_inc(s[g]["o_out"], 1)
                        dve.wait_ge(s[g]["ds_mm"], c + 1)
                        for h in range(HG):
                            last = V.scalar_tensor_tensor(out=state[:, HG * g + h], in0=state[:, HG * g + h],
                                                          scalar=ex[:, g, TOT, h:h + 1],
                                                          in1=ps(g, 2, 0, 1, P, P)[:, 0, h], op0=ALU.mult, op1=ALU.add)
                        last.then_inc(s[g]["state_out"], 1)
                    for g in both:
                        g4 = gate[0:C, :].rearrange("p (a k h d) -> p a k h d", a=2, k=1, h=HG)[:, g]
                        dve.wait_ge(gate_in, 16 * c + 16)
                        dve.wait_ge(s[g]["o_out"], c + 1)
                        steps[g].after(V.tensor_tensor(mat(y, g, 0, 1, P), mat(o, g, 0, 1, P), g4, ALU.mult))
                    for g in both:
                        dve.wait_ge(s[g]["ors_out"], 2 * c + 2)
                        V.tensor_tensor(mat(y, g, 0, 1, P), mat(y, g, 0, 1, P),
                                        column(ors[0:C, g:g + 1, :], C, P), ALU.mult).then_inc(s[g]["y_out"], 1)

                    assert all(x.n == N_STEPS for x in steps)

                over_chunks(dve, chunk)

            @block.tensor
            def _(pe):
                for g in both:
                    pe.sem_inc(s[g]["u_mm"], 1)
                pe.wait_ge(masks_in, 32)

                def chunk(c, C):
                    def product(g, bank, k, lhs, rhs, r, n, turn=False):
                        for h in range(HG):
                            out = ps(g, bank, k, k + 1, r, n)[:, 0, h]
                            if turn:
                                last = nc.tensor.transpose(out, lhs(h), m.ident[0:rhs, 0:rhs])
                            else:
                                last = nc.tensor.matmul(out, lhs(h), rhs(h), start=True, stop=True)
                        return last

                    mat = lambda t, g, k, n=C: (lambda h: t[0:C, g, k, h, 0:n])
                    feat = lambda g, k: (lambda h: qkv[:, g, k, h, 0:C])
                    S = lambda g: (lambda h: state[:, HG * g + h, :])
                    Q, K, VV = 0, 1, 2
                    for g in both:
                        gs = m.gates[0:C, bass.ds(c, 1), HG * g:HG * g + HG].rearrange("p o h -> p (o h)")
                        b0 = m.ps[:, 4 * g, :]
                        pe.wait_ge(s[g]["staged"], c + 1)
                        alone(pe, m)
                        nc.tensor.matmul(b0[0:C, 0:HG], masks[0:C, UPPER, 0:C], gs, start=True, stop=True)
                        nc.tensor.matmul(b0[:, HG:2 * HG], m.ones[0:C, :], gs, start=True, stop=True)\
                            .then_inc(s[g]["sums_mm"], 1)
                        pe.wait_ge(s[g]["gu_ready"], c + 1)
                        nc.tensor.matmul(ps(g, 1, 0, 1, C, C)[:, 0], m.ones[0:C, 0:C], gu[0:C, g, 0, :, 0:C],
                                         start=True, stop=True).then_inc(s[g]["rows_mm"], 1)
                        pe.wait_ge(s[g]["state_out"], c + 1)
                        product(g, 2, 0, feat(g, K), feat(g, Q), C, C)
                        product(g, 2, 1, feat(g, K), feat(g, K), C, C)
                        pe.wait_ge(s[g]["y_turned"], c + 1)
                        product(g, 3, 0, feat(g, K), P, C, P, turn=True)
                        product(g, 3, 1, feat(g, VV), P, C, P, turn=True).then_inc(s[g]["turn_mm"], 1)
                    for g in both:
                        pe.wait_ge(s[g]["n_out"], c + 1)
                        product(g, 0, 0, mat(nn, g, 1), C, C, C, turn=True).then_inc(s[g]["nt_mm"], 1)
                    for g in both:
                        pe.wait_ge(s[g]["blocks_out"], c + 1)
                        product(g, 1, 0, mat(D1, g, 1), mat(D1, g, 0), C, C)
                        product(g, 1, 1, mat(D1, g, 0), mat(D1, g, 1), C, C).then_inc(s[g]["sq_mm"], 1)
                    for g in both:
                        pe.wait_ge(s[g]["sq_out"], c + 1)
                        product(g, 2, 0, mat(D1, g, 1), mat(N2, g, 0), C, C)
                        product(g, 2, 1, mat(N2, g, 0), mat(D1, g, 1), C, C)
                        product(g, 3, 0, mat(N2, g, 1), mat(N2, g, 0), C, C).then_inc(s[g]["quad_mm"], 1)
                    for g in both:
                        pe.wait_ge(s[g]["quad_out"], 2 * c + 2)
                        product(g, 0, 0, mat(G1, g, 1), mat(N4, g, 0), C, C)
                        product(g, 0, 1, mat(N4, g, 0), mat(G1, g, 1), C, C).then_inc(s[g]["t8_mm"], 1)
                    for j in range(len(spans(C))):
                        for g in both:
                            if j:
                                pe.wait_ge(s[g]["lift_out"], 4 * c + j)
                            else:
                                pe.wait_ge(s[g]["between_out"], c + 1)
                                pe.wait_ge(s[g]["t8_out"], c + 1)
                            product(g, 1, 0, mat(between, g, j), mat(T_, g, 0), C, C).then_inc(s[g]["lt_mm"], 1)
                        for g in both:
                            pe.wait_ge(s[g]["lt_out"], 4 * c + j + 1)
                            product(g, 2, 0, mat(T_, g, 1), mat(U, g, 0), C, C)
                            product(g, 2, 1, mat(U, g, 0), mat(T_, g, 1), C, C).then_inc(s[g]["lift_mm"], 1)
                    for g in both:
                        pe.wait_ge(s[g]["lift_out"], 4 * c + len(spans(C)))
                        product(g, 3, 0, feat(g, K), S(g), C, P)
                        product(g, 3, 1, feat(g, Q), S(g), C, P).then_inc(s[g]["ks_mm"], 1)
                    for g in both:
                        pe.wait_ge(s[g]["rhs_out"], c + 1)
                        product(g, 0, 0, mat(T_, g, 1), mat(rhs, g, 0, P), C, P).then_inc(s[g]["u_mm"], 1)
                    for g in both:
                        pe.wait_ge(s[g]["u_out"], c + 1)
                        product(g, 1, 0, mat(nn, g, 0), mat(u, g, 0, P), C, P).then_inc(s[g]["o_mm"], 1)
                        product(g, 2, 0, mat(kv, g, 0, P), mat(u, g, 0, P), P, P).then_inc(s[g]["ds_mm"], 1)
                    for g in both:
                        pe.wait_ge(s[g]["y_out"], c + 2)
                        product(g, 3, 0, mat(y, g, 0, P), C, P, C, turn=True).then_inc(s[g]["y_mm"], 1)

                over_chunks(pe, chunk)



def delta_samples(nc, m, io):
    NS_ = NB * B_H
    with ExitStack() as own:
        E = own.enter_context
        sb = lambda name, shape: E(nc.sbuf_tensor("ds_" + name, shape, F32))
        S = sb("state", [P, NS_, P])
        eg, t, u = sb("eg", [P, NB, B_H]), sb("t", [P, NB, B_H]), sb("u", [P, NB, B_H])
        diag, ku = sb("diag", [P, B_H, P]), sb("ku", [P, B_H, P])
        gate, norm_g = sb("gate", [NB, 512]), sb("norm_g", [P, 1])
        o, osq, rs = sb("o", [P, NB, B_H]), sb("osq", [P, NS_]), sb("rs", [P, NS_])
        names = "in_ eg_out ks_mm own_step diag_out bcast_mm ku_out state_out o_mm osq_out sum_mm rs_out gate_mm stored"
        s = {x: m.sem("ds_" + x) for x in names.split()}
        heads = lambda f: m.mixT[:, f:f + B_H, L:T].rearrange("p h b -> p b h")
        with nc.Block() as block:
            @block.sync
            def _(sp):
                sp.dma_start(S[:], io["state_b_s"][0].rearrange("b h k v -> k (b h) v")).then_inc(s["in_"], 16)
                sp.dma_start(gate[:], m.tok[L:T, TOK_R:TOK_R + 512]).then_inc(s["in_"], 16)
                with nc.allow_non_contiguous_dma(reason="a gain vector onto partitions"):
                    sp.dma_start(norm_g[:], io["norm_b"].rearrange("o p -> p o")).then_inc(s["in_"], 16)
                sp.wait_ge(s["state_out"], NB)
                sp.dma_start(io["sb_s"][0].rearrange("b h k v -> k (b h) v"), S[:]).then_inc(s["stored"], 16)
                sp.wait_ge(s["stored"], 16)

            @block.scalar
            def _(act):
                nc.scalar.activation(eg[:], m.gates[:, NT:NT + NB, 0:4], ACT.Exp).then_inc(s["eg_out"], 1)
                act.wait_ge(s["o_mm"], 1)
                nc.scalar.copy(o[:], m.ps[:, 3, 0:NS_].rearrange("p (b h) -> p b h", h=B_H))
                nc.scalar.activation(osq[:], m.ps[:, 3, 0:NS_], ACT.Square).then_inc(s["osq_out"], 1)
                act.wait_ge(s["sum_mm"], 1)
                nc.scalar.activation(rs[:], m.ps[:, 4, 0:NS_], ACT.Sqrt, scale=1.0 / P, bias=m.eps[:, 0:1])\
                    .then_inc(s["rs_out"], 1)

            @block.tensor
            def _(pe):
                pe.wait_ge(s["in_"], 48)
                for n in range(NS_):
                    last = nc.tensor.matmul(m.ps[:, 0, n:n + 1], S[:, n, :], m.mixT[:, B_H + n % B_H, L + n // B_H:
                                                                                   L + n // B_H + 1],
                                            start=True, stop=True)
                last.then_inc(s["ks_mm"], 1)
                for h in range(B_H):
                    last = nc.tensor.transpose(m.ps[:, 5, h * NB:(h + 1) * NB], gate[:, h * P:(h + 1) * P],
                                               m.ident[0:NB, 0:NB])
                last.then_inc(s["gate_mm"], 1)
                with pe.Fori(0, NB) as b:
                    pe.wait_ge(s["diag_out"], b + 1)
                    nc.tensor.matmul(m.ps[:, 1, :].rearrange("p (h c) -> p h c", h=B_H), m.ones[:], diag[:],
                                     start=True, stop=True).then_inc(s["bcast_mm"], 1)
                pe.wait_ge(s["state_out"], NB)
                for n in range(NS_):
                    last = nc.tensor.matmul(m.ps[:, 3, n:n + 1], S[:, n, :],
                                            m.mixT[:, n % B_H, L + n // B_H:L + n // B_H + 1], start=True, stop=True)
                last.then_inc(s["o_mm"], 1)
                pe.wait_ge(s["osq_out"], 1)
                nc.tensor.matmul(m.ps[:, 4, 0:NS_], m.ones[:], osq[:], start=True, stop=True).then_inc(s["sum_mm"], 1)

            @block.vector
            def _(dve):
                steps = Steps(dve, s["own_step"])
                dve.wait_ge(s["eg_out"], 1)
                dve.wait_ge(s["ks_mm"], 1)
                steps.after(nc.vector.tensor_tensor(t[:], m.ps[:, 0, 0:NS_].rearrange("p (b h) -> p b h", h=B_H),
                                                    eg[:], ALU.mult))
                steps.after(nc.vector.tensor_tensor(t[:], heads(2 * B_H), t[:], ALU.subtract))
                steps.after(nc.vector.tensor_tensor(u[:], t[:], m.gates[:, NT:NT + NB, 4:8], ALU.mult))
                n0 = steps.n
                wide = lambda ap: ap.rearrange("p b h -> p h b").to_broadcast([P, B_H, P])
                eye = m.ident[:].rearrange("p (o c) -> p o c", o=1).to_broadcast([P, B_H, P])
                with dve.Fori(0, NB) as b:
                    steps = Steps(dve, s["own_step"], 2 * b + n0)
                    sample = S[:, bass.ds(4 * b, 4), :]
                    one = bass.ds(b, 1)
                    nc.vector.tensor_tensor(diag[:], eye, wide(u[:, one, :]), ALU.mult).then_inc(s["diag_out"], 1)
                    steps.after(nc.vector.tensor_tensor(sample, sample, wide(eg[:, one, :]), ALU.mult))
                    dve.wait_ge(s["bcast_mm"], b + 1)
                    k = m.mixT[:, B_H:2 * B_H, bass.ds(L + b, 1)].to_broadcast([P, B_H, P])
                    steps.after(nc.vector.tensor_tensor(ku[:], m.ps[:, 1, :].rearrange("p (h c) -> p h c", h=B_H), k,
                                                        ALU.mult))
                    nc.vector.tensor_tensor(sample, sample, ku[:], ALU.add).then_inc(s["state_out"], 1)
                steps = Steps(dve, s["own_step"], 2 * NB + n0)
                dve.wait_ge(s["osq_out"], 1)
                steps.after(nc.vector.tensor_scalar(o[:], o[:], norm_g[:, 0:1], None, ALU.mult))
                dve.wait_ge(s["gate_mm"], 1)
                steps.after(nc.vector.tensor_tensor(o[:], o[:], m.ps[:, 5, 0:NS_].rearrange("p (h b) -> p b h", b=NB),
                                                    ALU.mult))
                dve.wait_ge(s["rs_out"], 1)
                steps.after(nc.vector.reciprocal(rs[:], rs[:]))
                out = m.actT[:, H:H + B_H, L:T].rearrange("p h b -> p b h")
                nc.vector.tensor_tensor(out, o[:], rs[:].rearrange("p (b h) -> p b h", h=B_H), ALU.mult)



def bias_rows(nc, m, io):
    with ExitStack() as own:
        E = own.enter_context
        buckets = E(nc.sbuf_tensor("br_buckets", [33, BIAS_W], F32))
        table = E(nc.sbuf_tensor("br_table", [33, H], F32))
        farthest = E(nc.sbuf_tensor("br_far", [32, H], F32))
        rows = E(nc.sbuf_tensor("br_rows", [H, BIAS_W], F32))
        vec = E(nc.sbuf_tensor("br_vec", [P, 4, 64], F32))
        dots = E(nc.sbuf_tensor("br_dots", [P, 2], F32))
        names = "in_ table_out mm rows_out stored dots_out lam_exp step"
        s = {x: m.sem("br_" + x) for x in names.split()}
        parts = [(a, min(512, BIAS_W - a)) for a in range(0, BIAS_W, 512)]
        with nc.Block() as block:
            @block.sync
            def _(sp):
                sp.dma_start(buckets[:], io["c_buckets"]).then_inc(s["in_"], 16)
                sp.dma_start(table[0:32], io["bias_table"]).then_inc(s["in_"], 16)
                sp.dma_start(farthest[:], io["bias_table"][31:32, :].to_broadcast([32, H])).then_inc(s["in_"], 16)
                for j, v in enumerate((io["lam_q1"], io["lam_k1"], io["lam_q2"], io["lam_k2"])):
                    sp.dma_start(vec[:, j], v.to_broadcast([P, 64])).then_inc(s["in_"], 16)
                sp.wait_ge(s["rows_out"], 1)
                sp.dma_start(m.bias, rows[:]).then_inc(s["stored"], 16)
                sp.wait_ge(s["stored"], 16)

            @block.vector
            def _(dve):
                steps = Steps(dve, s["step"])
                dve.memset(table[32:33], NEG)
                dve.wait_ge(s["in_"], 112)
                nc.vector.tensor_tensor(table[0:32], table[0:32], farthest[:], ALU.subtract).then_inc(s["table_out"], 1)
                for j in range(2):
                    steps.after(nc.vector.tensor_tensor(vec[:, 2 * j], vec[:, 2 * j], vec[:, 2 * j + 1], ALU.mult))
                    last = nc.vector.tensor_reduce(dots[:, j:j + 1], vec[:, 2 * j], AX, ALU.add)
                last.then_inc(s["dots_out"], 1)
                dve.wait_ge(s["mm"], 1)
                for j, (a, n) in enumerate(parts):
                    last = nc.vector.tensor_copy(rows[:, a:a + n], m.ps[0:H, j, 0:n])
                last.then_inc(s["rows_out"], 1)
                dve.wait_ge(s["lam_exp"], 1)
                steps.after(nc.vector.tensor_tensor(m.lam[:], dots[:, 1:2], dots[:, 0:1], ALU.subtract))
                nc.vector.tensor_scalar(m.lam[:], m.lam[:], -LAM_INIT, None, ALU.add)

            @block.scalar
            def _(act):
                act.wait_ge(s["dots_out"], 1)
                nc.scalar.activation(dots[:], dots[:], ACT.Exp).then_inc(s["lam_exp"], 1)

            @block.tensor
            def _(pe):
                pe.wait_ge(s["table_out"], 1)
                for j, (a, n) in enumerate(parts):
                    last = nc.tensor.matmul(m.ps[0:H, j, 0:n], table[:], buckets[:, a:a + n], start=True, stop=True)
                last.then_inc(s["mm"], 1)


def load_kv(nc, m, tok, tag):
    with ExitStack() as own:
        E = own.enter_context
        k = E(nc.sbuf_tensor(f"{tag}_k", [P, NT, KV * P], F32))
        kv_in, turned, cleared = (m.sem(f"{tag}_{x}") for x in ("in", "turned", "cleared"))
        with nc.Block() as block:
            @block.sync
            def _(sp):
                sp.wait_ge(cleared, 1)
                for dst, c0 in ((k, TOK_K), (m.v, TOK_V)):
                    src = tok[:, c0:c0 + KV * P]
                    sp.dma_start(dst[:, 0:FULL, :], src[0:FULL * P].rearrange("(t p) c -> p t c", p=P))\
                        .then_inc(kv_in, 16)
                    sp.dma_start(dst[0:LAST, FULL, :], src[FULL * P:T]).then_inc(kv_in, 16)
                sp.wait_ge(kv_in, 64)

            @block.tensor
            def _(pe):
                pe.wait_ge(kv_in, 64)
                for g in range(KV):
                    for t in range(NT):
                        r = P if t < FULL else LAST
                        last = nc.tensor.transpose(m.ps[:, 3 * g + t // 4, t % 4 * P:t % 4 * P + r],
                                                   k[0:r, t, g * P:(g + 1) * P], m.ident[0:r, 0:r])
                last.then_inc(turned, 1)

            @block.vector
            def _(dve):
                dve.memset(m.v[:, FULL, :], 0.0).then_inc(cleared, 1)
                dve.wait_ge(turned, 1)
                for g in range(KV):
                    for j in range(3):
                        n = min(512, T - 512 * j)
                        nc.vector.tensor_copy(m.kT[:, g, 512 * j:512 * j + n], m.ps[:, 3 * g + j, 0:n])



class Plan:

    def __init__(self, t):
        self.t, self.R, self.nb, self.q0 = t, P if t < FULL else TAIL, t + 1, t * P
        self.W = self.q0 + self.R
        self.regions, self.turns, self.out = ((0, 2), (4, 5), 6) if self.W <= 1024 else ((0, 3), (6,), 7)
        self.groups = [(a, min(4, self.nb - a)) for a in range(0, self.nb, 4)]


def pipeline(first, last, stages):
    for k in range(first, last + max(lag for _, lag in stages)):
        for stage, lag in stages:
            if first <= k - lag < last:
                stage(k - lag)


def prompt_attention(nc, m, tok, diff, out_gain):
    NC = 2 if diff else 1
    TURN = 2 if diff else 1
    tag = "aa" if diff else "ac"
    NEAR = 2 * P
    with ExitStack() as own:
        E = own.enter_context
        sb = lambda name, shape: E(nc.sbuf_tensor(f"{tag}_{name}", shape, F32))
        bias = sb("bias", [P, H, NEAR])
        q = sb("q", [P, 2, NC, P])
        prob = sb("prob", [P, 2, NC, L])
        mix = sb("mix", [P, 2, L]) if diff else None
        probT = sb("probT", [P, 2, NT, P])
        mx, den, inv = sb("mx", [P, 2, NC]), sb("den", [P, 4, NC]), sb("inv", [P, 4, NC])
        ratio = sb("ratio", [P, 2]) if diff else None
        gate, o, y = sb("gate", [P, 2, D]), sb("o", [P, 2, D]), sb("y", [P, D])
        upside = o[:].rearrange("p a (h c) -> p (a h) c", c=NEAR)
        flip = sb("flip", [P, P])
        oss, rs, minus_half = sb("oss", [P, H]), sb("rs", [P, H]), sb("minus_half", [P, H])
        gain = sb("gain", [P, 1])
        names = ("bias_in bias_mm bias_out gate_in gain_in gain_out q_ready scores_mm near_out maxed exp_half "
                 "combined turned probs_out pv_mm o_out rs_out y_ready y_mm y_turned half_set step gated recip_out "
                 "ratio_out max_out")
        s = {x: m.sem(f"{tag}_{x}") for x in names.split()}

        plans = [Plan(t) for t in range(NT)]
        heads = [(p, h) for p in plans for h in range(H)]
        groups_before = [sum(len(p.groups) for p, _ in heads[:n]) for n in range(len(heads) + 1)]
        parts = [(0, FULL * H), (FULL * H, NT * H)]

        def region(n, c, w0, w1):
            p = heads[n][0]
            at = p.regions[c if diff else n % 2] * 512
            return m.ps[:].rearrange("p b c -> p (b c)")[0:p.R, at + w0:at + w1]

        def out_place(n):
            p = heads[n][0]
            return m.ps[0:p.R, p.out, 0:P]

        def turn_bank(n, k):
            p = heads[n][0]
            return p.turns[(groups_before[n] + k) % len(p.turns)]

        def at_tile_end(stage):
            return lambda n: stage(heads[n][0]) if heads[n][1] == H - 1 else None

        with nc.Block() as block:
            @block.sync
            def _(sp):
                src = bass.AP(m.bias.tensor, FULL * P - P, [[1, P], [BIAS_W, H], [1, NEAR]])
                sp.dma_start(upside, src).then_inc(s["bias_in"], 16)
                sp.dma_start(flip[:], m.flip).then_inc(s["bias_in"], 16)
                with nc.allow_non_contiguous_dma(reason="a gain vector onto partitions"):
                    if diff:
                        sp.dma_start(gain[:], out_gain.rearrange("o p -> p o")).then_inc(s["gain_in"], 16)
                for p in plans:
                    if p.t >= 2:
                        sp.wait_ge(s["y_ready"], p.t - 1)
                    if p.t >= 1:
                        sp.wait_ge(s["gate_in"], 16 * p.t)
                    sp.dma_start(gate[0:p.R, p.t % 2, :], tok[p.q0:p.q0 + p.R, TOK_G:TOK_G + D])\
                        .then_inc(s["gate_in"], 16)

            @block.gpsimd
            def _(pool):
                if diff:
                    nc.gpsimd.memset(minus_half[:], -0.5).then_inc(s["half_set"], 1)
                    pool.wait_ge(s["half_set"], 1)
                    pool.wait_ge(s["gain_in"], 16)
                    nc.gpsimd.tensor_scalar(gain[:], gain[:], 1.0 - LAM_INIT, None, ALU.mult).then_inc(s["gain_out"], 1)

                def queries(n):
                    p, h = heads[n]
                    if n >= 2:
                        pool.wait_ge(s["scores_mm"], NC * (n - 1))
                    for c in range(NC):
                        last = nc.gpsimd.tensor_tensor(q[:, n % 2, c, 0:p.R], m.qT[:, h, p.q0:p.q0 + p.R],
                                                       m.halves_wide[:, c if diff else 2, 0:p.R], ALU.mult)
                    last.then_inc(s["q_ready"], 1)

                def root(p):
                    pool.wait_ge(s["rs_out"], 2 * p.t + 1)
                    nc.gpsimd.tensor_tensor(rs[0:p.R], rs[0:p.R], minus_half[0:p.R], ALU.pow).then_inc(s["rs_out"], 1)

                for a, b in parts:
                    pipeline(a, b, [(queries, 0)] + ([(at_tile_end(root), TURN + 4)] if diff else []))

            @block.tensor
            def _(pe):
                pe.wait_ge(s["bias_in"], 32)
                for k in range(4):
                    last = nc.tensor.matmul(m.ps[:, k, :].rearrange("p (h c) -> p h c", c=NEAR), flip[:],
                                            upside[:, 2 * k:2 * k + 2, :], start=True, stop=True)
                last.then_inc(s["bias_mm"], 1)
                pe.wait_ge(s["bias_out"], 1)

                def scores(n):
                    p, h = heads[n]
                    pe.wait_ge(s["q_ready"], n + 1)
                    for c in range(NC):
                        done = NC * (n - 1) + c + 1 if diff else n - 1
                        if done >= 1:
                            pe.wait_ge(s["exp_half"], done)
                        for w in range(0, p.W, 512):
                            w1 = min(w + 512, p.W)
                            last = nc.tensor.matmul(region(n, c, w, w1), q[:, n % 2, c, 0:p.R],
                                                    m.kT[:, h // G, w:w1], start=True, stop=True)
                        last.then_inc(s["scores_mm"], 1)

                def turn(n, ks):
                    p, h = heads[n]
                    src = mix[:, n % 2] if diff else prob[:, n % 2, 0]
                    pe.wait_ge(s["combined"] if diff else s["exp_half"], n + 1)
                    for k in ks:
                        b0, bn = p.groups[k]
                        used = groups_before[n] + k + 1 - len(p.turns)
                        if used >= 1:
                            pe.wait_ge(s["probs_out"], used)
                        for b in range(b0, b0 + bn):
                            w1 = min(b * P + P, p.W)
                            last = nc.tensor.transpose(m.ps[0:w1 - b * P, turn_bank(n, k),
                                                            (b - b0) * P:(b - b0) * P + p.R],
                                                       src[0:p.R, b * P:w1], m.ident[0:p.R, 0:p.R])
                        last.then_inc(s["turned"], 1)

                def turn_first(n):
                    turn(n, range(len(heads[n][0].groups))[:2])

                def turn_rest(n):
                    if len(heads[n][0].groups) > 2:
                        turn(n, range(len(heads[n][0].groups))[2:])

                def values(n):
                    p, h = heads[n]
                    pe.wait_ge(s["probs_out"], groups_before[n + 1])
                    if n >= 1:
                        pe.wait_ge(s["o_out"], n)
                    for b in range(p.nb):
                        last = nc.tensor.matmul(out_place(n), probT[:, n % 2, b, 0:p.R],
                                                m.v[:, b, h // G * P:h // G * P + P], start=(b == 0),
                                                stop=(b == p.nb - 1))
                    last.then_inc(s["pv_mm"], 1)

                def turn_out(half):
                    def stage(p):
                        pe.wait_ge(s["y_ready"], p.t + 1)
                        if 2 * p.t + half >= 1:
                            pe.wait_ge(s["y_turned"], 2 * p.t + half)
                        for h in range(4):
                            last = nc.tensor.transpose(m.ps[:, 7, h * P:h * P + p.R],
                                                       y[0:p.R, (4 * half + h) * P:(4 * half + h + 1) * P],
                                                       m.ident[0:p.R, 0:p.R])
                        last.then_inc(s["y_mm"], 1)
                    return at_tile_end(stage)

                for a, b in parts:
                    if a:
                        pe.wait_ge(s["o_out"], a)
                        pe.wait_ge(s["y_turned"], 2 * a // H)
                    pipeline(a, b, [(scores, 0), (turn_first, TURN), (values, TURN + 1), (turn_rest, TURN),
                                    (turn_out(0), TURN + 5), (turn_out(1), TURN + 6)])

            @block.scalar
            def _(act):
                def exps(n):
                    p, h = heads[n]
                    for c in range(NC):
                        act.wait_ge(s["maxed"], NC * n + c + 1)
                        if n >= 2 and diff:
                            act.wait_ge(s["combined"], n - 1)
                        elif n >= 2:
                            act.wait_ge(s["turned"], groups_before[n - 1])
                        dst = prob[0:p.R, n % 2, c, 0:p.W]
                        src = region(n, c, 0, p.W) if diff or p.t < 2 else dst
                        nc.scalar.activation(dst, src, ACT.Exp, bias=mx[0:p.R, n % 2, c:c + 1],
                                             accum_out=den[0:p.R, n % 4, c:c + 1]).then_inc(s["exp_half"], 1)

                def copy_turned(n):
                    p, h = heads[n]
                    for k, (b0, bn) in enumerate(p.groups):
                        act.wait_ge(s["turned"], groups_before[n] + k + 1)
                        if k == 0 and n >= 2:
                            act.wait_ge(s["pv_mm"], n - 1)
                        bank = turn_bank(n, k)
                        whole = bn if (b0 + bn) * P <= p.W else bn - 1
                        if whole:
                            last = nc.scalar.copy(
                                probT[:, n % 2, b0:b0 + whole, 0:p.R],
                                m.ps[:, bank, 0:whole * P].rearrange("p (b c) -> p b c", c=P)[:, :, 0:p.R])
                        if whole < bn:
                            K = p.W - (b0 + whole) * P
                            last = nc.scalar.copy(probT[0:K, n % 2, b0 + whole, 0:p.R],
                                                  m.ps[0:K, bank, whole * P:whole * P + p.R])
                        last.then_inc(s["probs_out"], 1)

                def output(n):
                    p, h = heads[n]
                    act.wait_ge(s["pv_mm"], n + 1)
                    dst = o[0:p.R, p.t % 2, h * P:h * P + P]
                    act.wait_ge(s["recip_out"], n + 1)
                    nc.scalar.activation(dst, out_place(n), ACT.Copy,
                                         scale=inv[0:p.R, n % 4, 0:1]).then_inc(s["o_out"], 1)

                def to_features(half):
                    def stage(p):
                        act.wait_ge(s["y_mm"], 2 * p.t + half + 1)
                        src = m.ps[:, 7, :].rearrange("p (h c) -> p h c", c=P)[:, :, 0:p.R]
                        dst = m.actT[:, 4 * half:4 * half + 4, p.q0:p.q0 + p.R]
                        if diff:
                            last = nc.scalar.activation(dst, src, ACT.Copy, scale=gain[:, 0:1])
                        else:
                            last = nc.scalar.copy(dst, src)
                        last.then_inc(s["y_turned"], 1)
                    return at_tile_end(stage)

                if diff:
                    act.wait_ge(s["gain_out"], 1)
                for a, b in parts:
                    pipeline(a, b, [(exps, 0), (copy_turned, TURN), (output, TURN + 1), (to_features(0), TURN + 5),
                                    (to_features(1), TURN + 6)])

            @block.vector
            def _(dve):
                dve.memset(probT[:, :, FULL, :], 0.0)
                dve.wait_ge(s["bias_mm"], 1)
                nc.vector.tensor_copy(bias[:], m.ps[:, 0:4, :].rearrange("p k (h c) -> p (k h) c", c=NEAR))\
                    .then_inc(s["bias_out"], 1)
                dve.wait_ge(s["bias_out"], 1)

                def maxima(n):
                    p, h = heads[n]
                    for c in range(NC):
                        dve.wait_ge(s["scores_mm"], NC * n + c + 1)
                        near = max(0, p.q0 - P)
                        part = region(n, c, near, p.W)
                        at = near - p.q0 + P
                        nc.vector.tensor_tensor(part, part, bias[0:p.R, h, at:at + p.W - near], ALU.add)\
                            .then_inc(s["near_out"], 1)
                        dve.wait_ge(s["near_out"], NC * n + c + 1)
                        if n >= 2 and c == 0:
                            dve.wait_ge(s["exp_half"], NC * (n - 1))
                        src = region(n, c, 0, p.W)
                        m1 = mx[0:p.R, n % 2, c:c + 1]
                        if diff or p.t < 2:
                            ins = nc.vector.tensor_reduce(m1, src, AX, ALU.max)
                        else:
                            dve.wait_ge(s["turned"], groups_before[n - 1])
                            ins = nc.vector.tensor_tensor_reduce(out=prob[0:p.R, n % 2, c, 0:p.W], in0=src,
                                                                 in1=m.chosen[p.t][0:p.R, 0:p.W], scale=1.0,
                                                                 scalar=-3e38, op0=ALU.add, op1=ALU.max,
                                                                 accum_out=m1)
                        ins.then_inc(s["max_out"], 1)
                        dve.wait_ge(s["max_out"], NC * n + c + 1)
                        nc.vector.tensor_scalar(m1, m1, -1.0, None, ALU.mult).then_inc(s["maxed"], 1)

                def combine(n):
                    p, h = heads[n]
                    dve.wait_ge(s["exp_half"], NC * (n + 1))
                    nc.vector.reciprocal(inv[0:p.R, n % 4, :], den[0:p.R, n % 4, :]).then_inc(s["recip_out"], 1)
                    if not diff:
                        return
                    dve.wait_ge(s["recip_out"], n + 1)
                    r = ratio[0:p.R, n % 2:n % 2 + 1]
                    nc.vector.scalar_tensor_tensor(out=r, in0=inv[0:p.R, n % 4, 1:2], scalar=m.lam[0:p.R, 0:1],
                                                   in1=den[0:p.R, n % 4, 0:1], op0=ALU.mult, op1=ALU.mult)\
                        .then_inc(s["ratio_out"], 1)
                    dve.wait_ge(s["ratio_out"], n + 1)
                    if n >= 2:
                        dve.wait_ge(s["turned"], groups_before[n - 1])
                    nc.vector.scalar_tensor_tensor(out=mix[0:p.R, n % 2, 0:p.W], in0=prob[0:p.R, n % 2, 1, 0:p.W],
                                                   scalar=r, in1=prob[0:p.R, n % 2, 0, 0:p.W], op0=ALU.mult,
                                                   op1=ALU.add).then_inc(s["combined"], 1)

                def gated(p):
                    R, w = p.R, (slice(0, p.R), p.t % 2)
                    dve.wait_ge(s["o_out"], H * (p.t + 1))
                    dve.wait_ge(s["gate_in"], 16 * p.t + 16)
                    if p.t >= 1:
                        dve.wait_ge(s["y_mm"], 2 * p.t)
                    if not diff:
                        nc.vector.tensor_tensor(y[0:R], o[w], gate[w], ALU.mult).then_inc(s["y_ready"], 1)
                        return
                    steps = Steps(dve, s["step"], 2 * p.t)
                    steps.after(nc.vector.tensor_tensor(y[0:R], o[w], o[w], ALU.mult))
                    steps.after(nc.vector.tensor_reduce(oss[0:R], y[0:R].rearrange("p (h d) -> p h d", d=P), AX,
                                                        ALU.add))
                    nc.vector.tensor_scalar(rs[0:R], oss[0:R], 1.0 / P, EPS, ALU.mult, ALU.add)\
                        .then_inc(s["rs_out"], 1)
                    nc.vector.tensor_tensor(y[0:R], o[w], gate[w], ALU.mult).then_inc(s["gated"], 1)

                def normed(p):
                    dve.wait_ge(s["rs_out"], 2 * p.t + 2)
                    dve.wait_ge(s["gated"], p.t + 1)
                    y3 = y[0:p.R].rearrange("p (h d) -> p h d", d=P)
                    r3 = rs[0:p.R].rearrange("p (h o) -> p h o", o=1).to_broadcast([p.R, H, P])
                    nc.vector.tensor_tensor(y3, y3, r3, ALU.mult).then_inc(s["y_ready"], 1)

                for a, b in parts:
                    pipeline(a, b, [(maxima, 0), (combine, 1), (at_tile_end(gated), TURN + 2)]
                             + ([(at_tile_end(normed), TURN + 4)] if diff else []))





def sample_attention(nc, m, io, tok, diff, cache_k, cache_v, out_gain):
    NC = 2 if diff else 1
    RB = H * NC
    RG = G * NC
    R = NB * RB
    NO = NB * H
    QP = 4
    N_SAMPLES = NB * (N_PAGES // QP)
    tag = "sa" if diff else "sc"
    with ExitStack() as own:
        E = own.enter_context
        sb = lambda name, shape: E(nc.sbuf_tensor(f"{tag}_{name}", shape, F32))
        qz = sb("qz", [P, NB * KV, R])
        ring = 4
        kpages = sb("kpages", [P, ring, QP, KV * P])
        kTs = sb("kTs", [P, KV, QP * P])
        vpages = sb("vpages", [P, 2, N_PAGES, KV * P])
        vnew, gate = sb("vnew", [NB, KV * P]), sb("gate", [NB, D])
        sel_b, sel_h, own_mask = sb("sel_b", [NB, R]), sb("sel_h", [H, R]), sb("own_mask", [NB, NB])
        near = sb("near", [H, PAGE + 1])
        prob = sb("prob", [R, PAST + NB])
        probT, newT = sb("probT", [P, N_PAGES, NO]), sb("newT", [NB, NO])
        mx, den, parity = sb("mx", [R, 2]), sb("den", [R, 2]), sb("parity", [R, 2])
        o, osq, rs = sb("o", [P, NO]), sb("osq", [P, NO]), sb("rs", [P, NO])
        gain = sb("gain", [P, 1])
        names = ("small_in zeroed q_out turned_a turned_d k_act k_dve scores_mm last_mm maxed step exped scaled pt_mm "
                 "pt_out pv_mm pv_b osq_out sum_mm rs_out gate_mm o_out")
        s = {x: m.sem(f"{tag}_{x}") for x in names.split()}
        k_in = [m.sem(f"{tag}_k_in{j}") for j in range(ring)]
        v_in = [m.sem(f"{tag}_v_in{j}") for j in range(2)]
        ck = cache_k.rearrange("n t a b c -> n t (a b c)") if diff else cache_k.rearrange("n t a b -> n t (a b)")
        cv = cache_v.rearrange("n t a b -> n t (a b)")
        N_PT = N_PAGES // QP
        n_small = 7 + (1 if diff else 0)

        def page(eng, dst, cache, index, sem):
            at = eng.value_load(m.pages[0:1, bass.ds(index, 1)], min_val=0, max_val=cache.shape[0] - 1)
            eng.dma_start(dst, cache[bass.ds(at, 1), :, :].rearrange("o t c -> t (o c)")).then_inc(sem, 16)

        def load_keys(eng, kq, b, js):
            for j in js:
                page(eng, kpages[:, b % ring, j, :], ck, kq * QP + (b * N_PAGES + j), k_in[b % ring])

        def load_values(eng, i, b, js):
            for j in js:
                page(eng, vpages[:, b, j, :], cv, i * (2 * N_PAGES) + (b * N_PAGES + j), v_in[b])

        SP_K, ACT_K = range(QP // 2), range(QP // 2, QP)
        SP_V, ACT_V = range(N_PAGES // 2), range(N_PAGES // 2, N_PAGES)

        with nc.Block() as block:
            @block.sync
            def _(sp):
                sp.dma_start(sel_b[:], io["c_sel_b2"] if diff else io["c_sel_b1"]).then_inc(s["small_in"], 16)
                sp.dma_start(sel_h[:], io["c_sel_h2"] if diff else io["c_sel_h1"]).then_inc(s["small_in"], 16)
                sp.dma_start(own_mask[:], io["c_own_mask"]).then_inc(s["small_in"], 16)
                sp.dma_start(parity[:], io["c_parity"][0:R]).then_inc(s["small_in"], 16)
                sp.dma_start(near[:], m.bias[:, FAR - PAGE:FAR + 1]).then_inc(s["small_in"], 16)
                sp.dma_start(vnew[:], tok[L:T, TOK_V:TOK_V + KV * P]).then_inc(s["small_in"], 16)
                sp.dma_start(gate[:], tok[L:T, TOK_G:TOK_G + D]).then_inc(s["small_in"], 16)
                if diff:
                    with nc.allow_non_contiguous_dma(reason="a gain vector onto partitions"):
                        sp.dma_start(gain[:], out_gain.rearrange("o p -> p o")).then_inc(s["small_in"], 16)
                with sp.Fori(0, N_PAGES // QP) as kq:
                    for b in range(NB):
                        sp.wait_ge(s["turned_d"], kq * NB + b + 1)
                        alone(sp, m)
                        load_keys(sp, kq, b, SP_K)
                with sp.Fori(0, NB // 2) as i:
                    for b in range(2):
                        sp.wait_ge(s["pv_b"], 2 * i + b + 1)
                        alone(sp, m)
                        load_values(sp, i, b, SP_V)

            @block.tensor
            def _(pe):
                pe.sem_inc(s["turned_d"], ring)
                pe.sem_inc(s["pv_b"], 2)
                pe.wait_ge(s["q_out"], 1)
                pe.wait_ge(s["small_in"], 16 * n_small)
                with pe.Fori(0, N_PAGES // QP) as kq:
                    def turn(b, g):
                        if g == 0:
                            pe.wait_ge(k_in[b % ring], (kq * (NB // ring) + b // ring) * (16 * QP) + 16 * QP)
                        pe.wait_ge(s["k_act"] if g == 0 else s["k_dve"], kq * NB + b + 1)
                        for j in range(QP):
                            last = nc.tensor.transpose(m.ps[:, 4 + g, j * P:(j + 1) * P],
                                                       kpages[:, b % ring, j, g * P:(g + 1) * P], m.ident[:])
                        last.then_inc(s["turned_a"] if g == 0 else s["turned_d"], 1)

                    def product(b, g):
                        pe.wait_ge(s["k_act"] if g == 0 else s["k_dve"], kq * NB + b + 2)
                        alone(pe, m)
                        last = nc.tensor.matmul(m.ps[0:R, bass.ds(kq, 1), :], qz[:, 2 * b + g, :], kTs[:, g, :],
                                                start=(b == 0 and g == 0), stop=(b == NB - 1 and g == KV - 1))
                        last.then_inc(s["scores_mm"], 1)

                    turn(0, 0)
                    for b in range(NB):
                        turn(b, 1)
                        product(b, 0)
                        if b < NB - 1:
                            turn(b + 1, 0)
                        product(b, 1)
                extra = dict(stop=True, skip_group_check=True)
                nc.tensor.matmul(m.ps[0:R, 3, 512 - PAGE:512], sel_h[:], near[:, 0:PAGE], start=False, **extra)
                if not diff:
                    for j in range(4):
                        nc.tensor.matmul(m.ps[0:R, j, :], sel_b[:], m.chosen_s[:, 512 * j:512 * j + 512],
                                         start=False, **extra)
                    nc.tensor.matmul(m.ps[0:R, 6, 0:NB], sel_b[:], m.chosen_s[:, PAST:PAST + NB], start=True,
                                     stop=False)
                else:
                    nc.tensor.matmul(m.ps[0:R, 6, 0:NB], sel_b[:], own_mask[:], start=True, stop=False)
                nc.tensor.matmul(m.ps[0:R, 6, 0:NB], sel_h[:], near[:, PAGE:PAGE + 1].to_broadcast([H, NB]),
                                 start=False, stop=False)
                for n in range(NB * KV):
                    last = nc.tensor.matmul(m.ps[0:R, 6, 0:NB], qz[:, n, :], m.kT[:, n % KV, L:T], start=False,
                                            stop=(n == NB * KV - 1))
                last.then_inc(s["last_mm"], 1)
                for h in range(H):
                    last = nc.tensor.transpose(m.ps[:, 7, 64 + h * NB:64 + h * NB + NB], gate[:, h * P:(h + 1) * P],
                                               m.ident[0:NB, 0:NB])
                last.then_inc(s["gate_mm"], 1)
                pe.wait_ge(s["scaled"], 1)
                pe.wait_ge(s["k_act"], 4 * NB + 1)
                pe.wait_ge(s["k_dve"], 4 * NB + 1)
                for j in range(N_PT):
                    if j >= 2:
                        pe.wait_ge(s["pt_out"], j - 1)
                    for b in range(QP):
                        last = nc.tensor.transpose(m.ps[:, 4 + j % 2, b * R:(b + 1) * R],
                                                   prob[:, (QP * j + b) * P:(QP * j + b + 1) * P], m.ident[0:R, 0:R])
                    last.then_inc(s["pt_mm"], 1)
                nc.tensor.transpose(m.ps[0:NB, 6, 0:R], prob[:, PAST:PAST + NB], m.ident[0:R, 0:R]).then_inc(s["pt_mm"], 1)
                pe.wait_ge(s["pt_out"], N_PT + 1)
                with pe.Fori(0, NB // 2) as i:
                    for b in range(2):
                        pe.wait_ge(v_in[b], i * (16 * N_PAGES) + 16 * N_PAGES)
                        alone(pe, m)
                        for g in range(KV):
                            cols = bass.ds(i * (2 * H) + (b * H + g * G), G)
                            for j in range(N_PAGES):
                                nc.tensor.matmul(m.ps[:, 0, cols], vpages[:, b, j, g * P:(g + 1) * P],
                                                 probT[:, j, cols], start=(j == 0), stop=False)
                            last = nc.tensor.matmul(m.ps[:, 0, cols], vnew[:, g * P:(g + 1) * P], newT[:, cols],
                                                    start=False, stop=True)
                        last.then_inc(s["pv_b"], 1)
                if diff:
                    pe.wait_ge(s["osq_out"], 1)
                    nc.tensor.matmul(m.ps[:, 1, 0:NO], m.ones[:], osq[:], start=True, stop=True).then_inc(s["sum_mm"], 1)

            @block.scalar
            def _(act):
                act.sem_inc(s["k_act"], 1)
                AHEAD = ring - 1
                for n in range(-AHEAD, N_SAMPLES):
                    if n + AHEAD < N_SAMPLES:
                        act.wait_ge(s["turned_d"], n + AHEAD + 1)
                        load_keys(act, (n + AHEAD) // NB, (n + AHEAD) % NB, ACT_K)
                    if n >= 0:
                        act.wait_ge(s["turned_a"], n + 1)
                        act.wait_ge(s["scores_mm"], 2 * n + 1)
                        nc.scalar.copy(kTs[:, 0, :], m.ps[:, 4, :]).then_inc(s["k_act"], 1)
                for b in range(2):
                    act.wait_ge(s["pv_b"], b + 1)
                    load_values(act, 0, b, ACT_V)
                act.wait_ge(s["maxed"], 1)
                keys = m.ps[0:R, 0:4, :].rearrange("p a b -> p (a b)")
                nc.scalar.activation(prob[:, 0:PAST], keys, ACT.Exp, bias=mx[:, 0:1], accum_out=den[:, 0:1])
                nc.scalar.activation(prob[:, PAST:], m.ps[0:R, 6, 0:NB], ACT.Exp, bias=mx[:, 0:1],
                                     accum_out=den[:, 1:2]).then_inc(s["exped"], 1)
                with act.Fori(1, NB // 2) as i:
                    for b in range(2):
                        act.wait_ge(s["pv_b"], 2 * i + b + 1)
                        alone(act, m)
                        load_values(act, i, b, ACT_V)
                act.wait_ge(s["pv_b"], NB + 2)
                nc.scalar.copy(o[:], m.ps[:, 0, 0:NO])
                nc.scalar.activation(osq[:], m.ps[:, 0, 0:NO], ACT.Square).then_inc(s["osq_out"], 1)
                if diff:
                    act.wait_ge(s["sum_mm"], 1)
                    nc.scalar.activation(rs[:], m.ps[:, 1, 0:NO], ACT.Sqrt, scale=1.0 / P, bias=m.eps[:, 0:1])\
                        .then_inc(s["rs_out"], 1)

            @block.vector
            def _(dve):
                dve.sem_inc(s["k_dve"], 1)
                dve.sem_inc(s["scores_mm"], 2)
                dve.memset(qz[:], 0.0).then_inc(s["zeroed"], 1)
                dve.wait_ge(s["zeroed"], 1)
                for b in range(NB):
                    for g in range(KV):
                        n = KV * b + g
                        for c in range(NC):
                            out = qz[:, n, RG * n:RG * n + RG].rearrange("p (h c) -> p h c", c=NC)[:, :, c]
                            src = m.qT[:, G * g:G * g + G, L + b]
                            last = nc.vector.tensor_scalar(out, src, m.halves[:, c:c + 1] if diff else float(P) ** -0.5,
                                                           None, ALU.mult)
                last.then_inc(s["q_out"], 1)
                with dve.Fori(0, N_PAGES // QP) as kq:
                    for b in range(NB):
                        dve.wait_ge(s["turned_d"], kq * NB + b + ring + 1)
                        dve.wait_ge(s["scores_mm"], kq * (2 * NB) + (2 * b + 2))
                        nc.vector.tensor_copy(kTs[:, 1, :], m.ps[:, 5, :]).then_inc(s["k_dve"], 1)
                steps = Steps(dve, s["step"])
                dve.wait_ge(s["last_mm"], 1)
                keys = m.ps[0:R, 0:4, :].rearrange("p a b -> p (a b)")
                nc.vector.tensor_reduce(mx[:, 0:1], keys, AX, ALU.max)
                steps.after(nc.vector.tensor_reduce(mx[:, 1:2], m.ps[0:R, 6, 0:NB], AX, ALU.max))
                nc.vector.tensor_scalar(mx[:, 0:1], mx[:, 0:1], mx[:, 1:2], -1.0, ALU.max, ALU.mult).then_inc(s["maxed"], 1)
                dve.wait_ge(s["exped"], 1)
                steps.after(nc.vector.tensor_tensor(den[:, 0:1], den[:, 0:1], den[:, 1:2], ALU.add))
                steps.after(nc.vector.reciprocal(den[:, 0:1], den[:, 0:1]))
                if diff:
                    steps.after(nc.vector.scalar_tensor_tensor(out=parity[:, 0:1], in0=parity[:, 1:2],
                                                               scalar=m.lam[:, 0:1], in1=parity[:, 0:1],
                                                               op0=ALU.mult, op1=ALU.add))
                    steps.after(nc.vector.tensor_tensor(den[:, 0:1], den[:, 0:1], parity[:, 0:1], ALU.mult))
                nc.vector.tensor_scalar(prob[:], prob[:], den[:, 0:1], None, ALU.mult).then_inc(s["scaled"], 1)

                def turned(dst, src):
                    if diff:
                        return nc.vector.tensor_reduce(dst, src.rearrange("p a (n c) -> p a n c", c=2), AX, ALU.add)
                    return nc.vector.tensor_copy(dst, src)

                for j in range(N_PT):
                    dve.wait_ge(s["pt_mm"], j + 1)
                    turned(probT[:, QP * j:QP * j + QP, :],
                           m.ps[:, 4 + j % 2, 0:QP * R].rearrange("p (a r) -> p a r", r=R)).then_inc(s["pt_out"], 1)
                dve.wait_ge(s["pt_mm"], N_PT + 1)
                turned(newT[:].rearrange("p (a n) -> p a n", a=1),
                       m.ps[0:NB, 6, 0:R].rearrange("p (a r) -> p a r", a=1)).then_inc(s["pt_out"], 1)
                dve.wait_ge(s["osq_out"], 1)
                dve.wait_ge(s["gate_mm"], 1)
                gates = m.ps[:, 7, 64:64 + NO].rearrange("p (h b) -> p b h", b=NB)
                o3 = o[:].rearrange("p (b h) -> p b h", h=H)
                out = m.actT[:, 0:H, L:T].rearrange("p h b -> p b h")
                if not diff:
                    nc.vector.tensor_tensor(out, o3, gates, ALU.mult)
                else:
                    steps.after(nc.vector.tensor_tensor(o3, o3, gates, ALU.mult))
                    steps.after(nc.vector.tensor_scalar(o[:], o[:], gain[:, 0:1], 1.0 - LAM_INIT, ALU.mult, ALU.mult))
                    dve.wait_ge(s["rs_out"], 1)
                    steps.after(nc.vector.reciprocal(rs[:], rs[:]))
                    nc.vector.tensor_tensor(out, o3, rs[:].rearrange("p (b h) -> p b h", h=H), ALU.mult)



def project_out(nc, m, w, chunks, tag):
    with ExitStack() as own:
        E = own.enter_context
        wt = E(nc.sbuf_tensor(f"{tag}_w", [P, chunks, D], F32))
        rows = E(nc.sbuf_tensor(f"{tag}_rows", [P, 2, chunks, P], F32))
        rows_ready, product, added = (m.sem(f"{tag}_{x}") for x in ("rows", "product", "added"))
        w_in = [[m.sem(f"{tag}_w_in{j}{k}") for k in range(2)] for j in range(2)]
        half = chunks // 2
        with nc.Block() as block:
            @block.sync
            def _(sp):
                for j in range(2):
                    for k in range(2):
                        quarter = slice(half * k, half * k + half), slice(512 * j, 512 * j + 512)
                        sp.dma_start(wt[:, quarter[0], quarter[1]],
                                     w.rearrange("(c p) n -> p c n", p=P)[:, quarter[0], quarter[1]])\
                            .then_inc(w_in[j][k], 16)

            @block.scalar
            def _(act):
                act.sem_inc(product, 4)

                def tile(t, turn, slot, r):
                    act.wait_ge(product, 2 * t + 2)
                    nc.scalar.copy(rows[:, slot, :, 0:r], m.actT[:, 0:chunks, bass.ds(t * P, r)])\
                        .then_inc(rows_ready, 1)

                over_tiles(act, tile)

            @block.tensor
            def _(pe):
                def tile(t, turn, slot, r):
                    pe.wait_ge(rows_ready, t + 1)
                    pe.wait_ge(added, t + 1)
                    for j in range(2):
                        for c in range(chunks):
                            if c % half == 0:
                                pe.wait_ge(w_in[j][c // half], 16)
                            last = nc.tensor.matmul(m.ps[0:r, 2 * slot + j, :], rows[:, slot, c, 0:r],
                                                    wt[:, c, j * 512:(j + 1) * 512], start=(c == 0),
                                                    stop=(c == chunks - 1))
                        last.then_inc(product, 1)

                over_tiles(pe, tile)

            @block.vector
            def _(dve):
                dve.sem_inc(added, 2)

                def tile(t, turn, slot, r):
                    dve.wait_ge(product, 2 * t + 6)
                    h = m.h[0:r, bass.ds(t, 1), :].rearrange("p o (a b) -> p (o a) b", b=512)
                    nc.vector.tensor_tensor(h, h, m.ps[0:r, 2 * slot:2 * slot + 2, :], ALU.add).then_inc(added, 1)

                over_tiles(dve, tile)


def move_rows(nc, m, tag, save):
    moved = m.sem(tag)
    with nc.Block() as block:
        @block.sync
        def _(sp):
            full = m.h_dram[0:FULL * P, :].rearrange("(t p) d -> p t d", p=P)
            pairs = [(full, m.h[:, 0:FULL, :]), (m.h_dram[FULL * P:T, :], m.h[0:LAST, FULL, :])]
            for dram, sbuf in pairs:
                sp.dma_start(*((dram, sbuf) if save else (sbuf, dram))).then_inc(moved, 16)
            sp.wait_ge(moved, 32)


def store_kv(nc, m, tok, outs):
    with nc.Block() as block:
        @block.sync
        def _(sp):
            for out, r0, r1, c0, c1 in outs:
                sp.dma_start(out, tok[r0:r1, c0:c1]).then_inc(m.s_out, 16)
                m.n_out += 1



def index_prompt(nc, m):
    with ExitStack() as own:
        E = own.enter_context
        k2 = E(nc.sbuf_tensor("ix_k2", [P, NT, P], F32))
        q = E(nc.sbuf_tensor("ix_q", [P, 2, P], F32))
        w = E(nc.sbuf_tensor("ix_w", [P, NT, 8], F32))
        r = E(nc.sbuf_tensor("ix_relu", [P, 2, L], F32))
        causal = E(nc.sbuf_tensor("ix_causal", [P, P], F32))
        names = "k_in w_in turned copied q_ready dots relued w_scaled summed step cleared"
        s = {x: m.sem("ix_" + x) for x in names.split()}
        tiles = [t for t in range(NT) if t * P >= TOPK]
        HI = 8

        def shape(t):
            R = P if t < FULL else TAIL
            return R, t * P + R

        def over_heads(eng, k, part):
            with eng.Fori(0, HI // 2) as a:
                for parity in range(2):
                    part(a, parity, k * HI + 2 * a + parity)

        with nc.Block() as block:
            @block.sync
            def _(sp):
                for half in range(2):
                    dst = slice(64 * half, 64 * half + 64)
                    src = m.tok1[:, TOK_R:TOK_R + 64]
                    sp.dma_start(k2[:, 0:FULL, dst], src[0:FULL * P].rearrange("(t p) c -> p t c", p=P))\
                        .then_inc(s["k_in"], 16)
                    sp.dma_start(k2[0:LAST, FULL, dst], src[FULL * P:T]).then_inc(s["k_in"], 16)
                src = m.tok1[:, TOK_R + 64:TOK_R + 72]
                sp.dma_start(w[:, 0:FULL, :], src[0:FULL * P].rearrange("(t p) c -> p t c", p=P)).then_inc(s["w_in"], 16)
                sp.dma_start(w[0:TAIL, FULL, :], src[FULL * P:L]).then_inc(s["w_in"], 16)
                sp.dma_start(causal[:], m.causal).then_inc(s["w_in"], 16)

            @block.gpsimd
            def _(pool):
                for k, t in enumerate(tiles):
                    R, W = shape(t)

                    def head(a, parity, n):
                        pool.wait_ge(s["dots"], n + 1)
                        alone(pool, m)
                        nc.gpsimd.tensor_tensor(q[:, parity, 0:R], m.qiT[:, bass.ds(a, 1), t * P:t * P + R],
                                                m.halves_wide[:, parity, 0:R], ALU.mult).then_inc(s["q_ready"], 1)

                    over_heads(pool, k, head)

            @block.tensor
            def _(pe):
                pe.sem_inc(s["dots"], 2)
                pe.wait_ge(s["k_in"], 64)
                for t in range(NT):
                    n = P if t < FULL else LAST
                    last = nc.tensor.transpose(m.ps[:, t // 4, t % 4 * P:t % 4 * P + n], k2[0:n, t, :],
                                               m.ident[0:n, 0:n])
                last.then_inc(s["turned"], 1)
                pe.wait_ge(s["copied"], 1)
                for k, t in enumerate(tiles):
                    R, W = shape(t)

                    def head(a, parity, n):
                        pe.wait_ge(s["q_ready"], n + 1)
                        pe.wait_ge(s["relued"], n + 1)
                        alone(pe, m)
                        for c in range(0, W, 512):
                            c1 = min(c + 512, W)
                            last = nc.tensor.matmul(m.ps[0:R, 3 * parity + c // 512, 0:c1 - c], q[:, parity, 0:R],
                                                    m.kiT[:, c:c1], start=True, stop=True)
                        last.then_inc(s["dots"], 1)

                    over_heads(pe, k, head)

            @block.scalar
            def _(act):
                act.wait_ge(s["turned"], 1)
                nc.scalar.copy(m.kiT[:], m.ps[:, 0:3, :].rearrange("p a b -> p (a b)")[:, 0:T]).then_inc(s["copied"], 1)
                act.sem_inc(s["relued"], 2)
                for k, t in enumerate(tiles):
                    R, W = shape(t)

                    def head(a, parity, n):
                        act.wait_ge(s["dots"], n + 3)
                        act.wait_ge(s["summed"], n + 1)
                        src = m.ps[0:R, 3 * parity:3 * parity + 3, :].rearrange("p a b -> p (a b)")[:, 0:W]
                        nc.scalar.activation(r[0:R, parity, 0:W], src, ACT.Relu).then_inc(s["relued"], 1)

                    over_heads(act, k, head)

            @block.vector
            def _(dve):
                for t in tiles:
                    R, W = shape(t)
                    last = dve.memset(m.chosen[t][0:R, :], 0.0)
                last.then_inc(s["cleared"], 1)
                dve.wait_ge(s["cleared"], 1)
                for k, t in enumerate(tiles):
                    R, W = shape(t)
                    d = m.chosen[t][0:R, W - R:W]
                    if k == 0:
                        dve.wait_ge(s["w_in"], 48)
                        nc.vector.tensor_scalar(w[:, 0:FULL], w[:, 0:FULL], float(HI) ** -0.5, None, ALU.mult)
                        nc.vector.tensor_scalar(w[0:TAIL, FULL], w[0:TAIL, FULL], float(HI) ** -0.5, None, ALU.mult)\
                            .then_inc(s["w_scaled"], 1)
                        dve.wait_ge(s["w_scaled"], 1)
                    nc.vector.tensor_tensor(d, d, causal[0:R, 0:R], ALU.add).then_inc(s["step"], 1)
                dve.wait_ge(s["step"], len(tiles))
                dve.sem_inc(s["summed"], 2)
                for k, t in enumerate(tiles):
                    R, W = shape(t)

                    def head(a, parity, n):
                        dve.wait_ge(s["relued"], n + 3)
                        nc.vector.scalar_tensor_tensor(out=m.chosen[t][0:R, :], in0=r[0:R, parity, 0:W],
                                                       scalar=w[0:R, t, bass.ds(2 * a + parity, 1)],
                                                       in1=m.chosen[t][0:R, :], op0=ALU.mult, op1=ALU.add)\
                            .then_inc(s["summed"], 1)
                        dve.wait_ge(s["summed"], n + 3)

                    over_heads(dve, k, head)


def index_samples(nc, m, io):
    HP = N_PAGES // 2
    with ExitStack() as own:
        E = own.enter_context
        sb = lambda name, shape: E(nc.sbuf_tensor("is_" + name, shape, F32))
        qz = sb("qz", [P, NB, 2, 8])
        RING = 4
        kp = sb("pages", [P, RING, HP, 2, 64])
        kT = sb("kT", [P, 2, HP * P])
        relu = sb("relu", [8, 2, PAST + NB])
        wi, wT, wz, eye = sb("wi", [NB, 8]), sb("wT", [8, NB]), sb("wz", [8, NB, NB]), sb("eye", [8, NB, NB])
        own_mask = sb("own", [NB, NB])
        names = "zeroed q_in w_in w_mm w_out wz_out turned kT_out dots relued summed"
        s = {x: m.sem("is_" + x) for x in names.split()}
        k_in = [m.sem(f"is_k_in{j}") for j in range(RING)]
        ci = io["cache_c_idx"][0]

        def load_keys(eng, b, pages):
            if b >= RING:
                eng.wait_ge(s["turned"], 2 * (b - RING) + 2)
            for j in pages:
                at = eng.value_load(m.pages[0:1, b * N_PAGES + j:b * N_PAGES + j + 1], min_val=0,
                                    max_val=ci.shape[0] - 1)
                eng.dma_start(kp[:, b % RING, j % HP, j // HP, :],
                              ci[bass.ds(at, 1), :, :].rearrange("o t c -> t (o c)")).then_inc(k_in[b % RING], 16)

        SP_PAGES, ACT_PAGES = range(HP), range(HP, N_PAGES)
        with nc.Block() as block:
            @block.sync
            def _(sp):
                for b in range(2):
                    load_keys(sp, b, SP_PAGES)
                sp.wait_ge(s["zeroed"], 1)
                with nc.allow_non_contiguous_dma(reason="query columns to other partitions"):
                    for half in range(2):
                        for parity in range(2):
                            for b in range(NB):
                                sp.dma_start(qz[half * 64:half * 64 + 64, b, half, parity:8:2],
                                             m.qiT[parity * 64:parity * 64 + 64, :, L + b]).then_inc(s["q_in"], 16)
                sp.dma_start(wi[:], m.tok1[L:T, TOK_R + 64:TOK_R + 72]).then_inc(s["w_in"], 16)
                sp.dma_start(eye[:], io["c_eye8"]).then_inc(s["w_in"], 16)
                sp.dma_start(own_mask[:], io["c_own_mask"]).then_inc(s["w_in"], 16)
                for b in range(2, NB):
                    load_keys(sp, b, SP_PAGES)

            @block.tensor
            def _(pe):
                pe.wait_ge(s["w_in"], 48)
                nc.tensor.transpose(m.ps[0:8, 6, 0:NB], wi[:], m.ident[0:NB, 0:NB]).then_inc(s["w_mm"], 1)
                pe.wait_ge(s["q_in"], 16 * 4 * NB)
                pe.wait_ge(s["wz_out"], 1)
                for b in range(NB):
                    slot = b % 2
                    pe.wait_ge(k_in[b % RING], 16 * N_PAGES * (b // RING + 1))
                    for j in range(2):
                        pe.wait_ge(s["kT_out"], 2 * b + j + 1)
                        for x in range(4):
                            last = nc.tensor.transpose(m.ps[:, 4, x * P:(x + 1) * P],
                                                       kp[:, b % RING, 4 * j + x].rearrange("p a b -> p (a b)"),
                                                       m.ident[:])
                        last.then_inc(s["turned"], 1)
                    pe.wait_ge(s["kT_out"], 2 * b + 3)
                    for j in range(5):
                        n = 5 * b + j
                        pe.wait_ge(s["relued"], n + 1)
                        if j < 4:
                            out, half = m.ps[0:8, 5 + n % 2, :], j // 2
                            rhs = kT[:, slot, j % 2 * 512:j % 2 * 512 + 512]
                        else:
                            out, half, rhs = m.ps[0:8, 5 + n % 2, 0:NB], 0, m.kiT[:, L:T]
                        nc.tensor.matmul(out, qz[:, b, half, :], rhs, start=True, stop=True).then_inc(s["dots"], 1)
                    for j in range(5):
                        pe.wait_ge(s["relued"], 5 * b + j + 3)
                        out = m.ps[0:NB, j, :] if j < 4 else m.ps[0:NB, 7, 0:NB]
                        rhs = relu[:, slot, 512 * j:512 * j + (512 if j < 4 else NB)]
                        last = nc.tensor.matmul(out, wz[:, b, :], rhs, start=(b == 0), stop=(b == NB - 1))
                    last.then_inc(s["summed"], 1)

            @block.scalar
            def _(act):
                act.sem_inc(s["relued"], 2)
                act.sem_inc(s["summed"], 2)
                for b in range(RING - 1):
                    load_keys(act, b, ACT_PAGES)
                for b in range(NB):
                    if b + RING - 1 < NB:
                        load_keys(act, b + RING - 1, ACT_PAGES)
                    act.wait_ge(s["summed"], b + 1)
                    for j in range(5):
                        n = 5 * b + j
                        act.wait_ge(s["dots"], n + 1)
                        w = 512 if j < 4 else NB
                        nc.scalar.activation(relu[:, b % 2, 512 * j:512 * j + w], m.ps[0:8, 5 + n % 2, 0:w], ACT.Relu,
                                             scale=64 ** -0.5).then_inc(s["relued"], 1)

            @block.vector
            def _(dve):
                dve.sem_inc(s["kT_out"], 1)
                dve.memset(qz[:], 0.0).then_inc(s["zeroed"], 1)
                dve.wait_ge(s["w_mm"], 1)
                nc.vector.tensor_copy(wT[:], m.ps[0:8, 6, 0:NB]).then_inc(s["w_out"], 1)
                dve.wait_ge(s["w_out"], 1)
                nc.vector.tensor_tensor(wz[:], wT[:].rearrange("p (b o) -> p b o", o=1).to_broadcast([8, NB, NB]),
                                        eye[:], ALU.mult).then_inc(s["wz_out"], 1)
                for b in range(NB):
                    for j in range(2):
                        dve.wait_ge(s["turned"], 2 * b + j + 1)
                        if b >= 2:
                            dve.wait_ge(s["dots"], 5 * (b - 1))
                        nc.vector.tensor_copy(kT[:, b % 2, 512 * j:512 * j + 512], m.ps[:, 4, :]).then_inc(s["kT_out"], 1)
                dve.wait_ge(s["summed"], NB + 2)
                nc.vector.tensor_copy(m.chosen_s[:, 0:PAST], m.ps[0:NB, 0:4, :].rearrange("p a b -> p (a b)"))
                nc.vector.tensor_tensor(m.chosen_s[:, PAST:], m.ps[0:NB, 7, 0:NB], own_mask[:], ALU.add)



def choose(nc, m, io):
    tiles = [(m.chosen[t], P if t < FULL else TAIL) for t in range(NT) if t * P >= TOPK] + [(m.chosen_s, NB)]
    NTL = len(tiles)
    BITS = 31
    with ExitStack() as own:
        E = own.enter_context
        sb = lambda name, shape, dt=F32: E(nc.sbuf_tensor("ch_" + name, shape, dt))
        wmax = max(x.shape[-1] for x, _ in tiles)
        hits, equal, rank = sb("hits", [P, wmax], BF16), sb("equal", [P, wmax]), sb("rank", [P, wmax])
        count, need, sign, below = (sb(x, [P, NTL]) for x in ("count", "need", "sign", "below"))
        extra, thresh, left = (sb(x, [P, NTL]) for x in ("extra", "thresh", "left"))
        cand, flip = sb("cand", [P, NTL], I32), sb("flip", [P, NTL], I32)
        bits = sb("bits", [P, BITS])
        next_bits = sb("next", [P, BITS], I32)
        bits_in, step, loop_step = m.sem("ch_bits_in"), m.sem("ch_step"), m.sem("ch_loop")

        def load_bits(sp):
            sp.dma_start(bits[:], m.bits).then_inc(bits_in, 16)
            sp.dma_start(next_bits[:], m.next_bits).then_inc(bits_in, 16)

        def search(dve):
            steps = Steps(dve, step)
            V = nc.vector
            dve.memset(count[:], 0.0)
            for j, (x, r) in enumerate(tiles):
                dve.memset(extra[:, j:j + 1], float(x.shape[-1] + 1 - 2 * TOPK))
            steps.after(dve.memset(cand[:], 1 << (BITS - 1)))
            for j, (x, r) in enumerate(tiles):
                steps.after(V.tensor_scalar(hits[0:r, 0:x.shape[-1]], x[0:r], 0.0, None, ALU.is_ge, ALU.add,
                                            accum_out=count[0:r, j:j + 1]))
            steps.after(V.tensor_scalar(below[:], count[:], float(TOPK), None, ALU.is_lt))
            steps.after(V.tensor_scalar(sign[:], below[:], -2.0, 1.0, ALU.mult, ALU.add))
            steps.after(V.tensor_tensor(need[:], below[:], extra[:], ALU.mult))
            steps.after(V.tensor_scalar(need[:], need[:], float(TOPK), None, ALU.add))
            for j, (x, r) in enumerate(tiles):
                last = V.tensor_scalar(x[0:r], x[0:r], sign[0:r, j:j + 1], None, ALU.mult)
                steps.after(last)
            dve.wait_ge(bits_in, 32)
            LOOP = NTL + 3
            with dve.Fori(0, BITS) as i:
                steps_i = Steps(dve, loop_step, LOOP * i)
                for j, (x, r) in enumerate(tiles):
                    ins = V.tensor_scalar(hits[0:r, 0:x.shape[-1]], x[0:r], cand[0:r, j:j + 1].bitcast(F32), None,
                                          ALU.is_ge, ALU.add, accum_out=count[0:r, j:j + 1])
                    steps_i.after(ins)
                steps_i.after(V.tensor_tensor(below[:], count[:], need[:], ALU.is_lt))
                steps_i.after(V.tensor_scalar(flip[:], below[:], bits[:, bass.ds(i, 1)], None, ALU.mult))
                steps_i.after(V.scalar_tensor_tensor(out=cand[:], in0=cand[:], scalar=next_bits[:, bass.ds(i, 1)],
                                                     in1=flip[:], op0=ALU.bitwise_xor, op1=ALU.bitwise_xor))
                assert steps_i.n == LOOP
            steps.after(V.tensor_tensor(thresh[:], cand[:].bitcast(F32), sign[:], ALU.mult))
            for j, (x, r) in enumerate(tiles):
                w = x.shape[-1]
                G_, Q, K = hits[0:r, 0:w], equal[0:r, 0:w], rank[0:r, 0:w]
                t = thresh[0:r, j:j + 1]
                steps.after(V.tensor_scalar(x[0:r], x[0:r], sign[0:r, j:j + 1], None, ALU.mult))
                steps.after(V.tensor_scalar(G_, x[0:r], t, None, ALU.is_gt, ALU.add,
                                            accum_out=count[0:r, j:j + 1]))
                steps.after(V.tensor_scalar(left[0:r, j:j + 1], count[0:r, j:j + 1], -1.0, float(TOPK), ALU.mult,
                                            ALU.add))
                steps.after(V.tensor_scalar(Q, x[0:r], t, None, ALU.is_equal))
                steps.after(V.tensor_tensor_scan(K, Q, Q, 0.0, ALU.add, ALU.max))
                steps.after(V.scalar_tensor_tensor(out=K, in0=K, scalar=left[0:r, j:j + 1], in1=Q, op0=ALU.is_le,
                                                   op1=ALU.mult))
                steps.after(V.tensor_tensor(G_, G_, K, ALU.add))
                steps.after(V.tensor_scalar(x[0:r], G_, -NEG, NEG, ALU.mult, ALU.add))

        w = io["w_in_o"][0]
        f_load, f_pe, f_act, _, f_out = feature_programs(own, nc, m, w, [(0, H, m.qT)], "pf1", False)
        spare = m.actT[:, KC:12, :].rearrange("p a b -> p (a b)")[:, 0:KC * 512].rearrange("p (c n) -> p c n", c=KC)
        t_load, t_store, t_pe, t_act, _ = token_programs(own, nc, m, w, GATE_COLS + KV_COLS, m.tok1, "ptg", False, spare)
        run(nc, [load_bits, t_load, f_load, t_store], [f_pe, f_out, t_pe], [f_act, t_act], [search])



def finish(nc, m, io):
    with ExitStack() as own:
        E = own.enter_context
        gain = E(nc.sbuf_tensor("fn_gain", [P, D], F32))
        squares = E(nc.sbuf_tensor("fn_sq", [P, D], F32))
        y = E(nc.sbuf_tensor("fn_y", [P, NT, D], F32))
        ss, rstd = E(nc.sbuf_tensor("fn_ss", [P, NT], F32)), E(nc.sbuf_tensor("fn_rstd", [P, NT], F32))
        gain_in, sq_step, root, step, y_out = (m.sem("fn_" + x) for x in ("gain_in", "sq", "root", "step", "y_out"))
        rows = lambda t: P if t < FULL else LAST
        with nc.Block() as block:
            @block.scalar
            def _(act):
                steps = Steps(act, sq_step)
                for t in range(NT):
                    r = rows(t)
                    steps.after(nc.scalar.activation(squares[0:r], m.h[0:r, t, :], ACT.Square,
                                                     accum_out=ss[0:r, t:t + 1]))
                for t in range(NT):
                    r = rows(t)
                    last = nc.scalar.activation(rstd[0:r, t:t + 1], ss[0:r, t:t + 1], ACT.Sqrt, scale=1.0 / D,
                                                bias=m.eps[0:r, 0:1])
                last.then_inc(root, 1)

            @block.vector
            def _(dve):
                dve.wait_ge(gain_in, 16)
                dve.wait_ge(root, 1)
                steps = Steps(dve, step)
                for t in range(NT):
                    r = rows(t)
                    steps.after(nc.vector.reciprocal(rstd[0:r, t:t + 1], rstd[0:r, t:t + 1]))
                    nc.vector.scalar_tensor_tensor(out=y[0:r, t], in0=m.h[0:r, t], scalar=rstd[0:r, t:t + 1],
                                                   in1=gain[0:r], op0=ALU.mult, op1=ALU.mult).then_inc(y_out, 1)

            @block.sync
            def _(sp):
                sp.dma_start(gain[:], row_view(io["final_norm"]).to_broadcast([P, D])).then_inc(gain_in, 16)
                yp = io["y_prompt"][0]
                first = P - N_META
                sp.wait_ge(y_out, 1)
                sp.dma_start(yp[0:first, :], y[N_META:P, 0, :]).then_inc(m.s_out, 16)
                with sp.Fori(1, FULL) as t:
                    sp.wait_ge(y_out, t + 1)
                    sp.dma_start(yp[bass.ds(t * P - N_META, P), :], y[:, bass.ds(t, 1), :]).then_inc(m.s_out, 16)
                sp.wait_ge(y_out, NT)
                sp.dma_start(yp[SEQ - TAIL:SEQ, :], y[0:TAIL, FULL, :]).then_inc(m.s_out, 16)
                sp.dma_start(io["y_sample"].rearrange("b o d -> (b o) d"), y[TAIL:LAST, FULL, :]).then_inc(m.s_out, 16)
                m.n_out += FULL + 2
                sp.wait_ge(m.s_out, 16 * m.n_out)



INPUTS = ['x_prompt', 'x_sample', 'cache_a_k', 'cache_a_v', 'state_b_s', 'state_b_conv', 'cache_c_k', 'cache_c_v',
          'cache_c_idx', 'page_table', 'meta', 'bias_table', 'final_norm', 'norm_e', 'w_in_e', 'w_out_e', 'lam_q1',
          'lam_k1', 'lam_q2', 'lam_k2', 'subln_a', 'conv_b', 'a_log_b', 'dt_bias_b', 'norm_b', 'norm_o', 'w_in_o',
          'w_out_o']


def buckets():
    d = FAR - np.arange(BIAS_W)
    n = np.maximum(d, 0)
    nf = np.maximum(n, 1).astype(np.float32)
    large = 16 + (np.log(nf / 16) / np.log(128 / 16) * 16).astype(np.int32)
    bucket = np.where(n < 16, n, np.minimum(large, 31))
    out = np.zeros((33, BIAS_W), np.float32)
    out[bucket, np.arange(BIAS_W)] = d >= 0
    out[32] = d < 0
    return out


def constants():
    i = np.arange(P)
    row, col = i[:, None], i[None, :]
    masks = [row <= col, row > col, row // 8 == col // 8]
    masks += [(row // (2 * b) == col // (2 * b)) & (row // b % 2 == 0) & (col // b % 2 == 1) for b in (8, 16, 32, 64)]
    return {"c_ident": np.eye(P, dtype=np.float32),
            "c_buckets": buckets(),
            "c_sel_b1": np.repeat(np.eye(NB), H, 1).astype(np.float32),
            "c_sel_b2": np.repeat(np.eye(NB), 2 * H, 1).astype(np.float32),
            "c_sel_h1": np.tile(np.eye(H), (1, NB)).astype(np.float32),
            "c_sel_h2": np.tile(np.repeat(np.eye(H), 2, 1), (1, NB)).astype(np.float32),
            "c_own_mask": (NEG * (1 - np.eye(NB))).astype(np.float32),
            "c_causal": (NEG * (i[None, :] > i[:, None])).astype(np.float32),
            "c_bits": np.tile(2.0 ** (30 - np.arange(31)), (P, 1)).astype(np.float32),
            "c_next_bits": np.tile(np.array([1 << (29 - k) if k < 30 else 0 for k in range(31)]), (P, 1))
            .astype(np.int32),
            "c_eye8": np.tile(8 ** -0.5 * np.eye(NB), (8, 1, 1)).astype(np.float32),
            "c_flip": np.eye(P, dtype=np.float32)[::-1].copy(),
            "c_parity": (i[:, None] % 2 == np.arange(2)).astype(np.float32),
            "c_halves": np.concatenate([64 ** -0.5 * (i[:, None] // 64 == np.arange(2)), np.full((P, 1), P ** -0.5)],
                                       1).astype(np.float32),
            "c_delta_masks": np.stack(masks, 1).astype(np.float32)}


OUTPUTS = {
    "y_prompt": (1, SEQ, D), "y_sample": (NB, 1, D),
    "pa_k": (1, 1, L, KV, 2, 64), "pa_v": (1, 1, L, KV, P), "pb_s": (1, 1, B_H, P, P), "pb_conv": (1, 1, 3, 1536),
    "pc_k": (1, 1, L, KV, P), "pc_v": (1, 1, L, KV, P), "pc_idx": (1, 1, L, 64),
    "sa_k": (1, NB, 1, KV, 2, 64), "sa_v": (1, NB, 1, KV, P), "sb_s": (1, NB, B_H, P, P), "sb_conv": (1, NB, 3, 1536),
    "sc_k": (1, NB, 1, KV, P), "sc_v": (1, NB, 1, KV, P), "sc_idx": (1, NB, 1, 64),
}


def kv_outputs(k_p, v_p, k_s, v_s):
    return [(k_p, 0, L, TOK_K, TOK_K + 256), (v_p, 0, L, TOK_V, TOK_V + 256),
            (k_s, L, T, TOK_K, TOK_K + 256), (v_s, L, T, TOK_V, TOK_V + 256)]


class Shared:
    pass


def build(nc, io):
    with ExitStack() as ctx:
        E = ctx.enter_context
        m = Shared()
        m.s_out, m.n_out = E(nc.semaphore("outputs_stored")), 0
        m.s_idle = E(nc.semaphore("waits_alone"))
        in_use = []

        def sem(name):
            in_use.append(nc.alloc_semaphore(name=name))
            return in_use[-1]

        def recycle():
            nc.clear_and_free_semaphores(in_use)
            in_use.clear()
            nc.all_engine_barrier()

        m.sem = sem
        dram = lambda name, shape: nc.dram_tensor(name, shape, F32, kind="Internal").ap()
        m.tok, m.tok1 = dram("tok_rows", (T, TOK_W)), dram("tok_rows_1", (T, TOK_W))
        m.h_dram = dram("h_rows", (T, D))
        m.bias = dram("bias_rows", (H, BIAS_W))
        m.causal, m.bits, m.next_bits, m.flip = io["c_causal"], io["c_bits"], io["c_next_bits"], io["c_flip"]
        m.ps = E(nc.psum_tensor("banks", [P, 8, 512], F32))
        m.ident = E(nc.sbuf_tensor("ident", [P, P], F32))
        m.ones = E(nc.sbuf_tensor("ones", [P, P], F32))
        m.eps = E(nc.sbuf_tensor("eps", [P, 1], F32))
        m.halves = E(nc.sbuf_tensor("halves", [P, 3], F32))
        m.halves_wide = E(nc.sbuf_tensor("halves_wide", [P, 3, P], F32))
        m.pages = E(nc.sbuf_tensor("pages", [1, NB * N_PAGES], I32))
        m.lam = E(nc.sbuf_tensor("lam", [P, 1], F32))
        m.actT = E(nc.sbuf_tensor("actT", [P, 12, T], F32))
        load_constants(nc, m, io)
        bias_rows(nc, m, io)
        with ExitStack() as scope:
            load, store, pe, act, dve = token_programs(scope, nc, m, io["w_in_e"][0], KV_COLS + GATE_COLS + REST_0,
                                                       m.tok, "pt0")
            m.h = scope.enter_context(nc.sbuf_tensor("h_in", [P, NT, D], F32))
            load_rows(nc, m, io, "ld0", load)
            norm_and_turn(nc, m, io["norm_e"][0], "n0")
            run(nc, [store], [pe], [act], [dve])
        store_kv(nc, m, m.tok, kv_outputs(io["pa_k"].rearrange("a b l k c d -> (a b l) (k c d)"),
                                          io["pa_v"].rearrange("a b l k d -> (a b l) (k d)"),
                                          io["sa_k"].rearrange("a b l k c d -> (a b l) (k c d)"),
                                          io["sa_v"].rearrange("a b l k d -> (a b l) (k d)")))
        with ExitStack() as layer:
            m.qT = layer.enter_context(nc.sbuf_tensor("a_qT", [P, H, T], F32))
            with ExitStack() as delta:
                m.mixT = delta.enter_context(nc.sbuf_tensor("b_qkvT", [P, 12, T], F32))
                m.gates = delta.enter_context(nc.sbuf_tensor("b_gates", [P, NT + NB, 8], F32))
                project_features(nc, m, io["w_in_e"][0], [(MID, 12, m.mixT)], "pf0")
                convolve_and_normalise(nc, m, io)
                delta_prompt(nc, m, io)
                delta_samples(nc, m, io)
            recycle()
            m.kT = layer.enter_context(nc.sbuf_tensor("a_kT", [P, KV, T], F32))
            m.v = layer.enter_context(nc.sbuf_tensor("a_v", [P, NT, KV * P], F32))
            load_kv(nc, m, m.tok, "kv0")
            prompt_attention(nc, m, m.tok, True, io["subln_a"])
            sample_attention(nc, m, io, m.tok, True, io["cache_a_k"][0], io["cache_a_v"][0], io["subln_a"])
        recycle()
        with ExitStack() as scope:
            load, store, pe, act, dve = token_programs(scope, nc, m, io["w_in_o"][0], REST_1, m.tok1, "pt1")
            m.h = scope.enter_context(nc.sbuf_tensor("h_mid", [P, NT, D], F32))
            load_rows(nc, m, io, "ld1", load)
            project_out(nc, m, io["w_out_e"][0], 12, "po0")
            norm_and_turn(nc, m, io["norm_o"][0], "n1")
            move_rows(nc, m, "h_saved", True)
            run(nc, [store], [pe], [act], [dve])
        with ExitStack() as layer:
            E1 = layer.enter_context
            m.qT = E1(nc.sbuf_tensor("c_qT", [P, H, T], F32))
            widths = {t: t * P + (P if t < FULL else TAIL) for t in range(NT) if t * P >= TOPK}
            m.chosen = {t: E1(nc.sbuf_tensor(f"c_chosen{t}", [P, w], F32)) for t, w in widths.items()}
            m.chosen_s = E1(nc.sbuf_tensor("c_chosen_s", [NB, PAST + NB], F32))
            with ExitStack() as index:
                m.qiT = index.enter_context(nc.sbuf_tensor("c_qiT", [P, 4, T], F32))
                m.kiT = index.enter_context(nc.sbuf_tensor("c_kiT", [P, T], F32))
                project_features(nc, m, io["w_in_o"][0], [(MID, 4, m.qiT)], "pfi")
                index_prompt(nc, m)
                index_samples(nc, m, io)
            choose(nc, m, io)
            store_kv(nc, m, m.tok1, kv_outputs(io["pc_k"].rearrange("a b l k d -> (a b l) (k d)"),
                                               io["pc_v"].rearrange("a b l k d -> (a b l) (k d)"),
                                               io["sc_k"].rearrange("a b l k d -> (a b l) (k d)"),
                                               io["sc_v"].rearrange("a b l k d -> (a b l) (k d)"))
                     + [(io["pc_idx"].rearrange("a b l d -> (a b l) d"), 0, L, TOK_R, TOK_R + 64),
                        (io["sc_idx"].rearrange("a b l d -> (a b l) d"), L, T, TOK_R, TOK_R + 64)])
            recycle()
            m.kT = E1(nc.sbuf_tensor("c_kT", [P, KV, T], F32))
            m.v = E1(nc.sbuf_tensor("c_v", [P, NT, KV * P], F32))
            load_kv(nc, m, m.tok1, "kv1")
            prompt_attention(nc, m, m.tok1, False, None)
            sample_attention(nc, m, io, m.tok1, False, io["cache_c_k"][0], io["cache_c_v"][0], None)
        m.h = E(nc.sbuf_tensor("h_out", [P, NT, D], F32))
        move_rows(nc, m, "h_loaded", False)
        project_out(nc, m, io["w_out_o"][0], 8, "po1")
        finish(nc, m, io)


def lay_out(nc, inputs):
    aps, arrays = {}, {}
    consts = constants()
    for name in INPUTS + list(consts):
        a = np.ascontiguousarray(consts[name] if name in consts else inputs[name])
        arrays[name + "_dram"] = a
        aps[name] = nc.dram_tensor(name + "_dram", a.shape, mybir.dt.from_np(a.dtype), kind="ExternalInput").ap()
    for name, shape in OUTPUTS.items():
        aps[name] = nc.dram_tensor(name + "_dram", shape, F32, kind="ExternalOutput").ap()
    build(nc, aps)
    return arrays


def kernel(**inputs):
    import concourse.bacc as bacc
    from concourse.bass_utils import run_bass_kernel_spmd

    nc = bacc.Bacc("TRN2", target_bir_lowering=False, num_devices=1)
    arrays = lay_out(nc, inputs)
    got = run_bass_kernel_spmd(nc, [arrays], core_ids=[0]).results[0]
    return tuple(got[name + "_dram"] for name in OUTPUTS)
```
